# Optimizing a Trainium2 kernel written in Bass

```python
import math
import jax, jax.numpy as jnp
from jax import lax
import numpy as np

D_MODEL = 1024
BATCH = 1
SEQ = 1024
DEPTH = 2
DEC_BATCH = 8
DEC_SEQ = 1
PAST_LEN = 1024
PAGE_SIZE = 128

N_HEADS = 16
HEAD_DIM = 64
N_KV_HEADS = 2
GROUP = N_HEADS // N_KV_HEADS
HD = N_HEADS * HEAD_DIM
KVD = N_KV_HEADS * HEAD_DIM
N_A_LAYERS = DEPTH // 2
N_B_LAYERS = DEPTH - N_A_LAYERS
WINDOW_A = 128
WINDOW_B = 512
Q_BLOCK = 128
CMP_BLOCK = 32
SEL_BLOCK = 64
CMP_PER_SEL = SEL_BLOCK // CMP_BLOCK
SEL_TOPK = 16
CMP_HIDDEN = 2 * HEAD_DIM
N_BRANCH = 3
N_BUCKETS = 32
T5_MAX_DISTANCE = 128
RMS_EPS = 1e-6
ATTN_SCALE = HEAD_DIM ** -0.5

kernel_name = 'yoco_swa_sink_nsa_adaln_decoder_step'

def rmsnorm(x, g):
    xf = x.astype(jnp.float32)
    y = xf * lax.rsqrt(jnp.mean(xf * xf, axis=-1, keepdims=True) + RMS_EPS)
    return (y * g.astype(jnp.float32)).astype(x.dtype)

def ada_params(c, w, b, n_parts):
    h = jax.nn.silu(c) @ w + b
    return [t[:, None, :] for t in jnp.split(h, n_parts, axis=-1)]

def modulate(x, g, shift, scale):
    return rmsnorm(x, g) * (1 + scale) + shift

def t5_bucket(dist):
    n = jnp.maximum(dist, 0)
    exact = N_BUCKETS // 2
    nf = jnp.maximum(n, exact).astype(jnp.float32)
    large = exact + (jnp.log(nf / exact) / math.log(T5_MAX_DISTANCE / exact) * (N_BUCKETS - exact)).astype(jnp.int32)
    return jnp.where(n < exact, n, jnp.minimum(large, N_BUCKETS - 1))

def t5_bias(table, dist):
    b = table.astype(jnp.float32)[t5_bucket(dist)]
    nq, nl = dist.shape
    return jnp.transpose(b, (2, 0, 1)).reshape(N_KV_HEADS, GROUP, nq, nl)

def masked_softmax(logits, valid, sink=None):
    logits = jnp.where(valid, logits, -jnp.inf)
    m = jnp.max(logits, axis=-1, keepdims=True)
    if sink is not None:
        m = jnp.maximum(m, sink)
    m = jnp.where(jnp.isfinite(m), m, 0.0)
    e = jnp.exp(logits - m)
    den = jnp.sum(e, axis=-1, keepdims=True)
    if sink is not None:
        den = den + jnp.exp(sink - m)
    return e / jnp.where(den > 0, den, 1.0)

def gqa_attend(q, k, v, dist, valid, table, sink=None):
    logits = jnp.einsum('nqgrd,nlgd->ngrql', q, k).astype(jnp.float32) * ATTN_SCALE + t5_bias(table, dist)
    p = masked_softmax(logits, valid, sink)
    return jnp.einsum('ngrql,nlgd->nqgrd', p.astype(v.dtype), v)

def window_attend(q, qpos, k, v, kpos, window, table, sink=None):
    dist = qpos[:, None] - kpos[None, :]
    valid = (dist >= 0) & (dist <= window) & (kpos[None, :] >= 0)
    return gqa_attend(q, k, v, dist, valid, table, sink)

def unblock(o):
    return jnp.moveaxis(o, 0, 1).reshape((o.shape[1], o.shape[0] * o.shape[2]) + o.shape[3:])

def window_attn_prompt(q, k, v, window, table, sink=None):
    s = q.shape[1]
    pad = ((0, 0), (window, 0), (0, 0), (0, 0))
    kp, vp = jnp.pad(k, pad), jnp.pad(v, pad)

    def block(b):
        s0 = b * Q_BLOCK
        qb = lax.dynamic_slice_in_dim(q, s0, Q_BLOCK, axis=1)
        kb = lax.dynamic_slice_in_dim(kp, s0, window + Q_BLOCK, axis=1)
        vb = lax.dynamic_slice_in_dim(vp, s0, window + Q_BLOCK, axis=1)
        qpos = s0 + jnp.arange(Q_BLOCK)
        kpos = s0 - window + jnp.arange(window + Q_BLOCK)
        return window_attend(qb, qpos, kb, vb, kpos, window, table, sink)

    return unblock(lax.map(block, jnp.arange(s // Q_BLOCK)))

def window_attn_sample(q, kv_new, buf, window, table, sink=None):
    lb, ds = buf.shape[1], q.shape[1]
    keys = jnp.concatenate([buf, kv_new], axis=1)
    qpos = PAST_LEN + jnp.arange(ds)
    kpos = PAST_LEN - lb + jnp.arange(lb + ds)
    o = window_attend(q, qpos, keys[:, :, 0], keys[:, :, 1], kpos, window, table, sink)
    return o, keys[:, -min(window, lb + ds):]

def a_project(x, c, g, w_ada, b_ada, w_in):
    n, t = x.shape[:2]
    shift, scale, gate = ada_params(c, w_ada, b_ada, 3)
    h = modulate(x, g, shift, scale)
    q, k, v, z = jnp.split(h @ w_in, [HD, HD + KVD, HD + 2 * KVD], axis=-1)
    q = q.reshape(n, t, N_KV_HEADS, GROUP, HEAD_DIM)
    kv = jnp.stack([k, v], axis=2).reshape(n, t, 2, N_KV_HEADS, HEAD_DIM)
    return q, kv, z, gate

def a_finish(x, o, z, gate, w_out):
    n, t = x.shape[:2]
    return x + gate * ((o.reshape(n, t, HD) * jax.nn.silu(z)) @ w_out)

def kv_side(s, c, g, w_ada, b_ada, w_in):
    n, t = s.shape[:2]
    shift, scale = ada_params(c, w_ada, b_ada, 2)
    h = modulate(s, g, shift, scale)
    rows = (h @ w_in).reshape(n, t, N_BRANCH, 2, N_KV_HEADS, HEAD_DIM)
    return rows[:, :, 0], rows[:, :, 1], rows[:, :, 2]

def pad_rows(rows, mult):
    extra = (-rows.shape[1]) % mult
    return jnp.pad(rows, ((0, 0), (0, extra), (0, 0), (0, 0), (0, 0)))

def compress(rows, pos, w1, w2):
    n, l = rows.shape[:2]
    blk = rows.reshape(n, l // CMP_BLOCK, CMP_BLOCK, 2, N_KV_HEADS, HEAD_DIM) + pos[None, None, :, :, None, :]
    hid = jax.nn.silu(jnp.einsum('ncbkgd,kbdh->nckgh', blk, w1))
    return jnp.einsum('nckgh,khd->nckgd', hid, w2)

def prompt_gather(sel_rows):
    n, s = sel_rows.shape[:2]
    blocks = sel_rows.reshape(n, s // SEL_BLOCK, SEL_BLOCK, 2, N_KV_HEADS, HEAD_DIM)
    nidx = jnp.arange(n)[:, None, None, None]
    gidx = jnp.arange(N_KV_HEADS)[None, :, None, None]

    def gather(idx):
        return blocks[nidx, idx, :, :, gidx]
    return gather

def paged_gather(pool, page_table, new_rows):
    n = page_table.shape[0]
    bpp = PAGE_SIZE // SEL_BLOCK
    n_past = PAST_LEN // SEL_BLOCK
    pool_b = pool.reshape(pool.shape[0], bpp, SEL_BLOCK, 2, N_KV_HEADS, HEAD_DIM)
    new_b = pad_rows(new_rows, SEL_BLOCK).reshape(n, -1, SEL_BLOCK, 2, N_KV_HEADS, HEAD_DIM)
    n_new = new_b.shape[1]
    nidx = jnp.arange(n)[:, None, None, None]
    gidx = jnp.arange(N_KV_HEADS)[None, :, None, None]

    def gather(idx):
        past = jnp.minimum(idx, n_past - 1)
        phys = page_table[nidx, past // bpp]
        from_pool = pool_b[phys, past % bpp, :, :, gidx]
        from_new = new_b[nidx, jnp.clip(idx - n_past, 0, n_new - 1), :, :, gidx]
        return jnp.where((idx >= n_past)[..., None, None, None], from_new, from_pool)
    return gather

def nsa_branches(q, qpos, ck, cv, gather_sel, wk, wv, wpos, table):
    n, nq = q.shape[:2]
    nc = ck.shape[1]
    ns = nc // CMP_PER_SEL
    cend = jnp.arange(nc) * CMP_BLOCK + (CMP_BLOCK - 1)
    cvalid = cend[None, :] <= qpos[:, None]
    logits = jnp.einsum('nqgrd,ncgd->ngrqc', q, ck).astype(jnp.float32) * ATTN_SCALE
    p_cmp = masked_softmax(logits, cvalid)
    o_cmp = jnp.einsum('ngrqc,ncgd->nqgrd', p_cmp.astype(cv.dtype), cv)
    imp = p_cmp.reshape(n, N_KV_HEADS, GROUP, nq, ns, CMP_PER_SEL).sum(axis=(2, 5))
    cur = qpos // SEL_BLOCK
    j = jnp.arange(ns)
    forced = (j[None, :] == 0) | (j[None, :] == cur[:, None]) | (j[None, :] == cur[:, None] - 1)
    allowed = j[None, :] <= cur[:, None]
    score = jnp.where(forced, jnp.inf, jnp.where(allowed, imp, -jnp.inf))
    top, idx = lax.top_k(score, min(SEL_TOPK, ns))
    kv_sel = gather_sel(idx)
    kpos = idx[..., None] * SEL_BLOCK + jnp.arange(SEL_BLOCK)
    svalid = (top > -jnp.inf)[..., None] & (kpos <= qpos[None, None, :, None, None])
    nl = idx.shape[-1] * SEL_BLOCK
    ks = kv_sel[..., 0, :].reshape(n, N_KV_HEADS, nq, nl, HEAD_DIM)
    vs = kv_sel[..., 1, :].reshape(n, N_KV_HEADS, nq, nl, HEAD_DIM)
    kpos = kpos.reshape(n, N_KV_HEADS, nq, nl)
    svalid = svalid.reshape(n, N_KV_HEADS, nq, nl)
    gidx = jnp.arange(N_KV_HEADS)[None, :, None, None]
    table3 = table.astype(jnp.float32).reshape(N_BUCKETS, N_KV_HEADS, GROUP)
    bias = table3[t5_bucket(qpos[None, None, :, None] - kpos), gidx]
    logits = jnp.einsum('nqgrd,ngqld->ngqrl', q, ks).astype(jnp.float32) * ATTN_SCALE + jnp.swapaxes(bias, -1, -2)
    p_sel = masked_softmax(logits, svalid[:, :, :, None, :])
    o_sel = jnp.einsum('ngqrl,ngqld->nqgrd', p_sel.astype(vs.dtype), vs)
    o_win = window_attend(q, qpos, wk, wv, wpos, WINDOW_B, table)
    return o_cmp, o_sel, o_win

def nsa_prompt(q, ck, cv, gather_sel, win_rows, table):
    s = q.shape[1]
    wp = jnp.pad(win_rows, ((0, 0), (WINDOW_B, 0), (0, 0), (0, 0), (0, 0)))

    def block(b):
        s0 = b * Q_BLOCK
        qb = lax.dynamic_slice_in_dim(q, s0, Q_BLOCK, axis=1)
        wb = lax.dynamic_slice_in_dim(wp, s0, WINDOW_B + Q_BLOCK, axis=1)
        qpos = s0 + jnp.arange(Q_BLOCK)
        wpos = s0 - WINDOW_B + jnp.arange(WINDOW_B + Q_BLOCK)
        return nsa_branches(qb, qpos, ck, cv, gather_sel, wb[:, :, 0], wb[:, :, 1], wpos, table)

    o_cmp, o_sel, o_win = lax.map(block, jnp.arange(s // Q_BLOCK))
    return unblock(o_cmp), unblock(o_sel), unblock(o_win)

def b_project(x, c, g, w_ada, b_ada, w_in):
    n, t = x.shape[:2]
    shift, scale, gate = ada_params(c, w_ada, b_ada, 3)
    h = modulate(x, g, shift, scale)
    q, z, gl = jnp.split(h @ w_in, [HD, HD + N_BRANCH * HD], axis=-1)
    q = q.reshape(n, t, N_KV_HEADS, GROUP, HEAD_DIM)
    z = z.reshape(n, t, N_BRANCH, N_HEADS, HEAD_DIM)
    gl = gl.reshape(n, t, N_BRANCH, N_HEADS)
    return q, z, gl, gate

def b_finish(x, o_cmp, o_sel, o_win, z, gl, gate, w_out):
    n, t = x.shape[:2]
    ob = jnp.stack([o_cmp, o_sel, o_win], axis=2).reshape(n, t, N_BRANCH, N_HEADS, HEAD_DIM)
    mix = jnp.sum(jax.nn.sigmoid(gl)[..., None] * ob * jax.nn.silu(z), axis=2)
    return x + gate * (mix.reshape(n, t, HD) @ w_out)

def setup_inputs(seed: int = 0) -> dict:
    key = jax.random.key(seed)
    ks = jax.random.split(key, 32)
    f32 = jnp.float32

    def nrm(k, shape, scale):
        return scale * jax.random.normal(k, shape, f32)

    n_pages = PAST_LEN // PAGE_SIZE
    n_phys = (5 * DEC_BATCH * n_pages) // 4
    lba = min(WINDOW_A, PAST_LEN)
    lbb = min(WINDOW_B, PAST_LEN)
    page_table = jax.random.permutation(ks[8], n_phys)[: DEC_BATCH * n_pages].reshape(DEC_BATCH, n_pages).astype(jnp.int32)
    d_in_a = HD + 2 * KVD + HD
    d_in_b = HD + N_BRANCH * HD + N_BRANCH * N_HEADS
    return {
        'x_prompt': nrm(ks[0], (BATCH, SEQ, D_MODEL), 1.0),
        'x_sample': nrm(ks[1], (DEC_BATCH, DEC_SEQ, D_MODEL), 1.0),
        'state_a_kv': nrm(ks[2], (N_A_LAYERS, DEC_BATCH, lba, 2, N_KV_HEADS, HEAD_DIM), 1.0),
        'cache_cmp_kv': nrm(ks[3], (n_phys, PAGE_SIZE, 2, N_KV_HEADS, HEAD_DIM), 1.0),
        'cache_sel_kv': nrm(ks[4], (n_phys, PAGE_SIZE, 2, N_KV_HEADS, HEAD_DIM), 1.0),
        'state_win_kv': nrm(ks[5], (DEC_BATCH, lbb, 2, N_KV_HEADS, HEAD_DIM), 1.0),
        'page_table': page_table,
        'c_prompt': nrm(ks[6], (BATCH, D_MODEL), 1.0),
        'c_sample': nrm(ks[7], (DEC_BATCH, D_MODEL), 1.0),
        'rel_bias_table': nrm(ks[9], (N_BUCKETS, N_HEADS), 0.2),
        'a_norm_g': 1.0 + nrm(ks[10], (N_A_LAYERS, D_MODEL), 0.02),
        'a_w_ada': nrm(ks[11], (N_A_LAYERS, D_MODEL, 3 * D_MODEL), 0.5 * D_MODEL ** -0.5),
        'a_b_ada': nrm(ks[12], (N_A_LAYERS, 3 * D_MODEL), 0.02),
        'a_w_in': nrm(ks[13], (N_A_LAYERS, D_MODEL, d_in_a), D_MODEL ** -0.5),
        'a_sinks': nrm(ks[14], (N_A_LAYERS, N_HEADS), 0.5),
        'a_w_out': nrm(ks[15], (N_A_LAYERS, HD, D_MODEL), HD ** -0.5),
        'kv_norm_g': 1.0 + nrm(ks[16], (D_MODEL,), 0.02),
        'kv_w_ada': nrm(ks[17], (D_MODEL, 2 * D_MODEL), 0.5 * D_MODEL ** -0.5),
        'kv_b_ada': nrm(ks[18], (2 * D_MODEL,), 0.02),
        'kv_w_in': nrm(ks[19], (D_MODEL, N_BRANCH * 2 * KVD), D_MODEL ** -0.5),
        'cmp_pos': nrm(ks[20], (CMP_BLOCK, 2, HEAD_DIM), 0.1),
        'cmp_w1': nrm(ks[21], (2, CMP_BLOCK, HEAD_DIM, CMP_HIDDEN), (CMP_BLOCK * HEAD_DIM) ** -0.5),
        'cmp_w2': nrm(ks[22], (2, CMP_HIDDEN, HEAD_DIM), CMP_HIDDEN ** -0.5),
        'b_norm_g': 1.0 + nrm(ks[23], (N_B_LAYERS, D_MODEL), 0.02),
        'b_w_ada': nrm(ks[24], (N_B_LAYERS, D_MODEL, 3 * D_MODEL), 0.5 * D_MODEL ** -0.5),
        'b_b_ada': nrm(ks[25], (N_B_LAYERS, 3 * D_MODEL), 0.02),
        'b_w_in': nrm(ks[26], (N_B_LAYERS, D_MODEL, d_in_b), D_MODEL ** -0.5),
        'b_w_out': nrm(ks[27], (N_B_LAYERS, HD, D_MODEL), HD ** -0.5),
        'final_norm_g': 1.0 + nrm(ks[28], (D_MODEL,), 0.02),
    }

def reference(x_prompt, x_sample, state_a_kv, cache_cmp_kv, cache_sel_kv, state_win_kv, page_table, c_prompt, c_sample, rel_bias_table, a_norm_g, a_w_ada, a_b_ada, a_w_in, a_sinks, a_w_out, kv_norm_g, kv_w_ada, kv_b_ada, kv_w_in, cmp_pos, cmp_w1, cmp_w2, b_norm_g, b_w_ada, b_b_ada, b_w_in, b_w_out, final_norm_g):
    xp, xs = x_prompt, x_sample
    n_dec, ds = xs.shape[:2]
    qpos_s = PAST_LEN + jnp.arange(ds)
    a_new_p, a_new_s = [], []
    for layer in range(DEPTH):
        if layer < N_A_LAYERS:
            i = layer
            sink = a_sinks[i].astype(jnp.float32).reshape(N_KV_HEADS, GROUP, 1, 1)
            q, kv, z, gate = a_project(xp, c_prompt, a_norm_g[i], a_w_ada[i], a_b_ada[i], a_w_in[i])
            o = window_attn_prompt(q, kv[:, :, 0], kv[:, :, 1], WINDOW_A, rel_bias_table, sink)
            xp = a_finish(xp, o, z, gate, a_w_out[i])
            a_new_p.append(kv[:, -min(WINDOW_A, kv.shape[1]):])
            q, kv, z, gate = a_project(xs, c_sample, a_norm_g[i], a_w_ada[i], a_b_ada[i], a_w_in[i])
            o, buf = window_attn_sample(q, kv, state_a_kv[i], WINDOW_A, rel_bias_table, sink)
            xs = a_finish(xs, o, z, gate, a_w_out[i])
            a_new_s.append(buf)
        else:
            if layer == N_A_LAYERS:
                cmp_p, sel_p, win_p = kv_side(xp, c_prompt, kv_norm_g, kv_w_ada, kv_b_ada, kv_w_in)
                cmp_s, sel_s, win_s = kv_side(xs, c_sample, kv_norm_g, kv_w_ada, kv_b_ada, kv_w_in)
                comp_p = compress(pad_rows(cmp_p, SEL_BLOCK), cmp_pos, cmp_w1, cmp_w2)
                past_cmp = cache_cmp_kv[page_table].reshape(n_dec, page_table.shape[1] * PAGE_SIZE, 2, N_KV_HEADS, HEAD_DIM)
                full_cmp = pad_rows(jnp.concatenate([past_cmp, cmp_s], axis=1), SEL_BLOCK)
                comp_s = compress(full_cmp, cmp_pos, cmp_w1, cmp_w2)
                gather_p = prompt_gather(sel_p)
                gather_s = paged_gather(cache_sel_kv, page_table, sel_s)
                lbb = state_win_kv.shape[1]
                win_keys_s = jnp.concatenate([state_win_kv, win_s], axis=1)
                wpos_s = PAST_LEN - lbb + jnp.arange(lbb + ds)
                new_win_kv_sample = win_keys_s[:, -min(WINDOW_B, lbb + ds):]
            j = layer - N_A_LAYERS
            q, z, gl, gate = b_project(xp, c_prompt, b_norm_g[j], b_w_ada[j], b_b_ada[j], b_w_in[j])
            o_cmp, o_sel, o_win = nsa_prompt(q, comp_p[:, :, 0], comp_p[:, :, 1], gather_p, win_p, rel_bias_table)
            xp = b_finish(xp, o_cmp, o_sel, o_win, z, gl, gate, b_w_out[j])
            q, z, gl, gate = b_project(xs, c_sample, b_norm_g[j], b_w_ada[j], b_b_ada[j], b_w_in[j])
            o_cmp, o_sel, o_win = nsa_branches(q, qpos_s, comp_s[:, :, 0], comp_s[:, :, 1], gather_s, win_keys_s[:, :, 0], win_keys_s[:, :, 1], wpos_s, rel_bias_table)
            xs = b_finish(xs, o_cmp, o_sel, o_win, z, gl, gate, b_w_out[j])
    y_prompt = rmsnorm(xp, final_norm_g)
    y_sample = rmsnorm(xs, final_norm_g)
    new_a_kv_prompt = jnp.stack(a_new_p)
    new_a_kv_sample = jnp.stack(a_new_s)
    new_win_kv_prompt = win_p[:, -min(WINDOW_B, win_p.shape[1]):]
    return (y_prompt, y_sample, new_a_kv_prompt, new_a_kv_sample, cmp_p, cmp_s, sel_p, sel_s, new_win_kv_prompt, new_win_kv_sample)


_drawn_inputs = setup_inputs


def setup_inputs(seed=0):
    import zlib

    import numpy as np

    out = dict(_drawn_inputs(seed))
    spreads = {}
    factors = {'cache_cmp_kv': 4.399,
     'cache_sel_kv': 8.0,
     'rel_bias_table': 8.0,
     'a_norm_g': 3.094,
     'a_sinks': 8.0,
     'kv_norm_g': 2.89,
     'cmp_pos': 8.0,
     'b_norm_g': 8.0,
     'b_b_ada': 8.0,
     'final_norm_g': 2.73}
    for name, (base, spread) in spreads.items():
        noise = np.random.default_rng([zlib.crc32(name.encode()), seed]).standard_normal(out[name].shape)
        drawn = base * np.exp(spread * noise) if base else spread * noise
        out[name] = __import__('jax').numpy.asarray(drawn.astype(out[name].dtype))
    for name, factor in factors.items():
        out[name] = (out[name] * factor).astype(out[name].dtype)
    return out
```

```python
from contextlib import ExitStack

import numpy as np
import concourse.bass as bass
from concourse import mybir

F32 = mybir.dt.float32
BF16 = mybir.dt.bfloat16
I32 = mybir.dt.int32
ALU = mybir.AluOpType
ACT = mybir.ActivationFunctionType
AX = mybir.AxisListType.X

P = 128
SEQ, DEC, PAST = 1024, 8, 1024
TOK = SEQ + DEC
DM = 1024
NC = DM // P
H, HDIM, KVH = 16, 64, 2
PAIRS = H // 2
QB = SEQ // P
WIN_A, WIN_B = 128, 512
CB, SB = 32, 64
NCB = PAST // CB
PAGES = PAST // P
THIRD = TOK // 3
NBIAS = PAST + P
NADA = 64
NTOK1 = DEC + 1
COPIES = 32
BIG = 1e30
SCALE = HDIM ** -0.5
EPS = 1e-6
CM_PAGES = 24

C_ID, C_CM, C_DN, C_DH, C_GS, C_FAR, C_EN, C_JW, C_M4, C_END = 0, 128, 384, 392, 408, 536, 664, 792, 808, 812
V_GA, V_GKV, V_GB, V_GF, V_BIAS, V_SINK, V_SINKS, V_POS, V_END = 0, 8, 16, 24, 32, 96, 112, 113, 145


def pair_plan(phase):
    branches = ["a"] if phase == "a" else ["cmp", "sel", "win"]
    jobs = [(b, s) for b in branches for s in range(2)]
    units, groups, plan = [], [], []
    for j, (b, s) in enumerate(jobs):
        if b == "cmp":
            units.append(dict(job=j, b=b, s=s, qb=None, keys=QB * NCB, first=0))
            continue
        for qb in range(QB):
            blocks = {"a": min(qb + 1, 2), "sel": qb + 1, "win": min(qb + 1, 5)}[b]
            units.append(dict(job=j, b=b, s=s, qb=qb, keys=blocks * P, first=qb + 1 - blocks))
    copies = 0
    for u, un in enumerate(units):
        un["groups"] = []
        n = 2 if un["b"] == "cmp" else -(-un["keys"] // 512)
        for i in range(n):
            groups.append(dict(kind="p", unit=u, part=i, last=(i == n - 1 and (u + 1 == len(units) or units[u + 1]["job"] != un["job"]))))
            un["groups"].append(groups[-1])
    pending, ended, turned = None, [], []

    def flush():
        nonlocal pending
        if pending is not None:
            plan.append(("pv", pending))
            if pending["last"]:
                ended.append(units[pending["unit"]]["job"])
            pending = None

    def turn(b):
        for half in range(2):
            g = dict(kind="o", b=b, part=half)
            plan.append(("tr", g))
            plan.append(("mix", g))

    for u in range(min(2, len(units))):
        plan += [("qk", u), ("sm", u), ("ex", u)]
    for u, un in enumerate(units):
        if u + 2 < len(units):
            plan.append(("qk", u + 2))
        for g in un["groups"]:
            plan.append(("tr", g))
            plan.append(("ev", g))
            flush()
            pending = g
        if turned:
            turn(turned.pop())
        while ended:
            j = ended.pop()
            plan.append(("oe", j))
            if j % 2:
                turned.append(jobs[j][0])
        if u + 2 < len(units):
            plan += [("sm", u + 2), ("ex", u + 2)]
    flush()
    plan.append(("oe", ended.pop()))
    turn(jobs[-1][0])
    n = c = m = 0
    order = []
    for what, g in plan:
        if what == "tr":
            g["n"] = n
            n += 1
            order.append(g)
            if g["kind"] == "p":
                g["c"] = c
                c += 1
            else:
                g["m"] = m
                m += 1
    for u, un in enumerate(units):
        un["trs"] = max(g["n"] for g in un["groups"]) + 1
    return dict(branches=branches, jobs=jobs, units=units, plan=plan, order=order,
                U=len(units), N=n, C=c, M=m, J=len(jobs))


def build(nc, t):
    ctx = ExitStack()
    with ctx:
        def sb(name, shape, dt=F32):
            return ctx.enter_context(nc.sbuf_tensor(name, shape, dt))

        sems = {}

        def sem(name):
            if name not in sems:
                sems[name] = ctx.enter_context(nc.semaphore(name))
            return sems[name]

        XT = sb("XT", [P, NC, TOK])
        HT = sb("HT", [P, NC, TOK])
        MT = sb("MT", [P, NC, TOK])
        KD = sb("KD", [P, 2, KVH, TOK])
        VT = sb("VT", [P, 2, QB, P])
        STR = sb("STR", [P, 2, SEQ])
        WR = sb("WR", [P, 8 * 1024 + 64])
        PB = sb("PB", [P, 3, TOK])
        PT = sb("PT", [P, 2, 512])
        QT = sb("QT", [P, TOK])
        OS = sb("OS", [P, QB, P])
        QS = sb("QS", [P, DEC * 144])
        ADA = sb("ADA", [P, NADA, NTOK1])
        AG = sb("AG", [P, 3, NC, NTOK1])
        CST = sb("CST", [P, C_END])
        VEC = sb("VEC", [P, V_END])
        CE = sb("CE", [P, NC, NTOK1])
        IDB = sb("IDB", [P, P], BF16)
        FARB = sb("FARB", [P, P], BF16)
        ONE = sb("ONE", [P, 2])
        EPT = sb("EPT", [P, 1])
        RS = sb("RS", [P, QB + 1])
        NM = sb("NM", [P, 3, QB])
        DEN = sb("DEN", [P, 6, QB])
        RG = sb("RG", [P, QB])
        NSK = sb("NSK", [P, H + 1])
        SZS = sb("SZS", [P, 3, NC, DEC])
        SG = sb("SG", [P, QB, 3 * H])
        SGS = sb("SGS", [P, 3])
        CKP = sb("CKP", [P, 8 * 8])
        CKS = sb("CKS", [P, DEC, NCB])
        CV = sb("CV", [P, 3, P])
        W2 = sb("W2", [P, 2, HDIM])
        PC = sb("PC", [P, 2])
        PCH = sb("PCH", [P, 2])
        KN = sb("KN", [P, 3, DEC])
        VN = sb("VN", [DEC, 3, P])
        PGT = sb("PGT", [1, DEC * PAGES], I32)
        SS = sb("SS", [P, 512])
        PS = ctx.enter_context(nc.psum_tensor("PS", [P, 8, 512], F32))
        PSf = PS[:, :, :].rearrange("p b n -> p (b n)")

        ident = CST[:, C_ID:C_ID + P]
        GL = STR[:, :, :].rearrange("p a n -> p (a n)")[:, 0:TOK]
        Hf = HT[:, :, :].rearrange("p c n -> p (c n)")
        Mf = MT[:, :, :].rearrange("p c n -> p (c n)")
        CM = [Mf[:, i * CM_PAGES * P:(i + 1) * CM_PAGES * P] for i in range(2)]
        TAB = QT[0:32, 0:DEC * H]
        CT = QT[:, P:P + NC * NTOK1].rearrange("p (c n) -> p c n", c=NC)
        OSf = OS[:, :, :].rearrange("p b n -> p (b n)")
        HS, HX, CK = OSf[:, 0:192], OSf[:, 192:384], OSf[:, 384:960]
        W1 = WR[:, 4096:8192].rearrange("p (k b h) -> p k b h", k=2, b=16)
        KDf = KD[:, :, :, :].rearrange("p a b n -> p (a b n)")

        def slot(i, base=None):
            w = WR if base is None else base
            return w[:, i * 1024:(i + 1) * 1024].rearrange("p (k m) -> p k m", m=P)

        SZ = {"a": WR[:, 7224:8256], "cmp": WR[:, 5160:6192], "sel": WR[:, 6192:7224], "win": WR[:, 7224:8256]}
        BR = {"a": 0, "cmp": 0, "sel": 1, "win": 2}
        KSRC = {"a": 0, "sel": 0, "win": 1}
        DN = {"a": 1, "cmp": 2, "sel": 3, "win": 4}
        DPT = {"a": 2, "cmp": 3, "sel": 5, "win": 7}
        NRM = {"a": 0, "b": 1, "f": 2}
        ADA0 = {"a": 0, "kv": 24, "b": 40}
        plans = {ph: pair_plan(ph) for ph in "ab"}
        CHUNKS = {"a": 2, "b": 4}
        L_A0, L_A, L_AO, L_KV, L_GL, L_B, L_BO = 0, 3, 19, 27, 35, 36, 68
        W_A0, W_A, W_AO, W_KV, W_GL, W_B = (3, 3, 3, 3), (4, 4, 4, 3), (12, 12, 4, 3), (14, 14, 6, 5), 7, (16, 16, 8, 8)

        def lin_set(i):
            return PS[:, 3 * (i % 2):3 * (i % 2) + 3, 0:THIRD]

        def third(ap):
            return ap.rearrange("p (a n) -> p a n", a=3)

        block = ctx.enter_context(nc.Block())

        @block.sync
        def _(sp):
            sp.dma_start(CT[:, :, :], t["c"]).then_inc(sem("c_in"), 16)
            sp.dma_start(CST[:, :], t["const"]).then_inc(sem("const_in"), 16)
            sp.dma_start(VEC[:, :], t["vec"]).then_inc(sem("vec_in"), 16)
            for s in range(8):
                sp.dma_start(slot(s), t["w_ada"][s]).then_inc(sem(f"w_full{s}"), 16)
            sp.dma_start(TAB[:, :], t["table"]).then_inc(sem("table_in"), 16)
            sp.dma_start(Mf[0:32, 0:NBIAS], t["onehot"]).then_inc(sem("table_in"), 16)
            sp.dma_start(Mf[:, 2048:2048 + NBIAS], t["causal"]).then_inc(sem("table_in"), 16)
            sp.dma_start(PGT[:, :], t["pages"]).then_inc(sem("pages_in"), 16)
            sp.dma_start(W2[:, :, :], t["w2"]).then_inc(sem("w2_in"), 16)
            for c in range(NC):
                sp.dma_start(XT[:, c, :], t["x"][:, c, :]).then_inc(sem(f"x_in{c % 2}"), 16)
            sp.dma_start(t["o_sa_k"], t["sa_kT"][:, :, 1:WIN_A]).then_inc(sem("stored"), 16)
            sp.dma_start(t["o_sa_v"], t["sa_v"][:, 1:WIN_A, :]).then_inc(sem("stored"), 16)
            sp.dma_start(t["o_sw_k"], t["sw_kT"][:, :, 1:WIN_B]).then_inc(sem("stored"), 16)
            sp.dma_start(t["o_sw_v"], t["sw_v"][:, 1:WIN_B, :]).then_inc(sem("stored"), 16)
            with sp.Fori(1, 3) as it:
                for s in range(8):
                    sp.wait_ge(sem("ada_mm"), (it - 1) * 8 + s + 1)
                    sp.dma_start(slot(s), t["w_ada"][bass.ds(it * 8 + s, 1)].rearrange("o p k m -> (o p) k m"))\
                      .then_inc(sem(f"w_full{s}"), 16)
            sp.wait_ge(sem("bias_row"), 1)
            for m in range(COPIES // DEC):
                sp.dma_start(t["scratch"][m * P:(m + 1) * P], PB[:, 0:2, :].rearrange("p a n -> p (a n)")[:, 0:NBIAS])\
                  .then_inc(sem("scratch"), 16)
            for s in range(3):
                sp.wait_ge(sem("ada_mm"), 16 + s + 1)
                sp.dma_start(slot(s), t["w_a0"][s]).then_inc(sem(f"w_full{s}"), 16)
            sp.wait_ge(sem("lin_ev"), L_A)
            for g in range(KVH):
                rows = slice(g * HDIM, (g + 1) * HDIM)
                sp.dma_start(t["o_kv_a"][0, rows, :], KD[rows, 0, g, SEQ - WIN_A:TOK]).then_inc(sem("stored"), 16)
            sp.dma_start(t["o_kv_a"][1], PB[:, 0, SEQ - WIN_A:TOK]).then_inc(sem("a_v_stored"), 16)
            sp.wait_ge(sem("a_v_stored"), 16)
            sp.wait_ge(sem("scratch"), 16 * COPIES // DEC)

            def loads(ph):
                pl, C = plans[ph], CHUNKS[ph]
                base = {"a": L_A, "b": L_B}[ph]
                with sp.Fori(0, PAIRS) as it:
                    for k in range(C):
                        sp.wait_ge(sem("lin_mm"), it * C + base - C + k + 1)
                        sp.dma_start(slot(k), t["w_" + ph][bass.ds(it * C + k, 1)].rearrange("o p k m -> (o p) k m"))\
                          .then_inc(sem(f"w_full{k}"), 16)
                    if ph == "a":
                        for k in range(5):
                            sp.wait_ge(sem("ada_mm"), it * 5 + 19 + k + 1)
                            sp.dma_start(slot(2 + k), t["w_ada"][bass.ds(it * 5 + 24 + k, 1)].rearrange("o p k m -> (o p) k m"))\
                              .then_inc(sem(f"ada_full{k}"), 16)
                    sp.wait_ge(sem(ph + "_sm"), it * pl["U"])
                    for a in range(P // COPIES):
                        strip = bass.AP(t["scratch"].tensor, P - a * COPIES, [[NBIAS, H], [H * NBIAS - 1, COPIES], [1, SEQ]])
                        sp.dma_start(STR[a * COPIES:(a + 1) * COPIES, :, :],
                                     strip[bass.ds(it * 2, 2)].rearrange("s p n -> p s n")).then_inc(sem(ph + "_strips"), 16)

            loads("a")
            sp.wait_ge(sem("lin_mm"), L_AO)
            sp.dma_start(Hf[:, 0:1024].rearrange("p (n k) -> p n k", n=DEC), t["sa_kT"].rearrange("n d k -> d n k"))\
              .then_inc(sem("a_dkv_in"), 16)
            sp.dma_start(Hf[:, 1024:2048].rearrange("p (n k) -> p n k", n=DEC), t["sa_v"].rearrange("n k d -> k n d"))\
              .then_inc(sem("a_dkv_in"), 16)
            sp.wait_ge(sem("a_sm"), PAIRS * plans["a"]["U"])

            def bias_rows(name):
                sp.dma_start(STR[:, :, :].rearrange("p a n -> p (a n)")[:, 0:NBIAS], t["scratch"][0:P]).then_inc(sem(name), 16)

            bias_rows("a_rows_in")
            with sp.Fori(0, 2) as it:
                for k in range(4):
                    sp.wait_ge(sem("lin_mm"), it * 4 + L_AO - 4 + k + 1)
                    if k in (2, 3):
                        sp.wait_ge(sem("ada_mm"), 64)
                    sp.dma_start(slot(k), t["w_ao"][bass.ds(it * 4 + k, 1)].rearrange("o p k m -> (o p) k m"))\
                      .then_inc(sem(f"w_full{k}"), 16)
            for k in range(8):
                sp.wait_ge(sem("lin_mm"), L_KV - 4 + k + 1)
                sp.dma_start(slot(k % 4), t["w_kv"][k]).then_inc(sem(f"w_full{k % 4}"), 16)
            sp.wait_ge(sem("ada_mm"), 64)
            sp.wait_ge(sem("a_mix"), PAIRS * plans["a"]["M"])
            sp.dma_start(WR[:, 4096:8192], t["w1"]).then_inc(sem("w1_in"), 16)
            sp.wait_ge(sem("lin_ev"), L_KV + 8)
            for j, part in ((0, KD[:, 0]), (1, KD[:, 1])):
                for g in range(KVH):
                    rows = slice(g * HDIM, (g + 1) * HDIM)
                    sp.dma_start(t["o_kv"][2 + 2 * j, rows, :], KD[rows, j, g, :]).then_inc(sem("stored"), 16)
            sp.dma_start(t["o_kv"][0], PB[:, 0, :]).then_inc(sem("kv_stored"), 16)
            sp.dma_start(t["o_kv"][1], PB[:, 1, :]).then_inc(sem("kv_stored"), 16)
            sp.dma_start(t["o_kv"][3], PB[:, 2, :]).then_inc(sem("kv_stored"), 16)
            sp.dma_start(t["o_kv"][5], QT[:, :]).then_inc(sem("kv_stored"), 16)
            sp.wait_ge(sem("lin_mm"), L_KV + 8)
            sp.dma_start(slot(3), t["w_gl"]).then_inc(sem("w_full3"), 16)
            sp.wait_ge(sem("pages_in"), 16)
            sp.wait_ge(sem("b_mod"), 1)
            sp.wait_ge(sem("b_mod_act"), 4)
            for st in range(6):
                k, third_ = divmod(st, 3)
                if st >= 2:
                    sp.wait_ge(sem("cm_mm"), st - 1)
                with sp.Fori(0, 24 if third_ < 2 else 16) as i:
                    page = sp.value_load(PGT[0:1, bass.ds(i + third_ * CM_PAGES, 1)], min_val=0, max_val=79)
                    sp.dma_start(CM[st % 2][:, bass.ds(i * P, P)],
                                 t["cmp_pool"][bass.ds(page, 1), k].rearrange("o p n -> (o p) n"))\
                      .then_inc(sem(f"cm_full{st % 2}"), 16)
            sp.wait_ge(sem("kv_stored"), 64)
            sp.wait_ge(sem("gl_ev"), 2)
            loads("b")
            sp.wait_ge(sem("lin_mm"), L_BO)
            with sp.Fori(0, DEC) as n:
                with sp.Fori(0, PAGES) as j:
                    page = sp.value_load(PGT[0:1, bass.ds(n * PAGES + j, 1)], min_val=0, max_val=79)
                    sp.dma_start(Hf[:, bass.ds((n * PAGES + j) * P, P)],
                                 t["sel_kT"][bass.ds(page, 1)].rearrange("o p n -> (o p) n")).then_inc(sem("sel_k_in"), 16)
            sp.wait_ge(sem("b_sm"), PAIRS * plans["b"]["U"])
            bias_rows("b_rows_in")
            sp.wait_ge(sem("b_mix"), PAIRS * plans["b"]["M"])
            with sp.Fori(0, DEC) as n:
                with sp.Fori(0, PAGES) as j:
                    page = sp.value_load(PGT[0:1, bass.ds(n * PAGES + j, 1)], min_val=0, max_val=79)
                    sp.dma_start(WR[:, bass.ds((n * PAGES + j) * P, P)],
                                 t["sel_v"][bass.ds(page, 1)].rearrange("o p n -> (o p) n")).then_inc(sem("sel_v_in"), 16)
            sp.wait_ge(sem("b_qk"), PAIRS * plans["b"]["U"])
            for k in range(4):
                sp.dma_start(slot(k, KDf), t["w_bo"][k]).then_inc(sem(f"wo_full{k}"), 16)
            sp.wait_ge(sem("d_qk"), DN["sel"])
            sp.dma_start(Hf[:, 0:4096].rearrange("p (n k) -> p n k", n=DEC), t["sw_kT"].rearrange("n d k -> d n k"))\
              .then_inc(sem("win_dkv_in"), 16)
            sp.dma_start(Hf[:, 4096:8192].rearrange("p (n j k) -> p n j k", n=DEC, j=4),
                         t["sw_v"].rearrange("n (j k) d -> k n j d", j=4)).then_inc(sem("win_dkv_in"), 16)
            for k in range(4):
                sp.wait_ge(sem("lin_mm"), L_BO + k + 1)
                sp.dma_start(slot(k, KDf), t["w_bo"][4 + k]).then_inc(sem(f"wo_full{k}"), 16)
            for c in range(NC):
                sp.wait_ge(sem("y_out"), c + 1)
                sp.dma_start(t["o_y"][:, c, :], HT[:, c, :]).then_inc(sem("stored"), 16)
            sp.wait_ge(sem("stored"), 16 * (4 + 2 + 4 + NC))

        @block.tensor
        def _(pe):
            def product(set_, w, rhs, m=P):
                for k in range(NC):
                    for a in range(3):
                        last = pe.matmul(PS[0:m, 3 * set_ + a, 0:THIRD], w[:, k, 0:m],
                                         rhs[:, k, a * THIRD:(a + 1) * THIRD],
                                         start=(k == 0), stop=(k == NC - 1))
                last.then_inc(sem("lin_mm"), 1)

            def ada(w, bank, i):
                for k in range(NC):
                    last = pe.matmul(PS[:, bank, i * NTOK1:(i + 1) * NTOK1], w[:, k, :], CE[:, k, :],
                                     start=(k == 0), stop=(k == NC - 1))
                last.then_inc(sem("ada_mm"), 1)

            def norm(name):
                pe.wait_ge(sem("sq"), NRM[name] * NC + NC)
                for i in range(QB + 1):
                    m = P if i < QB else DEC
                    for c in range(NC):
                        last = pe.matmul(PS[0:m, 6, i:i + 1], HT[:, c, i * P:i * P + m], ONE[:, 0:1],
                                         start=(c == 0), stop=(c == NC - 1))
                last.then_inc(sem("ms"), 1)
                pe.wait_ge(sem("rstd"), NRM[name] * 2 + 2)
                for i in range(QB + 1):
                    m = P if i < QB else DEC
                    last = pe.matmul(PSf[:, i * P:i * P + m], RS[0:m, i:i + 1].to_broadcast([m, P]),
                                     CST[0:m, C_ID:C_ID + m], start=True, stop=True)
                last.then_inc(sem("rb"), 1)

            pe.wait_ge(sem("table_in"), 48)
            for a in range(3):
                last = pe.matmul(PS[:, 3 + a, 0:384], TAB[:, :],
                                 Mf[0:32, a * 384:(a + 1) * 384], start=True, stop=True)
            last.then_inc(sem("row_mm"), 1)
            pe.wait_ge(sem("silu_c"), 1)
            with pe.Fori(0, 3) as it:
                for s in range(8):
                    if s % 4 == 0:
                        pe.wait_ge(sem("ada_ev"), it * 2)
                    pe.wait_ge(sem(f"w_full{s}"), it * 16 + 16)
                    ada(slot(s), s // 4, s % 4)
            pe.wait_ge(sem("ada_ev"), 6)
            pe.wait_ge(sem("ones"), 1)
            pe.wait_ge(sem("const_in"), 16)
            norm("a")
            pe.wait_ge(sem("a_mod"), 1)
            pe.wait_ge(sem("a_mod_act"), 4)
            for k in range(3):
                pe.wait_ge(sem(f"w_full{k}"), 16 * (W_A0[k] + 1))
                if k == 1:
                    pe.wait_ge(sem("row_ev"), 1)
                if k == 2:
                    pe.wait_ge(sem("lin_ev"), 1)
                product(k % 2, slot(k), HT)
            pe.wait_ge(sem("lin_ev"), L_A)

            def turn_values(src, new, tag):
                for i in range(QB):
                    last = pe.transpose(PS[:, 4 + i // 4, (i % 4) * P:(i % 4 + 1) * P], src[:, i * P:(i + 1) * P], ident)
                pe.transpose(PS[0:DEC, 6, 0:P], src[:, SEQ:TOK], ident).then_inc(sem(tag), 1)

            turn_values(PB[:, 0, :], 0, "a_vt")
            pe.wait_ge(sem("a_vt_ev"), 2)

            def pairs(ph):
                pl, C = plans[ph], CHUNKS[ph]
                base, wbase = {"a": (L_A, W_A), "b": (L_B, W_B)}[ph]
                units, jobs = pl["units"], pl["jobs"]
                for g in range(KVH):
                    with pe.Fori(g * PAIRS // 2, (g + 1) * PAIRS // 2) as it:
                        pe.wait_ge(sem(ph + "_sm"), it * pl["U"])
                        pe.wait_ge(sem(ph + "_eva"), it * ((pl["C"] + 1) // 2))
                        pe.wait_ge(sem(ph + "_evd"), it * (pl["C"] // 2))
                        pe.wait_ge(sem(ph + "_mix"), it * pl["M"])
                        pe.wait_ge(sem(ph + "_oe"), it * pl["J"])
                        for k in range(C):
                            pe.wait_ge(sem(f"w_full{k}"), it * 16 + 16 * (wbase[k] + 1))
                            pe.wait_ge(sem("lin_ev"), it * C + base + (k - 1 if k else 0))
                            product(k % 2, slot(k), HT)
                        if ph == "a":
                            for k in range(5):
                                pe.wait_ge(sem(f"ada_full{k}"), it * 16 + 16)
                                ada(slot(2 + k), 7, k)
                        pe.wait_ge(sem("lin_ev"), it * C + base + C)
                        for what, x in pl["plan"]:
                            if what == "qk":
                                un = units[x]
                                if x >= 2:
                                    pe.wait_ge(sem(ph + "_sm"), it * pl["U"] + x - 1)
                                rows = slice(un["s"] * HDIM, (un["s"] + 1) * HDIM)
                                if un["b"] == "cmp":
                                    for qb in range(QB):
                                        keys = CKP[rows, :].rearrange("p (j g b) -> p j g b", j=8, g=2)[:, :, g, :]
                                        last = pe.matmul(PS[:, 2 * (x % 2), qb * NCB:(qb + 1) * NCB],
                                                         QT[rows, qb * P:(qb + 1) * P], keys, start=True, stop=True)
                                else:
                                    far = (un["b"] == "a" and un["qb"] >= 1) or (un["b"] == "win" and un["qb"] >= 4)
                                    for k0 in range(0, un["keys"], 512):
                                        n = min(512, un["keys"] - k0)
                                        key0 = un["first"] * P + k0
                                        last = pe.matmul(PS[:, 2 * (x % 2) + k0 // 512, 0:n],
                                                         QT[rows, un["qb"] * P:(un["qb"] + 1) * P],
                                                         KD[rows, KSRC[un["b"]], g, key0:key0 + n],
                                                         start=True, stop=not (far and k0 == 0))
                                        if far and k0 == 0:
                                            last = pe.matmul(PS[:, 2 * (x % 2), 0:P], IDB[:, :], FARB[:, :],
                                                             start=False, stop=True)
                                last.then_inc(sem(ph + "_qk"), 1)
                            elif what == "tr":
                                if x["n"] >= 2:
                                    before = pl["order"][x["n"] - 2]
                                    if before["kind"] == "o":
                                        pe.wait_ge(sem(ph + "_mix"), it * pl["M"] + before["m"] + 1)
                                    elif before["c"] % 2:
                                        pe.wait_ge(sem(ph + "_evd"), it * (pl["C"] // 2) + before["c"] // 2 + 1)
                                    else:
                                        pe.wait_ge(sem(ph + "_eva"), it * ((pl["C"] + 1) // 2) + before["c"] // 2 + 1)
                                bank = 4 + x["n"] % 2
                                if x["kind"] == "o":
                                    job = 2 * pl["branches"].index(x["b"]) + 1
                                    pe.wait_ge(sem(ph + "_oe"), it * pl["J"] + job + 1)
                                    for i in range(4):
                                        last = pe.transpose(PS[:, bank, i * P:(i + 1) * P], OS[:, 4 * x["part"] + i, :], ident)
                                else:
                                    u = x["unit"]
                                    un = units[u]
                                    pe.wait_ge(sem(ph + "_ex"), it * pl["U"] + u + 1)
                                    if un["b"] == "cmp":
                                        for i in range(4):
                                            qb = 4 * x["part"] + i
                                            last = pe.transpose(PS[0:NCB, bank, i * P:(i + 1) * P],
                                                                PB[:, u % 3, qb * NCB:(qb + 1) * NCB], ident)
                                    else:
                                        at = 513 if ph == "a" else 0
                                        for i in range(min(4, un["keys"] // P - 4 * x["part"])):
                                            k0 = at + (4 * x["part"] + i) * P
                                            last = pe.transpose(PS[:, bank, i * P:(i + 1) * P], PB[:, u % 3, k0:k0 + P], ident)
                                last.then_inc(sem(ph + "_tr"), 1)
                            elif what == "pv":
                                u = x["unit"]
                                un = units[u]
                                c = x["c"]
                                if c % 2:
                                    pe.wait_ge(sem(ph + "_evd"), it * (pl["C"] // 2) + c // 2 + 1)
                                else:
                                    pe.wait_ge(sem(ph + "_eva"), it * ((pl["C"] + 1) // 2) + c // 2 + 1)
                                j = un["job"]
                                if j >= 2 and un["qb"] in (None, 0) and x["part"] == 0:
                                    pe.wait_ge(sem(ph + "_oe"), it * pl["J"] + j - 1)
                                if ph == "a" and j == 1 and un["qb"] == 0:
                                    pe.wait_ge(sem("a_ada_ev"), it + 1)
                                if un["b"] == "cmp":
                                    for i in range(4):
                                        qb = 4 * x["part"] + i
                                        last = pe.matmul(PS[:, 6 + j % 2, qb * HDIM:(qb + 1) * HDIM],
                                                         PT[0:NCB, c % 2, i * P:(i + 1) * P],
                                                         CV[0:NCB, 2, g * HDIM:(g + 1) * HDIM], start=True, stop=True)
                                else:
                                    blocks = un["keys"] // P
                                    for i in range(min(4, blocks - 4 * x["part"])):
                                        b = 4 * x["part"] + i
                                        last = pe.matmul(PS[:, 6 + j % 2, un["qb"] * HDIM:(un["qb"] + 1) * HDIM],
                                                         PT[:, c % 2, i * P:(i + 1) * P],
                                                         VT[:, KSRC[un["b"]], un["first"] + b, g * HDIM:(g + 1) * HDIM],
                                                         start=(b == 0), stop=(b == blocks - 1))
                                last.then_inc(sem(ph + "_pv"), 1)

            pairs("a")

            def decode_scores(b, keys, new):
                for k0 in range(0, keys, 512):
                    n_ = min(512, keys - k0)
                    for n in range(DEC):
                        last = pe.matmul(PSf[:, k0:k0 + n_], QS[:, n * P:(n + 1) * P],
                                         (CKS[:, n, :] if b == "cmp" else Hf[:, n * keys + k0:n * keys + k0 + n_]),
                                         start=(n == 0), stop=(n == DEC - 1))
                if new is not None:
                    for n in range(DEC):
                        last = pe.matmul(PSf[:, keys:keys + 1], QS[:, n * P:(n + 1) * P], KN[:, new, n:n + 1],
                                         start=(n == 0), stop=(n == DEC - 1))
                last.then_inc(sem("d_qk"), 1)

            def decode_values(b, keys, values, new):
                pe.wait_ge(sem("d_p"), DN[b])
                for i in range(keys // P):
                    pe.transpose(PSf[:, 2048 + i * P:2048 + (i + 1) * P], PB[:, 2, i * P:(i + 1) * P], ident)
                pe.transpose(PS[0:DEC, 6, 0:P], SS[:, 0:DEC], ident).then_inc(sem("d_tr"), 1)
                pe.wait_ge(sem("d_pt"), DPT[b])
                pe.matmul(PS[:, 7, 0:P], VN[:, new, :], SS[0:DEC, 16:16 + P], start=True, stop=True)
                for n in range(DEC):
                    for i in range(keys // P):
                        last = pe.matmul(PS[:, 7, n * H:(n + 1) * H], values(n, i),
                                         PB[:, 0, i * P + n * H:i * P + (n + 1) * H],
                                         start=False, stop=True,
                                         skip_group_check=True)
                last.then_inc(sem("d_pv"), 1)

            plA, plB = plans["a"], plans["b"]
            pe.wait_ge(sem("a_dkv_in"), 32)
            pe.wait_ge(sem("a_mix"), PAIRS * plA["M"])
            pe.wait_ge(sem("a_oe"), PAIRS * plA["J"])
            decode_scores("a", WIN_A, 0)
            decode_values("a", WIN_A, lambda n, i: Hf[:, 1024 + n * P:1024 + (n + 1) * P], 0)

            pe.wait_ge(sem("d_out"), DN["a"])
            pe.wait_ge(sem("lin_ev"), L_AO)
            with pe.Fori(0, 2) as it:
                for k in range(4):
                    pe.wait_ge(sem(f"w_full{k}"), it * 16 + 16 * (W_AO[k] + 1))
                    pe.wait_ge(sem("lin_ev"), it * 4 + L_AO + (k - 1 if k else 0))
                    product(k % 2, slot(k), MT)
            pe.wait_ge(sem("lin_ev"), L_KV)
            norm("b")
            pe.wait_ge(sem("kv_mod"), 1)
            pe.wait_ge(sem("kv_mod_act"), 4)
            for k in range(8):
                pe.wait_ge(sem(f"w_full{k % 4}"), 16 * (W_KV[k % 4] + k // 4 + 1))
                if k:
                    pe.wait_ge(sem("lin_ev"), L_KV + k - 1)
                product(k % 2, slot(k % 4), HT)
            pe.wait_ge(sem("lin_ev"), L_KV + 8)
            turn_values(PB[:, 2, :], 0, "sel_vt")
            pe.wait_ge(sem("sel_vt_ev"), 2)
            turn_values(QT[:, :], 1, "win_vt")
            pe.wait_ge(sem("win_vt_ev"), 2)
            pe.wait_ge(sem("b_mod"), 1)
            pe.wait_ge(sem("b_mod_act"), 4)
            pe.wait_ge(sem("w_full3"), 16 * (W_GL + 1))
            product(0, slot(3), HT, 3 * H)
            pe.wait_ge(sem("lin_ev"), L_GL + 1)
            for i in range(QB):
                last = pe.transpose(PS[:, 6, i * 3 * H:(i + 1) * 3 * H], GL[0:3 * H, i * P:(i + 1) * P], CST[0:3 * H, C_ID:C_ID + 3 * H])
            pe.transpose(PS[0:DEC, 7, 0:3 * H], GL[0:3 * H, SEQ:TOK], CST[0:3 * H, C_ID:C_ID + 3 * H])\
              .then_inc(sem("gl_tr"), 1)
            pe.wait_ge(sem("gl_ev"), 2)
            pe.matmul(PS[:, 6, 0:3 * H], CST[0:DEC, C_EN:C_EN + P], SS[0:DEC, 0:3 * H], start=True, stop=True)\
              .then_inc(sem("gs_mm"), 1)
            pe.wait_ge(sem("w1_in"), 16)
            pe.wait_ge(sem("w2_in"), 16)
            for k in range(2):
                for b in range(16):
                    last = pe.matmul(PS[:, 3, k:k + 1], W1[:, k, b, :], VEC[:, V_POS + 16 * k + b:V_POS + 16 * k + b + 1],
                                     start=(b == 0), stop=(b == 15))
            last.then_inc(sem("pc_mm"), 1)
            for st in range(6):
                k, third_ = divmod(st, 3)
                loads_ = sum(24 if s % 3 < 2 else 16 for s in range(st % 2, st + 1, 2))
                pe.wait_ge(sem(f"cm_full{st % 2}"), 16 * loads_)
                if third_ == 2:
                    pe.wait_ge(sem("cm_own"), k + 1)
                if st >= 2:
                    pe.wait_ge(sem("hid"), st - 1)
                for b in range(16):
                    last = pe.matmul(PS[:, st % 2, 0:CM_PAGES * 8], W1[:, k, b, :], CM[st % 2][:, b::16],
                                     start=(b == 0), stop=(b == 15))
                last.then_inc(sem("cm_mm"), 1)
                pe.wait_ge(sem("hid"), st + 1)
                if st:
                    pe.wait_ge(sem("ckv_ev"), min(st, 3))
                if k == 0:
                    for half in range(2):
                        last = pe.matmul(PS[half * HDIM:(half + 1) * HDIM, 2, 0:CM_PAGES * 8], W2[:, 0, :], HS[:, :],
                                         start=True, stop=True)
                else:
                    hs = HX.rearrange("p (n g c) -> p n g c", n=3, g=2)
                    for n in range(3):
                        for g in range(KVH):
                            q, at = (3 * third_ + n) % 4 * NCB, (3 * third_ + n) // 4 * P + g * HDIM
                            last = pe.matmul(PS[q:q + NCB, 2, at:at + HDIM], hs[:, n, g], W2[:, 1, :], start=True, stop=True)
                last.then_inc(sem("ckv_mm"), 1)
            pe.wait_ge(sem("ckv_ev"), 5)
            pe.wait_ge(sem("gs_ev"), 1)
            pe.wait_ge(sem("lin_ev"), L_B)
            pairs("b")
            pe.wait_ge(sem("b_mix"), PAIRS * plB["M"])
            pe.wait_ge(sem("b_oe"), PAIRS * plB["J"])
            decode_scores("cmp", NCB, None)
            pe.wait_ge(sem("d_p"), DN["cmp"])
            pe.matmul(PS[:, 1, 0:NCB], CST[:, C_GS:C_GS + P], PB[:, 1, 0:NCB], start=True, stop=True).then_inc(sem("imp_mm"), 1)
            pe.transpose(PS[:, 4, 0:P], PB[:, 2, 0:P], ident).then_inc(sem("d_tr"), 1)
            pe.wait_ge(sem("d_pt"), DPT["cmp"])
            for i in range(2):
                last = pe.matmul(PS[:, 7, i * 4 * H:(i + 1) * 4 * H], CV[:, i, :], PB[:, 0, i * 4 * H:(i + 1) * 4 * H],
                                 start=True, stop=True)
            last.then_inc(sem("d_pv"), 1)
            pe.wait_ge(sem("sel_k_in"), 16 * DEC * PAGES)
            pe.wait_ge(sem("imp_done"), 1)
            decode_scores("sel", PAST, 1)
            pe.wait_ge(sem("d_out"), DN["cmp"])
            pe.wait_ge(sem("sel_v_in"), 16 * DEC * PAGES)
            decode_values("sel", PAST, lambda n, i: WR[:, (n * PAGES + i) * P:(n * PAGES + i + 1) * P], 1)
            pe.wait_ge(sem("win_dkv_in"), 32)
            decode_scores("win", WIN_B, 2)
            pe.wait_ge(sem("d_out"), DN["sel"])
            decode_values("win", WIN_B, lambda n, i: Hf[:, 4096 + (n * 4 + i) * P:4096 + (n * 4 + i + 1) * P], 2)
            pe.wait_ge(sem("d_out"), DN["win"])
            for k in range(8):
                pe.wait_ge(sem(f"wo_full{k % 4}"), 16 * (k // 4 + 1))
                pe.wait_ge(sem("lin_ev"), L_BO + (k - 1 if k else 0))
                product(k % 2, slot(k % 4, KDf), MT)
            pe.wait_ge(sem("lin_ev"), L_BO + 8)
            norm("f")

        @block.scalar
        def _(act):
            act.wait_ge(sem("c_in"), 16)
            act.activation(CE[:, :, :], CT[:, :, :], ACT.Tanh, scale=0.5).then_inc(sem("tanh_c"), 1)

            def norm(name, ready):
                for c in range(NC):
                    ready(c)
                    act.activation(HT[:, c, :], XT[:, c, :], ACT.Square).then_inc(sem("sq"), 1)
                act.wait_ge(sem("ms"), NRM[name] + 1)
                act.activation(RS[:, 0:QB], PS[:, 6, 0:QB], ACT.Sqrt, scale=1.0 / DM, bias=EPT[:, :]).then_inc(sem("std"), 1)
                act.activation(RS[0:DEC, QB:QB + 1], PS[0:DEC, 6, QB:QB + 1], ACT.Sqrt, scale=1.0 / DM, bias=EPT[0:DEC, :])\
                   .then_inc(sem("std"), 1)

            def modulate(name, src, part):
                act.wait_ge(sem(name + "_ag"), 1)
                for c in range(1, NC, 2):
                    act.activation(HT[:, c, 0:SEQ], src[:, c, 0:SEQ], ACT.Identity, scale=AG[:, part, c, 0:1],
                                   bias=ADA[:, ADA0[name] + c, 0:1]).then_inc(sem(name + "_mod_act"), 1)

            act.wait_ge(sem("ones"), 2)

            def first(c):
                if c == 0:
                    act.wait_ge(sem("x_in0"), 64)
                    act.wait_ge(sem("x_in1"), 64)

            norm("a", first)
            act.wait_ge(sem("a_y"), NC)
            modulate("a", HT, 0)
            act.wait_ge(sem("a_vt"), 1)
            act.activation(VT[:, 0, :, :].rearrange("p b n -> p (b n)"), PSf[:, 2048:3072], ACT.Copy).then_inc(sem("a_vt_ev"), 1)

            def pairs(ph):
                pl, C = plans[ph], CHUNKS[ph]
                base = {"a": L_A, "b": L_B}[ph]
                units = pl["units"]
                with act.Fori(0, PAIRS) as it:
                    for k in range(1, C):
                        act.wait_ge(sem("lin_mm"), it * C + base + k + 1)
                        if k == 1:
                            act.wait_ge(sem(ph + "_tr"), it * pl["N"])
                        act.activation(third(PB[:, k % 3, :]), lin_set(k), ACT.Tanh, scale=0.5).then_inc(sem(ph + "_tanh"), 1)
                    for what, x in pl["plan"]:
                        if what == "ex":
                            un = units[x]
                            act.wait_ge(sem(ph + "_sm"), it * pl["U"] + x + 1)
                            if un["b"] == "cmp":
                                act.activation(PB[:, x % 3, 0:un["keys"]], PB[:, x % 3, 0:un["keys"]], ACT.Exp)\
                                   .then_inc(sem(ph + "_ex"), 1)
                            elif ph == "a":
                                act.activation(PB[:, x % 3, 512:513 + un["keys"]], PB[:, x % 3, 0:1 + un["keys"]], ACT.Exp,
                                               scale=-1.0, bias=NM[:, x % 3, 0:1],
                                               accum_out=DEN[:, un["job"], un["qb"]:un["qb"] + 1]).then_inc(sem(ph + "_ex"), 1)
                            else:
                                act.activation(PB[:, x % 3, 0:un["keys"]], PB[:, x % 3, 0:un["keys"]], ACT.Exp,
                                               scale=-1.0, bias=NM[:, x % 3, 0:1],
                                               accum_out=DEN[:, un["job"], un["qb"]:un["qb"] + 1]).then_inc(sem(ph + "_ex"), 1)
                        elif what == "ev" and x["c"] % 2 == 0:
                            c, un = x["c"], units[x["unit"]]
                            act.wait_ge(sem(ph + "_tr"), it * pl["N"] + x["n"] + 1)
                            act.wait_ge(sem(ph + "_pv"), it * pl["C"] + max(c - 1, 0))
                            m = NCB if un["b"] == "cmp" else P
                            n = 512 if un["b"] == "cmp" else min(512, un["keys"] - 512 * x["part"])
                            act.activation(PT[0:m, c % 2, 0:n], PS[0:m, 4 + x["n"] % 2, 0:n], ACT.Copy).then_inc(sem(ph + "_eva"), 1)

            pairs("a")

            def decode(b, keys, extra):
                act.wait_ge(sem("d_sm"), DN[b])
                act.activation(PB[:, 1, 0:keys + extra], PB[:, 0, 0:keys + extra], ACT.Exp, scale=-1.0,
                               bias=SS[:, 200:201], accum_out=SS[:, 201:202]).then_inc(sem("d_ex"), 1)
                act.wait_ge(sem("d_tr"), DN[b])
                if b == "cmp":
                    act.activation(PB[:, 0, 0:P], PS[:, 4, 0:P], ACT.Copy).then_inc(sem("d_pt"), 1)
                else:
                    act.activation(PB[:, 0, 0:keys], PSf[:, 2048:2048 + keys], ACT.Copy).then_inc(sem("d_pt"), 1)

            decode("a", WIN_A, 2)
            norm("b", lambda c: act.wait_ge(sem("lin_ev"), L_AO + c + 1))
            act.wait_ge(sem("b_y"), NC)
            modulate("kv", MT, 1)
            act.wait_ge(sem("sel_vt"), 1)
            act.activation(VT[:, 0, :, :].rearrange("p b n -> p (b n)"), PSf[:, 2048:3072], ACT.Copy).then_inc(sem("sel_vt_ev"), 1)
            act.wait_ge(sem("win_vt"), 1)
            act.activation(VT[:, 1, :, :].rearrange("p b n -> p (b n)"), PSf[:, 2048:3072], ACT.Copy).then_inc(sem("win_vt_ev"), 1)
            act.wait_ge(sem("lin_mm"), L_KV + 8)
            modulate("b", MT, 2)
            act.wait_ge(sem("lin_mm"), L_GL + 1)
            act.activation(third(GL[0:3 * H, :]), PS[0:3 * H, 0:3, 0:THIRD], ACT.Tanh, scale=0.5).then_inc(sem("gl_tanh"), 1)
            act.wait_ge(sem("pc_ev"), 2)
            for st in range(6):
                act.wait_ge(sem("cm_mm"), st + 1)
                if st:
                    act.wait_ge(sem("hid"), st)
                    act.wait_ge(sem("ckv_mm"), st)
                act.activation(HX[:, :], PS[:, st % 2, 0:CM_PAGES * 8], ACT.Tanh, scale=0.5, bias=PCH[:, st // 3:st // 3 + 1])\
                   .then_inc(sem("hid_tanh"), 1)
            pairs("b")
            decode("cmp", NCB, 0)
            decode("sel", PAST, 1)
            decode("win", WIN_B, 1)
            norm("f", lambda c: act.wait_ge(sem("lin_ev"), L_BO + c + 1))

        @block.vector
        def _(dve):
            chain = [0]

            def step(ins):
                chain[0] += 1
                ins.then_inc(sem("dve_step"), 1)
                dve.wait_ge(sem("dve_step"), chain[0])

            dve.memset(ONE[:, :], 1.0).then_inc(sem("ones"), 1)
            dve.memset(EPT[:, :], EPS).then_inc(sem("ones"), 1)
            dve.memset(QS[:, :], 0.0).then_inc(sem("qs_zero"), 1)
            dve.wait_ge(sem("tanh_c"), 1)
            step(dve.scalar_tensor_tensor(CE[:, :, :].rearrange("p a b -> p (a b)"), CE[:, :, :].rearrange("p a b -> p (a b)"), 1.0,
                                          CT[:, :, :].rearrange("p a b -> p (a b)"), ALU.add, ALU.mult))
            dve.tensor_scalar(CE[:, :, :], CE[:, :, :], 0.5, None, ALU.mult).then_inc(sem("silu_c"), 1)
            dve.wait_ge(sem("row_mm"), 1)
            row = PB[:, 0:2, :].rearrange("p a n -> p (a n)")[:, 0:NBIAS]
            dve.scalar_tensor_tensor(row.rearrange("p (a n) -> p a n", a=3), PS[:, 3:6, 0:384], 1.0 / SCALE,
                                     Mf[:, 2048:2048 + NBIAS].rearrange("p (a n) -> p a n", a=3), ALU.mult, ALU.add)\
               .then_inc(sem("bias_row"), 1)
            dve.wait_ge(sem("bias_row"), 1)
            dve.wait_ge(sem("const_in"), 16)
            dve.wait_ge(sem("vec_in"), 16)
            dve.tensor_copy(IDB[:, :], ident)
            dve.tensor_copy(FARB[:, :], CST[:, C_FAR:C_FAR + P])
            dve.tensor_scalar(NSK[:, :], VEC[:, V_SINK:V_SINK + H + 1], -1.0, None, ALU.mult).then_inc(sem("row_ev"), 1)
            dve.wait_ge(sem("row_ev"), 1)
            with dve.Fori(0, 3) as it:
                for b in range(2):
                    dve.wait_ge(sem("ada_mm"), it * 8 + 4 * b + 4)
                    dve.tensor_tensor(ADA[:, bass.ds(it * 8 + 4 * b, 4), :],
                                      PS[:, b, 0:4 * NTOK1].rearrange("p (a n) -> p a n", a=4),
                                      VEC[:, bass.ds(it * 8 + V_BIAS + 4 * b, 4)].unsqueeze(2).to_broadcast([P, 4, NTOK1]), ALU.add)\
                       .then_inc(sem("ada_ev"), 1)
            dve.wait_ge(sem("ada_ev"), 6)

            def gains(name, part, g0):
                a0 = ADA0[name]
                dve.scalar_tensor_tensor(AG[:, part, :, :], ADA[:, a0 + NC:a0 + 2 * NC, :], 1.0,
                                         VEC[:, g0:g0 + NC].unsqueeze(2).to_broadcast([P, NC, NTOK1]), ALU.add, ALU.mult)\
                   .then_inc(sem(name + "_ag"), 1)
                dve.wait_ge(sem(name + "_ag"), 1)

            gains("a", 0, V_GA)

            def norm(name, dst):
                dve.wait_ge(sem("std"), NRM[name] * 2 + 2)
                dve.reciprocal(RS[:, 0:QB], RS[:, 0:QB]).then_inc(sem("rstd"), 1)
                dve.reciprocal(RS[0:DEC, QB:QB + 1], RS[0:DEC, QB:QB + 1]).then_inc(sem("rstd"), 1)
                dve.wait_ge(sem("rb"), NRM[name] + 1)
                for c in range(NC):
                    if dst is None:
                        dve.scalar_tensor_tensor(HT[:, c, :], XT[:, c, :], VEC[:, V_GF + c:V_GF + c + 1], PSf[:, 0:TOK],
                                                 ALU.mult, ALU.mult).then_inc(sem("y_out"), 1)
                    else:
                        dve.tensor_tensor(dst[:, c, :], XT[:, c, :], PSf[:, 0:TOK], ALU.mult).then_inc(sem(name + "_y"), 1)

            def modulate(name, src, part):
                a0 = ADA0[name]
                for c in range(0, NC, 2):
                    dve.tensor_scalar(HT[:, c, 0:SEQ], src[:, c, 0:SEQ], AG[:, part, c, 0:1], ADA[:, a0 + c, 0:1],
                                      ALU.mult, ALU.add)
                step(dve.tensor_tensor(HT[:, :, SEQ:TOK], src[:, :, SEQ:TOK], AG[:, part, :, 1:NTOK1], ALU.mult))
                dve.tensor_tensor(HT[:, :, SEQ:TOK], HT[:, :, SEQ:TOK], ADA[:, a0:a0 + NC, 1:NTOK1], ALU.add)\
                   .then_inc(sem(name + "_mod"), 1)

            norm("a", HT)
            dve.wait_ge(sem("a_y"), NC)
            modulate("a", HT, 0)
            dve.wait_ge(sem("scratch"), 16 * COPIES // DEC)
            for k, dst in enumerate((KD[:, 0, 0, :], KD[:, 0, 1, :], PB[:, 0, :])):
                dve.wait_ge(sem("lin_mm"), L_A0 + k + 1)
                dve.tensor_copy(third(dst), lin_set(k)).then_inc(sem("lin_ev"), 1)
            dve.wait_ge(sem("lin_ev"), L_A)

            def new_keys(j, kd):
                for g in range(KVH):
                    rows = slice(g * HDIM, (g + 1) * HDIM)
                    dve.tensor_copy(KN[rows, j, :], KD[rows, kd, g, SEQ:TOK]).then_inc(sem("new_keys"), 1)

            new_keys(0, 0)
            dve.wait_ge(sem("a_vt"), 1)
            dve.tensor_copy(VN[:, 0, :], PS[0:DEC, 6, 0:P]).then_inc(sem("a_vt_ev"), 1)
            dve.wait_ge(sem("a_v_stored"), 16)
            dve.wait_ge(sem("qs_zero"), 1)

            def pairs(ph):
                pl, C = plans[ph], CHUNKS[ph]
                base = {"a": L_A, "b": L_B}[ph]
                units, jobs = pl["units"], pl["jobs"]
                RC = sum(1 if b == "a" else 3 if b == "cmp" else 2 for b, _ in jobs)
                CC = 4 * sum(1 for un in units if un["b"] == "cmp")
                for g in range(KVH):
                    with dve.Fori(g * PAIRS // 2, (g + 1) * PAIRS // 2) as it:
                        dve.wait_ge(sem("lin_mm"), it * C + base + 1)
                        dve.tensor_copy(third(QT[:, :]), lin_set(0)).then_inc(sem("lin_ev"), 1)
                        dve.wait_ge(sem("lin_ev"), it * C + base + 1)
                        for s in range(2):
                            dve.tensor_copy(QS[g * HDIM:(g + 1) * HDIM, :].rearrange("p (n x) -> p n x", x=144)
                                            [:, :, bass.ds(it * 2 + s, 1)].rearrange("p n o -> p (n o)"),
                                            QT[s * HDIM:(s + 1) * HDIM, SEQ:TOK]).then_inc(sem("qs_set"), 1)
                        for k in range(1, C):
                            b = pl["branches"][k - 1]
                            dve.wait_ge(sem(ph + "_tanh"), it * (C - 1) + k)
                            dve.scalar_tensor_tensor(third(SZ[b]), third(PB[:, k % 3, :]), 1.0, lin_set(k), ALU.add, ALU.mult)\
                               .then_inc(sem("lin_ev"), 1)
                            dve.wait_ge(sem("lin_ev"), it * C + base + k + 1)
                            dve.tensor_copy(SZS[:, BR[b], bass.ds(it, 1), :].rearrange("p o n -> p (o n)"), SZ[b][:, SEQ:TOK])\
                               .then_inc(sem("szs_set"), 1)
                        if ph == "a":
                            dve.wait_ge(sem("ada_mm"), it * 5 + 24 + 5)
                            dve.tensor_tensor(ADA[:, bass.ds(it * 5 + 24, 5), :],
                                              PS[:, 7, 0:5 * NTOK1].rearrange("p (a n) -> p a n", a=5),
                                              VEC[:, bass.ds(it * 5 + V_BIAS + 24, 5)].unsqueeze(2).to_broadcast([P, 5, NTOK1]), ALU.add)\
                               .then_inc(sem("a_ada_ev"), 1)
                            for s in range(3):
                                dve.tensor_copy(PB[:, s, 0:1], NSK[:, bass.ds(it * 2, 1)]).then_inc(sem("sink_set"), 1)
                        for what, x in pl["plan"]:
                            if what == "sm":
                                un = units[x]
                                L = un["keys"]
                                if x == 0:
                                    dve.wait_ge(sem(ph + "_strips"), it * 64 + 64)
                                if ph == "a" and x < 3:
                                    dve.wait_ge(sem("sink_set"), it * 6 + 3)
                                if x >= 3:
                                    dve.wait_ge(sem(ph + "_tr"), it * pl["N"] + units[x - 3]["trs"])
                                if ph == "a" and QB <= x < QB + 3:
                                    dve.tensor_scalar(PB[:, x % 3, 0:1], NSK[:, bass.ds(it * 2 + 1, 1)], 1.0, None, ALU.mult).then_inc(sem("sink_set"), 1)
                                    dve.wait_ge(sem("sink_set"), it * 6 + 3 + x - QB + 1)
                                if un["b"] == "cmp":
                                    cc = 3 * x
                                    dve.wait_ge(sem(ph + "_qk"), it * pl["U"] + x + 1)
                                    xx = PB[:, x % 3, 0:L]
                                    x3 = xx.rearrange("p (q c) -> p q c", q=QB)
                                    dve.scalar_tensor_tensor(xx, PS[:, 2 * (x % 2), 0:L], -SCALE, CST[:, C_CM:C_CM + L],
                                                             ALU.mult, ALU.add).then_inc(sem("cmp_step"), 1)
                                    dve.wait_ge(sem("cmp_step"), it * CC + cc + 1)
                                    dve.tensor_reduce(NM[:, x % 3, :], x3, AX, ALU.min).then_inc(sem("cmp_step"), 1)
                                    dve.wait_ge(sem("cmp_step"), it * CC + cc + 2)
                                    dve.tensor_scalar(NM[:, x % 3, :], NM[:, x % 3, :], BIG / 10, None, ALU.min).then_inc(sem("cmp_step"), 1)
                                    dve.wait_ge(sem("cmp_step"), it * CC + cc + 3)
                                    dve.scalar_tensor_tensor(x3, x3, -1.0, NM[:, x % 3, :].unsqueeze(2).to_broadcast([P, QB, NCB]),
                                                             ALU.mult, ALU.add).then_inc(sem(ph + "_sm"), 1)
                                else:
                                    at = 1 if ph == "a" else 0
                                    dve.wait_ge(sem(ph + "_qk"), it * pl["U"] + x + 1)
                                    dve.memset(NM[:, x % 3, 1:2], 0.0)
                                    dve.tensor_tensor_reduce(PB[:, x % 3, at:at + L], PSf[:, 1024 * (x % 2):1024 * (x % 2) + L],
                                                             STR[:, un["s"], SEQ - L:SEQ], -SCALE,
                                                             (PB[:, x % 3, 0:1] if ph == "a" else 3 * BIG), ALU.add, ALU.min,
                                                             NM[:, x % 3, 0:1]).then_inc(sem(ph + "_sm"), 1)
                            elif what == "ev" and x["c"] % 2:
                                c, un = x["c"], units[x["unit"]]
                                if un["b"] == "cmp" and x["part"] == 1:
                                    dve.wait_ge(sem(ph + "_ex"), it * pl["U"] + x["unit"] + 1)
                                    dve.tensor_reduce(DEN[:, un["job"], :], PB[:, x["unit"] % 3, 0:un["keys"]]
                                                      .rearrange("p (q c) -> p q c", q=QB), AX, ALU.add).then_inc(sem("cmp_step"), 1)
                                dve.wait_ge(sem(ph + "_tr"), it * pl["N"] + x["n"] + 1)
                                dve.wait_ge(sem(ph + "_pv"), it * pl["C"] + max(c - 1, 0))
                                m = NCB if un["b"] == "cmp" else P
                                n = 512 if un["b"] == "cmp" else min(512, un["keys"] - 512 * x["part"])
                                dve.tensor_copy(PT[0:m, c % 2, 0:n], PS[0:m, 4 + x["n"] % 2, 0:n]).then_inc(sem(ph + "_evd"), 1)
                            elif what == "oe":
                                b, s = jobs[x]
                                rc0 = sum(1 if jobs[i][0] == "a" else 3 if jobs[i][0] == "cmp" else 2 for i in range(x))
                                lastg = [g_ for un in units if un["job"] == x for g_ in un["groups"]][-1]
                                dve.wait_ge(sem(ph + "_pv"), it * pl["C"] + lastg["c"] + 1)
                                if b == "cmp":
                                    dve.wait_ge(sem("cmp_step"), it * CC + 6 + x + 1)
                                    dve.tensor_scalar(DEN[:, x, :], DEN[:, x, :], 1.0 / BIG, None, ALU.max).then_inc(sem(ph + "_rc"), 1)
                                    rc0 += 1
                                    dve.wait_ge(sem(ph + "_rc"), it * RC + rc0)
                                dve.wait_ge(sem(ph + "_oe"), it * pl["J"] + x)
                                dve.reciprocal(RG[:, :], DEN[:, x, :]).then_inc(sem(ph + "_rc"), 1)
                                rc0 += 1
                                dve.wait_ge(sem(ph + "_rc"), it * RC + rc0)
                                if ph == "b":
                                    dve.tensor_tensor(RG[:, :], RG[:, :],
                                                      SG[:, :, bass.ds(it * 2 + BR[b] * H + s, 1)].rearrange("p q o -> p (q o)"),
                                                      ALU.mult).then_inc(sem(ph + "_rc"), 1)
                                    rc0 += 1
                                    dve.wait_ge(sem(ph + "_rc"), it * RC + rc0)
                                if x >= 2 and s == 0:
                                    og = [o for o in pl["order"] if o["kind"] == "o" and o["b"] == jobs[x - 1][0]][-1]
                                    dve.wait_ge(sem(ph + "_tr"), it * pl["N"] + og["n"] + 1)
                                dve.tensor_tensor(OS[:, :, s * HDIM:(s + 1) * HDIM],
                                                  PS[:, 6 + x % 2, :].rearrange("p (q d) -> p q d", q=QB),
                                                  RG[:, :].unsqueeze(2).to_broadcast([P, QB, HDIM]), ALU.mult).then_inc(sem(ph + "_oe"), 1)
                            elif what == "mix":
                                half = slice(512 * x["part"], 512 * x["part"] + 512)
                                dve.wait_ge(sem(ph + "_tr"), it * pl["N"] + x["n"] + 1)
                                out = MT[:, bass.ds(it, 1), half].rearrange("p o n -> p (o n)")
                                if x["b"] == pl["branches"][0]:
                                    dve.scalar_tensor_tensor(out, PS[:, 4 + x["n"] % 2, :], 0.5, SZ[x["b"]][:, half],
                                                             ALU.mult, ALU.mult).then_inc(sem(ph + "_mix"), 1)
                                else:
                                    ms = x["m"] - 1
                                    dve.scalar_tensor_tensor(SS[:, :], PS[:, 4 + x["n"] % 2, :], 0.5, SZ[x["b"]][:, half],
                                                             ALU.mult, ALU.mult).then_inc(sem("mix_step"), 1)
                                    dve.wait_ge(sem("mix_step"), it * (pl["M"] - 2) + ms)
                                    dve.wait_ge(sem(ph + "_mix"), it * pl["M"] + x["m"] - 1)
                                    dve.tensor_tensor(out, out, SS[:, :], ALU.add).then_inc(sem(ph + "_mix"), 1)
                                    dve.wait_ge(sem(ph + "_mix"), it * pl["M"] + x["m"] + 1)

            pairs("a")
            dve.wait_ge(sem("szs_set"), 8)
            dve.wait_ge(sem("sink_set"), 48)

            def decode(b, keys, extra, new):
                dve.wait_ge(sem("d_qk"), DN[b])
                nm, den, r = SS[:, 200:201], SS[:, 201:202], SS[:, 202:203]
                if b == "cmp":
                    step(dve.tensor_scalar(PB[:, 0, 0:keys], PSf[:, 0:keys], -SCALE, None, ALU.mult))
                    dve.tensor_reduce(nm, PB[:, 0, 0:keys], AX, ALU.min).then_inc(sem("d_sm"), 1)
                else:
                    if b == "a":
                        dve.tensor_copy(PB[:, 0, keys + 1:keys + 2], NSK[:, H:H + 1])
                    dve.tensor_tensor_reduce(PB[:, 0, 0:keys + 1], PSf[:, 0:keys + 1],
                                             STR[:, :, :].rearrange("p a n -> p (a n)")[:, PAST - keys:PAST + 1], -SCALE,
                                             (NSK[:, H:H + 1] if b == "a" else 3 * BIG), ALU.add, ALU.min, nm)\
                       .then_inc(sem("d_sm"), 1)
                dve.wait_ge(sem("d_ex"), DN[b])
                step(dve.reciprocal(r, den))
                if b == "cmp":
                    step(dve.tensor_scalar(PB[:, 1, 0:keys], PB[:, 1, 0:keys], r, None, ALU.mult))
                    dve.scalar_tensor_tensor(PB[:, 2, 0:P].rearrange("p (r c) -> p r c", r=4),
                                             PB[:, 1, 0:keys].unsqueeze(1).to_broadcast([P, 4, keys]), SGS[:, 0:1],
                                             CST[:, C_M4:C_M4 + 4].unsqueeze(2).to_broadcast([P, 4, keys]), ALU.mult, ALU.mult)\
                       .then_inc(sem("d_p"), 1)
                    return
                gate = ONE[:, 0:1] if b == "a" else SGS[:, BR[b]:BR[b] + 1]
                step(dve.tensor_scalar(PB[:, 2, 0:keys + 1], PB[:, 1, 0:keys + 1], r, gate, ALU.mult, ALU.mult))
                dve.tensor_scalar(SS[:, 0:DEC], CST[:, C_DN:C_DN + DEC], PB[:, 2, keys:keys + 1], None, ALU.mult)\
                   .then_inc(sem("d_p"), 1)
                dve.wait_ge(sem("d_tr"), DN[b])
                dve.tensor_copy(SS[0:DEC, 16:16 + P], PS[0:DEC, 6, 0:P]).then_inc(sem("d_pt"), 1)

            def decode_out(b, first_):
                dve.wait_ge(sem("d_pv"), DN[b])
                os_ = SS[:, 256:320].rearrange("p (c n) -> p c n", c=NC)
                for g in range(KVH):
                    for s in range(2):
                        src = PS[g * HDIM:(g + 1) * HDIM, 7, 0:P].rearrange("p (n g c s) -> p g s c n", n=DEC, g=2, s=2)[:, g, s]
                        ins = dve.tensor_copy(os_[s * HDIM:(s + 1) * HDIM, 4 * g:4 * g + 4, :], src)
                step(ins)
                out = MT[:, :, SEQ:TOK]
                if first_:
                    dve.scalar_tensor_tensor(out, os_, 0.5, SZS[:, BR[b], :, :], ALU.mult, ALU.mult).then_inc(sem("d_out"), 1)
                else:
                    o2 = SS[:, 320:384].rearrange("p (c n) -> p c n", c=NC)
                    step(dve.scalar_tensor_tensor(o2, os_, 0.5, SZS[:, BR[b], :, :], ALU.mult, ALU.mult))
                    dve.tensor_tensor(out, out, o2, ALU.add).then_inc(sem("d_out"), 1)
                dve.wait_ge(sem("d_out"), DN[b])

            dve.wait_ge(sem("a_rows_in"), 16)
            dve.wait_ge(sem("new_keys"), 2)
            decode("a", WIN_A, 2, 0)
            decode_out("a", True)

            def residual(base, name, a0, c, k, looped):
                gate = ADA[:, bass.ds(c + a0, 1), :].rearrange("p o n -> p (o n)") if looped else ADA[:, a0 + c, :]
                x = XT[:, bass.ds(c, 1), :].rearrange("p o n -> p (o n)") if looped else XT[:, c, :]
                b0 = 3 * (k % 2)
                dve.tensor_tensor(SS[:, 384:392], PS[:, b0 + 2, 2 * P + 80:THIRD], gate[:, 1:NTOK1], ALU.mult).then_inc(sem("res_step"), 1)
                for a in range(3):
                    n = THIRD if a < 2 else THIRD - DEC
                    dve.scalar_tensor_tensor(x[:, a * THIRD:a * THIRD + n], PS[:, b0 + a, 0:n], gate[:, 0:1],
                                             x[:, a * THIRD:a * THIRD + n], ALU.mult, ALU.add)
                return x

            with dve.Fori(0, 2) as it:
                for k in range(4):
                    dve.wait_ge(sem("lin_mm"), it * 4 + L_AO + k + 1)
                    dve.wait_ge(sem("lin_ev"), it * 4 + L_AO + k)
                    x = residual(L_AO, "a", 16, it * 4 + k, k, True)
                    dve.wait_ge(sem("res_step"), it * 4 + k + 1)
                    dve.tensor_tensor(x[:, SEQ:TOK], x[:, SEQ:TOK], SS[:, 384:392], ALU.add).then_inc(sem("lin_ev"), 1)
            dve.wait_ge(sem("a_ada_ev"), 8)
            gains("kv", 1, V_GKV)
            gains("b", 2, V_GB)
            norm("b", MT)
            dve.wait_ge(sem("b_y"), NC)
            modulate("kv", MT, 1)
            kv_dst = (PB[:, 0, :], PB[:, 1, :], KD[:, 0, 0, :], KD[:, 0, 1, :], PB[:, 2, :], KD[:, 1, 0, :], KD[:, 1, 1, :], QT[:, :])
            for k, dst in enumerate(kv_dst):
                dve.wait_ge(sem("lin_mm"), L_KV + k + 1)
                dve.tensor_copy(third(dst), lin_set(k)).then_inc(sem("lin_ev"), 1)
            dve.wait_ge(sem("lin_ev"), L_KV + 8)
            new_keys(1, 0)
            new_keys(2, 1)
            for j, tag in ((1, "sel_vt"), (2, "win_vt")):
                dve.wait_ge(sem(tag), 1)
                dve.tensor_copy(VN[:, j, :], PS[0:DEC, 6, 0:P]).then_inc(sem(tag + "_ev"), 1)
            modulate("b", MT, 2)
            dve.wait_ge(sem("gl_tanh"), 1)
            dve.tensor_scalar(GL[0:3 * H, :], GL[0:3 * H, :], 1.0, 0.5, ALU.add, ALU.mult).then_inc(sem("lin_ev"), 1)
            dve.wait_ge(sem("gl_tr"), 1)
            dve.tensor_copy(SG[:, :, :].rearrange("p q c -> p (q c)"), PS[:, 6, 0:QB * 3 * H]).then_inc(sem("gl_ev"), 1)
            dve.tensor_copy(SS[0:DEC, 0:3 * H], PS[0:DEC, 7, 0:3 * H]).then_inc(sem("gl_ev"), 1)
            dve.wait_ge(sem("gs_mm"), 1)
            own = SS[:, 64:112].rearrange("p (b h) -> p b h", b=3)
            step(dve.tensor_tensor(own, PS[:, 6, 0:3 * H].rearrange("p (b h) -> p b h", b=3),
                                   CST[:, C_DH:C_DH + H].unsqueeze(1).to_broadcast([P, 3, H]), ALU.mult))
            dve.tensor_reduce(SGS[:, :], own, AX, ALU.add).then_inc(sem("gs_ev"), 1)
            dve.wait_ge(sem("gs_ev"), 1)
            dve.wait_ge(sem("pc_mm"), 1)
            dve.tensor_copy(PC[:, :], PS[:, 3, 0:2]).then_inc(sem("pc_ev"), 1)
            dve.tensor_scalar(PCH[:, :], PS[:, 3, 0:2], 0.5, None, ALU.mult).then_inc(sem("pc_ev"), 1)
            dve.wait_ge(sem("pc_ev"), 2)
            for st in range(6):
                k, third_ = divmod(st, 3)
                if third_ == 2:
                    if st >= 2:
                        dve.wait_ge(sem("cm_mm"), st - 1)
                    pages = CM[st % 2][:, 16 * P:24 * P].rearrange("p (j g x) -> p j g x", j=8, g=2)
                    for g in range(KVH):
                        for par in range(2):
                            src = PB[g * HDIM:(g + 1) * HDIM, k, 0:SEQ].rearrange("p (j x r) -> p r j x", j=8, r=2)[:, par]
                            ins = dve.tensor_copy(pages[par * HDIM:(par + 1) * HDIM, :, g, :], src)
                    ins.then_inc(sem("cm_own"), 1)
                dve.wait_ge(sem("hid_tanh"), st + 1)
                if st:
                    dve.wait_ge(sem("ckv_mm"), st)
                n = CM_PAGES * 8
                step(dve.tensor_scalar(HS[:, :], PS[:, st % 2, 0:n], PC[:, k:k + 1], None, ALU.add))
                last = dve.scalar_tensor_tensor(HS[:, :], HX[:, :], 1.0, HS[:, :], ALU.add, ALU.mult)
                if k == 1:
                    step(last)
                    for n_ in range(3):
                        last = dve.tensor_copy(HX.rearrange("p (n g j b) -> p n g j b", n=3, g=2, j=8)[:, n_],
                                               HS.rearrange("p (n j g b) -> p n g j b", n=3, j=8, g=2)[:, n_])
                last.then_inc(sem("hid"), 1)
                dve.wait_ge(sem("ckv_mm"), st + 1)
                if k == 0:
                    dve.tensor_scalar(CK[:, third_ * n:(third_ + 1) * n], PS[:, 2, 0:n], 0.5, None, ALU.mult).then_inc(sem("ckv_ev"), 1)
                elif third_ == 2:
                    dve.tensor_scalar(CV[:, 0:2, :].rearrange("p n c -> p (n c)"), PS[:, 2, 0:2 * P], 0.5, None, ALU.mult)\
                       .then_inc(sem("ckv_ev"), 1)
                    dve.tensor_scalar(CV[0:NCB, 2, :], PS[0:NCB, 2, 2 * P:3 * P], 0.5, None, ALU.mult).then_inc(sem("ckv_ev"), 1)
            dve.wait_ge(sem("ckv_ev"), 5)
            dve.tensor_copy(CKP[:, :], CK[:, 512:576]).then_inc(sem("cks"), 1)
            for g in range(KVH):
                rows = slice(g * HDIM, (g + 1) * HDIM)
                dve.tensor_copy(CKS[rows, :, :].rearrange("p n (j b) -> p (n j) b", b=4),
                                CK[rows, 0:512].rearrange("p (m g b) -> p m g b", g=2, b=4)[:, :, g, :]).then_inc(sem("cks"), 1)
            dve.wait_ge(sem("kv_stored"), 64)
            pairs("b")
            dve.wait_ge(sem("szs_set"), 32)
            dve.wait_ge(sem("qs_set"), 32)
            decode("cmp", NCB, 0, None)
            dve.wait_ge(sem("imp_mm"), 1)
            imp, eq, mn, dr = SS[:, 400:416], SS[:, 416:430], SS[:, 206:207], SS[:, 207:208]
            pen = SS[:, 432:448]
            step(dve.tensor_reduce(imp, PS[:, 1, 0:NCB].rearrange("p (j c) -> p j c", c=2), AX, ALU.add))
            step(dve.tensor_reduce(mn, imp[:, 1:15], AX, ALU.min))
            step(dve.scalar_tensor_tensor(eq, imp[:, 1:15], mn, CST[:, C_JW + 1:C_JW + 15], ALU.is_equal, ALU.mult))
            step(dve.tensor_reduce(dr, eq, AX, ALU.max))
            step(dve.tensor_scalar(pen, CST[:, C_JW:C_JW + 16], dr, -BIG / SCALE, ALU.is_equal, ALU.mult))
            dve.wait_ge(sem("b_rows_in"), 16)
            rowf = STR[:, :, :].rearrange("p a n -> p (a n)")
            row2 = QT
            dve.tensor_tensor(row2[:, 0:PAST].rearrange("p (j x) -> p j x", j=16), rowf[:, 0:PAST].rearrange("p (j x) -> p j x", j=16),
                              pen.unsqueeze(2).to_broadcast([P, 16, SB]), ALU.add)
            dve.tensor_copy(row2[:, PAST:PAST + 1], rowf[:, PAST:PAST + 1]).then_inc(sem("imp_done"), 1)
            dve.wait_ge(sem("imp_done"), 1)
            decode_out("cmp", True)
            dve.wait_ge(sem("d_qk"), DN["sel"])
            dve.wait_ge(sem("new_keys"), 6)
            nm, den, r = SS[:, 200:201], SS[:, 201:202], SS[:, 202:203]
            dve.tensor_tensor_reduce(PB[:, 0, 0:PAST + 1], PSf[:, 0:PAST + 1], row2[:, 0:PAST + 1], -SCALE, 3 * BIG,
                                     ALU.add, ALU.min, nm).then_inc(sem("d_sm"), 1)
            dve.wait_ge(sem("d_ex"), DN["sel"])
            step(dve.reciprocal(r, den))
            step(dve.tensor_scalar(PB[:, 2, 0:PAST + 1], PB[:, 1, 0:PAST + 1], r, SGS[:, 1:2], ALU.mult, ALU.mult))
            dve.tensor_scalar(SS[:, 0:DEC], CST[:, C_DN:C_DN + DEC], PB[:, 2, PAST:PAST + 1], None, ALU.mult).then_inc(sem("d_p"), 1)
            dve.wait_ge(sem("d_tr"), DN["sel"])
            dve.tensor_copy(SS[0:DEC, 16:16 + P], PS[0:DEC, 6, 0:P]).then_inc(sem("d_pt"), 1)
            decode_out("sel", False)
            decode("win", WIN_B, 1, 2)
            decode_out("win", False)
            for k in range(8):
                dve.wait_ge(sem("lin_mm"), L_BO + k + 1)
                dve.wait_ge(sem("lin_ev"), L_BO + k)
                x = residual(L_BO, "b", 56, k, k, False)
                dve.wait_ge(sem("res_step"), 8 + k + 1)
                dve.tensor_tensor(x[:, SEQ:TOK], x[:, SEQ:TOK], SS[:, 384:392], ALU.add).then_inc(sem("lin_ev"), 1)
            norm("f", None)


def kernel(**inputs):
    import concourse.bacc as _bacc
    from concourse.bass_utils import run_bass_kernel_spmd as _run

    f = {k: np.asarray(v) for k, v in inputs.items()}
    chunked = lambda a: np.ascontiguousarray(a.reshape(NC, P, -1).transpose(1, 0, 2))

    def tiles(w):
        return np.ascontiguousarray(w.reshape(NC, P, -1, P).transpose(2, 1, 0, 3))

    def vec(a):
        return a.reshape(-1, P).T

    x = np.concatenate([f["x_prompt"][0], f["x_sample"][:, 0]], 0).T
    c = np.concatenate([f["c_prompt"], f["c_sample"]], 0).T
    wa, wkv, wb = f["a_w_in"][0], f["kv_w_in"], f["b_w_in"][0]
    hd, kvd = H * HDIM, KVH * HDIM

    def both(w):
        return np.concatenate([w, w], 1)

    def kv_cols(w, at):
        return [both(w[:, at:at + HDIM]), both(w[:, at + HDIM:at + 2 * HDIM]), w[:, at + kvd:at + 2 * kvd]]

    w_a0 = np.concatenate(kv_cols(wa, hd), 1)
    pair = lambda w, at, i: w[:, at + i * P:at + (i + 1) * P]
    w_a = np.concatenate([pair(wa, at, i) for i in range(PAIRS) for at in (0, hd + 2 * kvd)], 1)
    w_kv = np.concatenate([wkv[:, 0:2 * kvd]] + kv_cols(wkv, 2 * kvd) + kv_cols(wkv, 4 * kvd), 1)
    w_b = np.concatenate([pair(wb, at, i) for i in range(PAIRS) for at in (0, hd, 2 * hd, 3 * hd)], 1)
    w_gl = np.concatenate([wb[:, 4 * hd:], np.zeros((DM, P - 3 * H), wb.dtype)], 1)
    w_ada = np.concatenate([tiles(f["a_w_ada"][0]), tiles(f["kv_w_ada"]), tiles(f["b_w_ada"][0])], 0)
    sink = f["a_sinks"][0]
    pos = f["cmp_pos"].reshape(16, 2, 2, HDIM).transpose(1, 3, 2, 0).reshape(P, 32)
    vecs = np.concatenate([vec(f["a_norm_g"][0]), vec(f["kv_norm_g"]), vec(f["b_norm_g"][0]), vec(f["final_norm_g"]),
                           vec(f["a_b_ada"][0]), vec(f["kv_b_ada"]), vec(f["b_b_ada"][0]),
                           np.tile(sink, (P, 1)), np.tile(sink, DEC)[:, None], pos], 1)
    w1 = f["cmp_w1"].reshape(2, 16, P, P).transpose(2, 0, 1, 3).reshape(P, 4096)
    w2 = f["cmp_w2"].transpose(1, 0, 2)
    pool = f["cache_cmp_kv"].reshape(-1, 4, 16, 2, 2, KVH, HDIM).transpose(0, 4, 3, 6, 5, 1, 2).reshape(-1, 2, P, P)
    sel, sa, sw = f["cache_sel_kv"], f["state_a_kv"][0], f["state_win_kv"]
    rows = lambda a, k: a[:, :, k].reshape(a.shape[0], a.shape[1], P)

    const = np.zeros((P, C_END), np.float32)
    const[:, C_ID:C_ID + P] = np.eye(P)
    q = np.arange(P)
    ends = np.arange(NCB) * CB + CB - 1
    for qb in range(QB):
        const[:, C_CM + qb * NCB:C_CM + (qb + 1) * NCB] = np.where(ends[None] <= qb * P + q[:, None], 0.0, BIG)
    const[q, C_DN + q // H] = 1.0
    const[q, C_DH + q % H] = 1.0
    const[:, C_GS:C_GS + P] = (q[:, None] // 8 == q[None] // 8)
    const[:, C_FAR:C_FAR + P] = np.where(q[:, None] <= q[None], 0.0, -BIG / SCALE)
    for n in range(DEC):
        const[n, C_EN + n * H:C_EN + (n + 1) * H] = 1.0
    const[:, C_JW:C_JW + 16] = np.arange(1, 17)
    const[q, C_M4 + q // H % 4] = 1.0
    dist = PAST - np.arange(NBIAS)
    n_ = np.maximum(dist, 0)
    large = 16 + (np.log(np.maximum(n_, 16).astype(np.float32) / np.float32(16)) / np.float32(np.log(8.0)) * np.float32(16)).astype(np.int32)
    bucket = np.where(n_ < 16, n_, np.minimum(large, 31))
    onehot = (np.arange(32)[:, None] == bucket[None]).astype(np.float32)
    causal = np.tile(np.where(dist < 0, -BIG / SCALE, 0.0).astype(np.float32), (P, 1))

    ins = dict(
        c=chunked(c), const=const, vec=vecs, w_ada=w_ada, table=np.tile(f["rel_bias_table"], (1, DEC)), onehot=onehot, causal=causal,
        pages=f["page_table"].reshape(1, -1).astype(np.int32), w2=w2, x=chunked(x),
        sa_kT=rows(sa, 0).transpose(0, 2, 1), sa_v=rows(sa, 1), sw_kT=rows(sw, 0).transpose(0, 2, 1), sw_v=rows(sw, 1),
        w_a0=tiles(w_a0), w_a=tiles(w_a), w_ao=tiles(f["a_w_out"][0]), w_kv=tiles(w_kv), w1=w1, w_gl=tiles(w_gl)[0],
        cmp_pool=pool, w_b=tiles(w_b), sel_kT=rows(sel, 0).transpose(0, 2, 1), sel_v=rows(sel, 1), w_bo=tiles(f["b_w_out"][0]),
    )
    outs = dict(o_sa_k=(DEC, P, WIN_A - 1), o_sa_v=(DEC, WIN_A - 1, P), o_sw_k=(DEC, P, WIN_B - 1), o_sw_v=(DEC, WIN_B - 1, P),
                o_kv_a=(2, P, WIN_A + DEC), o_kv=(6, P, TOK), o_y=(P, NC, TOK))
    nc = _bacc.Bacc("TRN2", target_bir_lowering=False, num_devices=1)
    t, arrays = {}, {}
    for name, a in ins.items():
        a = np.ascontiguousarray(a)
        arrays[name] = a
        t[name] = nc.dram_tensor(name, a.shape, mybir.dt.from_np(a.dtype), kind="ExternalInput").ap()
    for name, shape in outs.items():
        t[name] = nc.dram_tensor(name, shape, F32, kind="ExternalOutput").ap()
    t["scratch"] = nc.dram_tensor("scratch", (COPIES * H, NBIAS), F32, kind="Internal").ap()
    build(nc, t)
    r = _run(nc, [arrays], core_ids=[0]).results[0]
    o = {name: np.asarray(r[name]) for name in outs}

    kvr = lambda k, v: np.stack([k, v], 0).reshape(2, KVH, HDIM, -1).transpose(3, 0, 1, 2)
    y = o["o_y"].transpose(1, 0, 2).reshape(DM, TOK).T
    a_new = kvr(o["o_kv_a"][0], o["o_kv_a"][1])
    cmp_r, sel_r, win_r = (kvr(o["o_kv"][2 * i], o["o_kv"][2 * i + 1]) for i in range(3))

    def shifted(k, v, new):
        old = np.stack([k.transpose(0, 2, 1), v], 2).reshape(DEC, -1, 2, KVH, HDIM)
        return np.concatenate([old, new[:, None]], 1)

    return (y[None, :SEQ], y[SEQ:, None],
            a_new[None, None, :WIN_A], shifted(o["o_sa_k"], o["o_sa_v"], a_new[WIN_A:])[None],
            cmp_r[None, :SEQ], cmp_r[SEQ:, None], sel_r[None, :SEQ], sel_r[SEQ:, None],
            win_r[None, SEQ - WIN_B:SEQ], shifted(o["o_sw_k"], o["o_sw_v"], win_r[SEQ:]))
```

```python
from contextlib import ExitStack

import numpy as np
import concourse.bass as bass
from concourse import mybir

F32 = mybir.dt.float32
BF16 = mybir.dt.bfloat16
I32 = mybir.dt.int32
ALU = mybir.AluOpType
ACT = mybir.ActivationFunctionType
AX = mybir.AxisListType.X

P = 128
SEQ, DEC, PAST = 1024, 8, 1024
TOK = SEQ + DEC
DM = 1024
NC = DM // P
H, HDIM, KVH = 16, 64, 2
PAIRS = H // 2
QB = SEQ // P
WIN_A, WIN_B = 128, 512
CB, SB = 32, 64
NCB = PAST // CB
PAGES = PAST // P
NPA = 6
THIRD = TOK // 3
NBIAS = PAST + P
NADA0, NADA = 16, 64
NTOK1 = DEC + 1
COPIES = 32
BIG = 1e30
SCALE = HDIM ** -0.5
EPS = 1e-6
CM_PAGES = 24

C_ID, C_CM, C_DN, C_DH, C_GS, C_FAR, C_EN, C_JW, C_M4, C_END = 0, 128, 384, 392, 408, 536, 664, 792, 808, 812
V_GA, V_GKV, V_GB, V_GF, V_BIAS, V_SINK, V_SINKS, V_POS, V_END = 0, 8, 16, 24, 32, 96, 112, 113, 145


def pair_plan(phase):
    branches = ["a"] if phase == "a" else ["cmp", "sel", "win"]
    jobs = [(b, s) for b in branches for s in range(2)]
    units, groups, plan = [], [], []
    for j, (b, s) in enumerate(jobs):
        if b == "cmp":
            units.append(dict(job=j, b=b, s=s, qb=None, keys=QB * NCB, first=0))
            continue
        for qb in range(QB):
            blocks = {"a": min(qb + 1, 2), "sel": qb + 1, "win": min(qb + 1, 5)}[b]
            units.append(dict(job=j, b=b, s=s, qb=qb, keys=blocks * P, first=qb + 1 - blocks))
    copies = 0
    for u, un in enumerate(units):
        un["groups"] = []
        n = 2 if un["b"] == "cmp" else -(-un["keys"] // 512)
        for i in range(n):
            groups.append(dict(kind="p", unit=u, part=i, last=(i == n - 1 and (u + 1 == len(units) or units[u + 1]["job"] != un["job"]))))
            un["groups"].append(groups[-1])
    pending, ended, turned = None, [], []

    def flush():
        nonlocal pending
        if pending is not None:
            plan.append(("pv", pending))
            if pending["last"]:
                ended.append(units[pending["unit"]]["job"])
            pending = None

    def turn(b):
        for half in range(2):
            g = dict(kind="o", b=b, part=half)
            plan.append(("tr", g))
            plan.append(("mix", g))

    for u in range(min(2, len(units))):
        plan += [("qk", u), ("sm", u), ("ex", u)]
    plan += [("slot", 0), ("slot_end", 0)]
    for u, un in enumerate(units):
        if u + 2 < len(units):
            plan.append(("qk", u + 2))
        for g in un["groups"]:
            plan.append(("tr", g))
            plan.append(("ev", g))
            flush()
            pending = g
            if g is un["groups"][0]:
                plan.append(("slot", u + 1))
        if turned:
            turn(turned.pop())
        while ended:
            j = ended.pop()
            plan.append(("oe", j))
            if j % 2:
                turned.append(jobs[j][0])
        if u + 2 < len(units):
            plan += [("sm", u + 2), ("ex", u + 2)]
        if u + 3 == len(units):
            plan.append(("qc", None))
        plan.append(("slot_end", u + 1))
    flush()
    plan.append(("oe", ended.pop()))
    plan.append(("slot", len(units) + 1))
    turn(jobs[-1][0])
    plan.append(("slot_end", len(units) + 1))
    n = c = m = 0
    order = []
    for what, g in plan:
        if what == "tr":
            g["n"] = n
            n += 1
            order.append(g)
            if g["kind"] == "p":
                g["c"] = c
                c += 1
            else:
                g["m"] = m
                m += 1
    for u, un in enumerate(units):
        un["trs"] = max(g["n"] for g in un["groups"]) + 1
    if phase == "a":
        runs = [("gate", "a", 0, (2, 2, 1)), ("ada", None, 0, (2, 3)), ("q", None, 1, (2, 1, 2)), ("turn", None, 0, (1, 1))]
    else:
        runs = [("gate", "win", 0, (3, 3, 3)), ("gate", "cmp", 1, (3, 3, 3)), ("q", None, 1, (3, 3, 3)), ("gate", "sel", 1, (3, 3, 3))]

    def filled(last):
        fills, slots, at = [], {}, 0
        for kind, b, after, spans in runs:
            for a, span in enumerate(spans):
                if not (last and after):
                    fl = dict(kind=kind, b=b, after=after, third=a, f=len(fills), mm=sum(1 for x in fills if x["kind"] in ("q", "gate")),
                              tanh=sum(1 for x in fills if x["kind"] == "gate"),
                              ev=sum(1 for x in fills if (x["kind"] == "q") == (kind == "q")), before=fills[-1] if fills else None)
                    fills.append(fl)
                    steps = NC
                    for i in range(span):
                        slots[at + i] = (fl, i * steps // span, (i + 1) * steps // span, i == span - 1)
                at += span
        assert at <= len(units) + 2
        out = []
        for what, g in plan:
            if what == "slot":
                if g in slots:
                    fl, k0, k1, end = slots[g]
                    out.append(("fill", (fl, k0, k1)))
                    if end:
                        out.append(("ft", fl))
            elif what == "slot_end":
                if g in slots and slots[g][3]:
                    out.append(("fe", slots[g][0]))
            elif not (what == "qc" and last):
                out.append((what, g))
        return fills, out

    fills, loop_plan = filled(False)
    _, last_plan = filled(True)
    first = [dict(kind=kind, b=b, after=0, third=a, tanh=3 * sum(1 for r in runs[:i] if r[2] and r[0] == "gate") + a)
             for i, (kind, b, after, _) in enumerate(runs) if after for a in range(3)]
    for i, fl in enumerate(first):
        fl["f"] = fl["mm"] = i
        fl["ev"] = fl["third"] if fl["kind"] == "q" else fl["tanh"]
    return dict(branches=branches, jobs=jobs, units=units, plan=loop_plan, last_plan=last_plan, order=order, first=first,
                U=len(units), N=n, C=c, M=m, J=len(jobs), FV=sum(1 for x in fills if x["kind"] != "q"), FM=sum(1 for x in fills if x["kind"] in ("q", "gate")),
                FT=sum(1 for x in fills if x["kind"] == "gate"))


def build(nc, t):
    ctx = ExitStack()
    with ctx:
        def sb(name, shape, dt=F32):
            return ctx.enter_context(nc.sbuf_tensor(name, shape, dt))

        sems = {}

        def sem(name):
            if name not in sems:
                sems[name] = ctx.enter_context(nc.semaphore(name))
            return sems[name]

        XT = sb("XT", [P, NC, TOK])
        HT = sb("HT", [P, NC, TOK])
        MT = sb("MT", [P, NC, TOK])
        KD = sb("KD", [P, 2, KVH, TOK])
        VT = sb("VT", [P, 2, QB, P])
        STR = sb("STR", [P, 2, SEQ])
        WR = sb("WR", [P, 8 * 1024 + 64])
        PB = sb("PB", [P, 3, TOK])
        PT = sb("PT", [P, 2, 512])
        QT = sb("QT", [P, TOK])
        OS = sb("OS", [P, QB, P])
        QS = sb("QS", [P, DEC * 144])
        ADA = sb("ADA", [P, NADA, NTOK1])
        AG = sb("AG", [P, 3, NC, NTOK1])
        CST = sb("CST", [P, C_END])
        VEC = sb("VEC", [P, V_END])
        CE = sb("CE", [P, NC, NTOK1])
        IDB = sb("IDB", [P, P], BF16)
        FARB = sb("FARB", [P, P], BF16)
        ONE = sb("ONE", [P, 2])
        EPT = sb("EPT", [P, 1])
        NM = sb("NM", [P, 3, QB])
        DEN = sb("DEN", [P, 6, QB])
        RG = sb("RG", [P, QB])
        NSK = sb("NSK", [P, H + 1])
        SZS = sb("SZS", [P, 3, NC, DEC])
        SG = sb("SG", [P, QB, 3 * H])
        SGS = sb("SGS", [P, 3])
        CKP = sb("CKP", [P, 8 * 8])
        CKS = sb("CKS", [P, DEC, NCB])
        CV = sb("CV", [P, 3, P])
        W2 = sb("W2", [P, 2, HDIM])
        PC = sb("PC", [P, 2])
        PCH = sb("PCH", [P, 2])
        KN = sb("KN", [P, 3, DEC])
        VN = sb("VN", [DEC, 3, P])
        PGT = sb("PGT", [1, DEC * PAGES], I32)
        SS = sb("SS", [P, 512])
        PS = ctx.enter_context(nc.psum_tensor("PS", [P, 8, 512], F32))
        PSf = PS[:, :, :].rearrange("p b n -> p (b n)")

        ident = CST[:, C_ID:C_ID + P]
        GL = STR[:, :, :].rearrange("p a n -> p (a n)")[:, 0:TOK]
        Hf = HT[:, :, :].rearrange("p c n -> p (c n)")
        Mf = MT[:, :, :].rearrange("p c n -> p (c n)")
        CM = [Mf[:, i * CM_PAGES * P:(i + 1) * CM_PAGES * P] for i in range(2)]
        TAB = QT[0:32, 0:DEC * H]
        CT = QT[:, P:P + NC * NTOK1].rearrange("p (c n) -> p c n", c=NC)
        OSf = OS[:, :, :].rearrange("p b n -> p (b n)")
        RA = KD[0:NTOK1, 0, :, :].rearrange("p a n -> p (a n)")
        HS, HX, CK = OSf[:, 0:192], OSf[:, 192:384], OSf[:, 384:960]
        W1 = WR[:, 4096:8192].rearrange("p (k b h) -> p k b h", k=2, b=16)
        KDf = KD[:, :, :, :].rearrange("p a b n -> p (a b n)")

        def slot(i, base=None):
            w = WR if base is None else base
            return w[:, i * 1024:(i + 1) * 1024].rearrange("p (k m) -> p k m", m=P)

        SZ = {"a": KD[:, 1, 1, :], "cmp": WR[:, 5160:6192], "sel": WR[:, 6192:7224], "win": WR[:, 7224:8256]}
        BR = {"a": 0, "cmp": 0, "sel": 1, "win": 2}
        KSRC = {"a": 0, "sel": 0, "win": 1}
        DN = {"a": 1, "cmp": 2, "sel": 3, "win": 4}
        DPT = {"a": 2, "cmp": 3, "sel": 5, "win": 7}
        NRM = {"a": 0, "b": 1, "f": 2}
        ADA0 = {"a": 0, "kv": 24, "b": 40}
        plans = {ph: pair_plan(ph) for ph in "ab"}
        CHUNKS = {"a": 2, "b": 4}
        SLOT = {"a": 1, "cmp": 1, "sel": 2, "win": 3}
        QN = {"a": KD[:, 1, 0, :], "b": WR[:, 4096:5128]}
        pa = plans["a"]
        FQ = 3 * PAIRS
        FV0 = {"a": 0, "b": PAIRS * 7}
        FV1 = {"a": 0, "b": PAIRS * 7 + 6}
        FM0 = {"a": 0, "b": 3 + (PAIRS - 1) * pa["FM"] + 3}
        FT0 = {"a": 0, "b": PAIRS * 3}
        FM_ALL = FM0["b"] + 3 * 4 * PAIRS
        L_A0, L_A, L_KV, L_GL, L_B = 0, 3, 3, 11, 12
        W_A0, W_A, W_AO, W_KV, W_GL, W_B = (2, 2, 2, 2), (3, 3, 3, 2), (11, 11, 3, 2), (13, 13, 5, 4), 6, (15, 15, 7, 7)

        w_slots = WR[:, 0:8192].rearrange("p (s k m) -> p s k m", s=8, k=NC)
        RP = [CV[:, :, :].rearrange("p n c -> p (n c)")[0:NTOK1, :], SS[0:NTOK1, 0:3 * P]]

        def lin_set(i):
            return PS[:, 3 * (i % 2):3 * (i % 2) + 3, 0:THIRD]

        def third(ap):
            return ap.rearrange("p (a n) -> p a n", a=3)

        block = ctx.enter_context(nc.Block())

        def compression_pages(eng, part, st):
            if st == 0:
                eng.wait_ge(sem("pages_in"), 16)
                eng.wait_ge(sem("b_mod"), 1)
                eng.wait_ge(sem("b_mod_act"), 4)
            k, third_ = divmod(st, 3)
            if st >= 2:
                eng.wait_ge(sem("cm_mm"), st - 1)
            with eng.Fori(0, 8 if third_ < 2 else (6, 5, 5)[part]) as i:
                page = eng.value_load(PGT[0:1, bass.ds(i * 3 + third_ * CM_PAGES + part, 1)], min_val=0, max_val=79)
                eng.dma_start(CM[st % 2][:, bass.ds(i * 3 * P + part * P, P)],
                              t["cmp_pool"][bass.ds(page, 1), k].rearrange("o p n -> (o p) n"))\
                   .then_inc(sem(f"cm_full{part}{st % 2}"), 16)

        def selected_pages(eng, i0, i1, dst, src, loaded):
            with eng.Fori(i0, i1) as i:
                page = eng.value_load(PGT[0:1, bass.ds(i, 1)], min_val=0, max_val=79)
                eng.dma_start(dst[:, bass.ds(i * P, P)], t[src][bass.ds(page, 1)].rearrange("o p n -> (o p) n")).then_inc(sem(loaded), 16)

        @block.gpsimd
        def _(pool):
            for st in range(6):
                compression_pages(pool, 1, st)
            pool.wait_ge(sem("fill_mm"), FM_ALL)
            selected_pages(pool, 0, 40, WR, "sel_v", "sel_v_in")
            last = (PAIRS - 1) * plans["b"]["M"]
            for i, m in enumerate((2, 4, 6)):
                pool.wait_ge(sem("b_mix"), last + m + 1)
                selected_pages(pool, 40 + 8 * i, 48 + 8 * i, WR, "sel_v", "sel_v_in")

        @block.sync
        def _(sp):
            sp.dma_start(CT[:, :, :], t["c"]).then_inc(sem("c_in"), 16)
            sp.dma_start(CST[:, :], t["const"]).then_inc(sem("const_in"), 16)
            sp.dma_start(VEC[:, :], t["vec"]).then_inc(sem("vec_in"), 16)
            for s in range(8):
                sp.dma_start(slot(s), t["w_ada"][s]).then_inc(sem(f"w_full{s}"), 16)
            sp.dma_start(TAB[:, :], t["table"]).then_inc(sem("table_in"), 16)
            sp.dma_start(Mf[0:32, 0:NBIAS], t["onehot"]).then_inc(sem("table_in"), 16)
            sp.dma_start(Mf[:, 2048:2048 + NBIAS], t["causal"]).then_inc(sem("table_in"), 16)
            sp.dma_start(PGT[:, :], t["pages"]).then_inc(sem("pages_in"), 16)
            sp.dma_start(W2[:, :, :], t["w2"]).then_inc(sem("w2_in"), 16)
            for c in range(NC):
                sp.dma_start(XT[:, c, :], t["x"][:, c, :]).then_inc(sem(f"x_in{c % 2}"), 16)
            for s in range(8):
                sp.wait_ge(sem("ada_group"), s // 4 + 1)
                sp.dma_start(slot(s), t["w_ada"][8 + s]).then_inc(sem(f"w_full{s}"), 16)
            sp.wait_ge(sem("bias_row"), 1)
            for m in range(COPIES // DEC):
                sp.dma_start(t["scratch"][m * P:(m + 1) * P], PB[:, 0:2, :].rearrange("p a n -> p (a n)")[:, 0:NBIAS])\
                  .then_inc(sem("scratch"), 16)
            for s in range(3):
                sp.wait_ge(sem("ada_group"), 3)
                sp.dma_start(slot(s), t["w_a0"][s]).then_inc(sem(f"w_full{s}"), 16)
            sp.wait_ge(sem("lin_ev"), L_A)
            for g in range(KVH):
                rows = slice(g * HDIM, (g + 1) * HDIM)
                sp.dma_start(t["o_kv_a"][0, rows, :], KD[rows, 0, g, SEQ - WIN_A:TOK]).then_inc(sem("stored"), 16)
            sp.dma_start(t["o_kv_a"][1], PB[:, 0, SEQ - WIN_A:TOK]).then_inc(sem("a_v_stored"), 16)
            sp.wait_ge(sem("a_v_stored"), 16)
            sp.wait_ge(sem("scratch"), 16 * COPIES // DEC)

            def loads(ph):
                pl, C = plans[ph], CHUNKS[ph]
                base = {"a": L_A, "b": L_B}[ph]
                FM, U = FM0[ph] + len(pl["first"]), pl["U"]

                def chunk(i, k):
                    sp.dma_start(slot(k), t["w_" + ph][bass.ds(i * C + k, 1)].rearrange("o p k m -> (o p) k m"))\
                      .then_inc(sem(f"w_full{k}"), 16)

                def strip(i, s):
                    for a in range(P // COPIES):
                        rows = bass.AP(t["scratch"].tensor, P - a * COPIES, [[NBIAS, H], [H * NBIAS - 1, COPIES], [1, SEQ]])
                        sp.dma_start(STR[a * COPIES:(a + 1) * COPIES, s, :],
                                     rows[bass.ds(i * 2 + s, 1)].rearrange("s p n -> (s p) n")).then_inc(sem(f"strip{s}"), 16)

                for k in range(C):
                    sp.wait_ge(sem("lin_mm"), {"a": k + 1, "b": L_GL + 1 if k == 3 else L_KV + 5 + k}[ph])
                    chunk(0, k)
                if ph == "a":
                    sp.wait_ge(sem("lin_mm"), L_A)
                    for k in range(NPA):
                        sp.dma_start(slot(2 + k), t["w_ada"][NADA0 + k]).then_inc(sem(f"ada_full{k}"), 16)
                for s in range(2):
                    strip(0, s)
                if ph == "a":
                    sp.dma_start(t["o_sa_k"], t["sa_kT"][:, :, 1:WIN_A]).then_inc(sem("stored"), 16)
                    sp.dma_start(t["o_sa_v"], t["sa_v"][:, 1:WIN_A, :]).then_inc(sem("stored"), 16)
                    sp.dma_start(t["o_sw_k"], t["sw_kT"][:, :, 1:WIN_B]).then_inc(sem("stored"), 16)
                    sp.dma_start(t["o_sw_v"], t["sw_v"][:, 1:WIN_B, :]).then_inc(sem("stored"), 16)
                with sp.Fori(0, PAIRS - 1) as it:
                    sp.wait_ge(sem("fill_mm"), it * pl["FM"] + FM)
                    for k in range(C - 1):
                        chunk(it + 1, k)
                    sp.wait_ge(sem("fill_mm"), it * pl["FM"] + FM + 3)
                    chunk(it + 1, C - 1)
                    sp.wait_ge(sem(ph + "_sm"), it * U + U - QB)
                    strip(it + 1, 0)
                    if ph == "a":
                        for k in range(NPA):
                            sp.wait_ge(sem("ada_mm"), it * 2 + k // 3 + 1)
                            sp.dma_start(slot(2 + k), t["w_ada"][bass.ds(it * NPA + NADA0 + NPA + k, 1)].rearrange("o p k m -> (o p) k m"))\
                              .then_inc(sem(f"ada_full{k}"), 16)
                    sp.wait_ge(sem(ph + "_sm"), it * U + U)
                    strip(it + 1, 1)

            loads("a")
            sp.wait_ge(sem("fill_mm"), FM0["b"])
            sp.dma_start(Hf[:, 0:1024].rearrange("p (n k) -> p n k", n=DEC), t["sa_kT"].rearrange("n d k -> d n k"))\
              .then_inc(sem("a_dkv_in"), 16)
            sp.dma_start(Hf[:, 1024:2048].rearrange("p (n k) -> p n k", n=DEC), t["sa_v"].rearrange("n k d -> k n d"))\
              .then_inc(sem("a_dkv_in"), 16)
            sp.wait_ge(sem("a_sm"), PAIRS * plans["a"]["U"])

            def bias_rows(name):
                sp.dma_start(STR[:, :, :].rearrange("p a n -> p (a n)")[:, 0:NBIAS], t["scratch"][0:P]).then_inc(sem(name), 16)

            bias_rows("a_rows_in")
            sp.wait_ge(sem("ada_mm"), 2 * PAIRS)
            for k in range(8):
                if k >= 4:
                    sp.wait_ge(sem("op_mm"), 3 * (k - 3))
                sp.dma_start(slot(k % 4), t["w_ao"][k]).then_inc(sem(f"w_full{k % 4}"), 16)
            for k in range(8):
                if k < 4:
                    sp.wait_ge(sem("op_mm"), 3 * (5 + k))
                else:
                    sp.wait_ge(sem("lin_mm"), L_KV + k - 3)
                sp.dma_start(slot(k % 4), t["w_kv"][k]).then_inc(sem(f"w_full{k % 4}"), 16)
            sp.wait_ge(sem("ada_mm"), 2 * PAIRS)
            sp.wait_ge(sem("a_mix"), PAIRS * plans["a"]["M"] + 1)
            sp.dma_start(WR[:, 4096:8192], t["w1"]).then_inc(sem("w1_in"), 16)
            sp.wait_ge(sem("lin_ev"), L_KV + 8)
            for j, part in ((0, KD[:, 0]), (1, KD[:, 1])):
                for g in range(KVH):
                    rows = slice(g * HDIM, (g + 1) * HDIM)
                    sp.dma_start(t["o_kv"][2 + 2 * j, rows, :], KD[rows, j, g, :]).then_inc(sem("stored"), 16)
            sp.dma_start(t["o_kv"][0], PB[:, 0, :]).then_inc(sem("kv_stored"), 16)
            sp.dma_start(t["o_kv"][1], PB[:, 1, :]).then_inc(sem("kv_stored"), 16)
            sp.dma_start(t["o_kv"][3], PB[:, 2, :]).then_inc(sem("kv_stored"), 16)
            sp.dma_start(t["o_kv"][5], QT[:, :]).then_inc(sem("kv_stored"), 16)
            sp.wait_ge(sem("lin_mm"), L_KV + 8)
            sp.dma_start(slot(3), t["w_gl"]).then_inc(sem("w_full3"), 16)
            for st in range(6):
                compression_pages(sp, 0, st)
            sp.wait_ge(sem("kv_stored"), 64)
            sp.wait_ge(sem("gl_ev"), 2)
            loads("b")
            sp.wait_ge(sem("fill_mm"), FM_ALL)
            selected_pages(sp, 0, DEC * PAGES, Hf, "sel_kT", "sel_k_in")
            sp.wait_ge(sem("b_sm"), PAIRS * plans["b"]["U"])
            bias_rows("b_rows_in")
            sp.wait_ge(sem("b_qk"), PAIRS * plans["b"]["U"])
            for k in range(4):
                sp.dma_start(slot(k, KDf), t["w_bo"][k]).then_inc(sem(f"wo_full{k}"), 16)
            sp.wait_ge(sem("d_qk"), DN["sel"])
            sp.dma_start(Hf[:, 0:4096].rearrange("p (n k) -> p n k", n=DEC), t["sw_kT"].rearrange("n d k -> d n k"))\
              .then_inc(sem("win_dkv_in"), 16)
            sp.dma_start(Hf[:, 4096:8192].rearrange("p (n j k) -> p n j k", n=DEC, j=4),
                         t["sw_v"].rearrange("n (j k) d -> k n j d", j=4)).then_inc(sem("win_dkv_in"), 16)
            for k in range(4):
                sp.wait_ge(sem("op_mm"), 3 * (NC + k + 1))
                sp.dma_start(slot(k, KDf), t["w_bo"][4 + k]).then_inc(sem(f"wo_full{k}"), 16)
            for c in range(NC):
                sp.wait_ge(sem("y_out"), c + 1)
                sp.dma_start(t["o_y"][:, c, :], HT[:, c, :]).then_inc(sem("stored"), 16)
            sp.wait_ge(sem("stored"), 16 * (4 + 2 + 4 + NC))

        @block.tensor
        def _(pe):
            def product(set_, w, rhs, m=P, name=None):
                for a in range(3):
                    if name and a == 2:
                        pe.wait_ge(sem(name + "_mod"), 1)
                    for k in range(NC):
                        if name and a == 0:
                            pe.wait_ge(sem(name + "_mod_act"), k + 1)
                        last = pe.matmul(PS[0:m, 3 * set_ + a, 0:THIRD], w[:, k, 0:m],
                                         rhs[:, k, a * THIRD:(a + 1) * THIRD],
                                         start=(k == 0), stop=(k == NC - 1))
                last.then_inc(sem("lin_mm"), 1)

            def mean_square(name, c):
                pe.wait_ge(sem("sq"), NRM[name] * NC + c + 1)
                for a in range(3):
                    last = pe.matmul(PS[:, 5 + a, 0:THIRD], ONE[:, 1:2].to_broadcast([P, P]), HT[:, c, a * THIRD:(a + 1) * THIRD],
                                     start=(c == 0), stop=(c == NC - 1))
                if c == NC - 1:
                    last.then_inc(sem("ms"), 1)

            def out_projection(name, w, full):
                n0 = 0 if name == "b" else 3 * NC
                for c in range(NC):
                    pe.wait_ge(*full(c))
                    for a in range(3):
                        if 3 * c + a >= 3:
                            pe.wait_ge(sem("op_ev"), n0 + 3 * (c - 1) + a + 1)
                        for k in range(NC):
                            last = pe.matmul(PS[:, a, 0:THIRD], w(c % 4)[:, k, :], MT[:, k, a * THIRD:(a + 1) * THIRD],
                                             start=(k == 0), stop=(k == NC - 1))
                        last.then_inc(sem("op_mm"), 1)
                    if c:
                        mean_square(name, c - 1)
                mean_square(name, NC - 1)

            pe.wait_ge(sem("table_in"), 48)
            for a in range(3):
                last = pe.matmul(PS[:, 5 + a, 0:384], TAB[:, :],
                                 Mf[0:32, a * 384:(a + 1) * 384], start=True, stop=True)
            last.then_inc(sem("row_mm"), 1)
            pe.wait_ge(sem("silu_c"), 1)
            for i in range(NADA0 // 4):
                for s in range(4):
                    pe.wait_ge(sem(f"w_full{4 * (i % 2) + s}"), i // 2 * 16 + 16)
                w4 = w_slots[:, 4 * (i % 2):4 * (i % 2) + 4]
                for k in range(NC):
                    last = pe.matmul(PS[0:NTOK1, i, :], CE[:, k, :], w4[:, :, k, :], start=(k == 0), stop=(k == NC - 1))
                last.then_inc(sem("ada_group"), 1)
            pe.wait_ge(sem("ones"), 1)
            pe.wait_ge(sem("const_in"), 16)
            for c in range(NC):
                if c == 0:
                    pe.wait_ge(sem("bias_row"), 1)
                mean_square("a", c)
            pe.wait_ge(sem("ada_rows"), NADA0 // 4)
            for i in range(NADA0):
                last = pe.transpose(PS[:, 4, i * NTOK1:(i + 1) * NTOK1], RA[:, i * P:(i + 1) * P], CST[0:NTOK1, C_ID:C_ID + NTOK1])
            last.then_inc(sem("ada_turned"), 1)
            for k in range(3):
                pe.wait_ge(sem(f"w_full{k}"), 16 * (W_A0[k] + 1))
                if k == 2:
                    pe.wait_ge(sem("lin_ev"), 1)
                product(k % 2, slot(k), HT, name=None if k else "a")
            pe.wait_ge(sem("lin_ev"), L_A)

            def turn_values(src, new, tag):
                for i in range(QB):
                    last = pe.transpose(PS[:, 4 + i // 4, (i % 4) * P:(i % 4 + 1) * P], src[:, i * P:(i + 1) * P], ident)
                pe.transpose(PS[0:DEC, 6, 0:P], src[:, SEQ:TOK], ident).then_inc(sem(tag), 1)

            turn_values(PB[:, 0, :], 0, "a_vt")
            pe.wait_ge(sem("a_vt_ev"), 2)

            def pairs(ph):
                pl, C = plans[ph], CHUNKS[ph]
                base, wbase = {"a": (L_A, W_A), "b": (L_B, W_B)}[ph]
                units, jobs, first = pl["units"], pl["jobs"], pl["first"]

                def third_product(fl, k0, k1, bank, load):
                    k_ = 0 if fl["kind"] == "q" else SLOT[fl["b"]]
                    if k0 == 0 and fl["third"] == 0:
                        pe.wait_ge(sem(f"w_full{k_}"), load)
                    for k in range(k0, k1):
                        last = pe.matmul(PS[:, bank, 0:THIRD], slot(k_)[:, k, :], HT[:, k, fl["third"] * THIRD:(fl["third"] + 1) * THIRD],
                                         start=(k == 0), stop=(k == NC - 1))
                    if k1 == NC:
                        last.then_inc(sem("fill_mm"), 1)

                for fl in first:
                    if fl["f"] >= 8:
                        pe.wait_ge(sem("fill_ev"), FV0[ph] + 1)
                    third_product(fl, 0, NC, fl["f"] % 8, 16 * (wbase[0 if fl["kind"] == "q" else SLOT[fl["b"]]] + 1))
                pe.wait_ge(sem("q_ev"), (FQ if ph == "b" else 0) + 3)
                if ph == "b":
                    pe.wait_ge(sem("fill_ev"), FV1[ph])

                def pair(g, it, last_):
                        for what, x in pl["last_plan" if last_ else "plan"]:
                            if what == "fill":
                                fl, k0, k1 = x
                                if k0 == 0:
                                    b_ = fl["before"]
                                    if b_ is None:
                                        if ph == "b":
                                            pe.wait_ge(sem("fill_ev"), it * pl["FV"] + FV1[ph])
                                    elif b_["kind"] == "q":
                                        pe.wait_ge(sem("q_ev"), it * 3 + (FQ if ph == "b" else 0) + 3 + b_["ev"] + 1)
                                    else:
                                        pe.wait_ge(sem("fill_ev"), it * pl["FV"] + FV1[ph] + b_["ev"] + 1)
                                if fl["kind"] == "ada":
                                    g3 = 3 * fl["third"]
                                    for k in range(k0, k1):
                                        if k == 0:
                                            for i in range(3):
                                                pe.wait_ge(sem(f"ada_full{g3 + i}"), it * 16 + 16)
                                        last = pe.matmul(PS[0:NTOK1, 7, 0:3 * P], CE[:, k, :], w_slots[:, 2 + g3:5 + g3, k, :],
                                                         start=(k == 0), stop=(k == NC - 1))
                                    if k1 == NC:
                                        last.then_inc(sem("ada_mm"), 1)
                                elif fl["kind"] == "turn":
                                    for i in range(3):
                                        last = pe.matmul(PS[:, 7, i * NTOK1:(i + 1) * NTOK1], RP[fl["third"]][:, i * P:(i + 1) * P],
                                                         CST[0:NTOK1, C_ID:C_ID + NTOK1], start=True, stop=True)
                                    last.then_inc(sem("ada_turned"), 1)
                                else:
                                    k_ = 0 if fl["kind"] == "q" else SLOT[fl["b"]]
                                    third_product(fl, k0, k1, 7, it * 16 + 16 * (wbase[k_] + 1 + fl["after"]))
                            elif what == "qk":
                                un = units[x]
                                if x == 0:
                                    pe.wait_ge(sem("q_ready"), it + (PAIRS if ph == "b" else 0) + 1)
                                if x >= 2:
                                    pe.wait_ge(sem(ph + "_sm"), it * pl["U"] + x - 1)
                                rows = slice(un["s"] * HDIM, (un["s"] + 1) * HDIM)
                                if un["b"] == "cmp":
                                    for qb in range(QB):
                                        keys = CKP[rows, :].rearrange("p (j g b) -> p j g b", j=8, g=2)[:, :, g, :]
                                        last = pe.matmul(PS[:, 2 * (x % 2), qb * NCB:(qb + 1) * NCB],
                                                         QT[rows, qb * P:(qb + 1) * P], keys, start=True, stop=True)
                                else:
                                    far = (un["b"] == "a" and un["qb"] >= 1) or (un["b"] == "win" and un["qb"] >= 4)
                                    for k0 in range(0, un["keys"], 512):
                                        n = min(512, un["keys"] - k0)
                                        key0 = un["first"] * P + k0
                                        last = pe.matmul(PS[:, 2 * (x % 2) + k0 // 512, 0:n],
                                                         QT[rows, un["qb"] * P:(un["qb"] + 1) * P],
                                                         KD[rows, KSRC[un["b"]], g, key0:key0 + n],
                                                         start=True, stop=not (far and k0 == 0))
                                        if far and k0 == 0:
                                            last = pe.matmul(PS[:, 2 * (x % 2), 0:P], IDB[:, :], FARB[:, :],
                                                             start=False, stop=True)
                                last.then_inc(sem(ph + "_qk"), 1)
                            elif what == "tr":
                                if x["n"] < 2:
                                    pe.wait_ge(sem(ph + "_mix"), it * pl["M"] + 1)
                                else:
                                    before = pl["order"][x["n"] - 2]
                                    if before["kind"] == "o":
                                        pe.wait_ge(sem(ph + "_mix"), it * pl["M"] + before["m"] + 2)
                                    elif before["c"] % 2:
                                        pe.wait_ge(sem(ph + "_evd"), it * (pl["C"] // 2) + before["c"] // 2 + 1)
                                    else:
                                        pe.wait_ge(sem(ph + "_eva"), it * ((pl["C"] + 1) // 2) + before["c"] // 2 + 1)
                                bank = 4 + x["n"] % 2
                                if x["kind"] == "o":
                                    job = 2 * pl["branches"].index(x["b"]) + 1
                                    pe.wait_ge(sem(ph + "_oe"), it * pl["J"] + job + 1)
                                    for i in range(4):
                                        last = pe.transpose(PS[:, bank, i * P:(i + 1) * P], OS[:, 4 * x["part"] + i, :], ident)
                                else:
                                    u = x["unit"]
                                    un = units[u]
                                    pe.wait_ge(sem(ph + "_ex"), it * pl["U"] + u + 1)
                                    if un["b"] == "cmp":
                                        for i in range(4):
                                            qb = 4 * x["part"] + i
                                            last = pe.transpose(PS[0:NCB, bank, i * P:(i + 1) * P],
                                                                PB[:, u % 3, qb * NCB:(qb + 1) * NCB], ident)
                                    else:
                                        at = 513 if ph == "a" else 0
                                        for i in range(min(4, un["keys"] // P - 4 * x["part"])):
                                            k0 = at + (4 * x["part"] + i) * P
                                            last = pe.transpose(PS[:, bank, i * P:(i + 1) * P], PB[:, u % 3, k0:k0 + P], ident)
                                last.then_inc(sem(ph + "_tr"), 1)
                            elif what == "pv":
                                u = x["unit"]
                                un = units[u]
                                c = x["c"]
                                if c % 2:
                                    pe.wait_ge(sem(ph + "_evd"), it * (pl["C"] // 2) + c // 2 + 1)
                                else:
                                    pe.wait_ge(sem(ph + "_eva"), it * ((pl["C"] + 1) // 2) + c // 2 + 1)
                                j = un["job"]
                                if j >= 1 and un["qb"] in (None, 0) and x["part"] == 0:
                                    pe.wait_ge(sem(ph + "_oe"), it * pl["J"] + j)
                                if un["b"] == "cmp":
                                    for i in range(4):
                                        qb = 4 * x["part"] + i
                                        last = pe.matmul(PS[:, 6, qb * HDIM:(qb + 1) * HDIM],
                                                         PT[0:NCB, c % 2, i * P:(i + 1) * P],
                                                         CV[0:NCB, 2, g * HDIM:(g + 1) * HDIM], start=True, stop=True)
                                else:
                                    blocks = un["keys"] // P
                                    for i in range(min(4, blocks - 4 * x["part"])):
                                        b = 4 * x["part"] + i
                                        last = pe.matmul(PS[:, 6, un["qb"] * HDIM:(un["qb"] + 1) * HDIM],
                                                         PT[:, c % 2, i * P:(i + 1) * P],
                                                         VT[:, KSRC[un["b"]], un["first"] + b, g * HDIM:(g + 1) * HDIM],
                                                         start=(b == 0), stop=(b == blocks - 1))
                                last.then_inc(sem(ph + "_pv"), 1)
                        if ph == "a":
                            pe.wait_ge(sem("fill_ev"), it * pl["FV"] + pl["FV"])

                for g, i0, i1 in ((0, 0, PAIRS // 2), (1, PAIRS // 2, PAIRS - 1)):
                    with pe.Fori(i0, i1) as it:
                        pair(g, it, False)
                pair(1, PAIRS - 1, True)

            pairs("a")

            def decode_scores(b, keys, new):
                for k0 in range(0, keys, 512):
                    n_ = min(512, keys - k0)
                    for n in range(DEC):
                        last = pe.matmul(PSf[:, k0:k0 + n_], QS[:, n * P:(n + 1) * P],
                                         (CKS[:, n, :] if b == "cmp" else Hf[:, n * keys + k0:n * keys + k0 + n_]),
                                         start=(n == 0), stop=(n == DEC - 1))
                if new is not None:
                    for n in range(DEC):
                        last = pe.matmul(PSf[:, keys:keys + 1], QS[:, n * P:(n + 1) * P], KN[:, new, n:n + 1],
                                         start=(n == 0), stop=(n == DEC - 1))
                last.then_inc(sem("d_qk"), 1)

            def decode_values(b, keys, values, new):
                pe.wait_ge(sem("d_p"), DN[b])
                for i in range(keys // P):
                    pe.transpose(PSf[:, 2048 + i * P:2048 + (i + 1) * P], PB[:, 2, i * P:(i + 1) * P], ident)
                pe.transpose(PS[0:DEC, 6, 0:P], SS[:, 0:DEC], ident).then_inc(sem("d_tr"), 1)
                pe.wait_ge(sem("d_pt"), DPT[b])
                pe.matmul(PS[:, 7, 0:P], VN[:, new, :], SS[0:DEC, 16:16 + P], start=True, stop=True)
                for n in range(DEC):
                    for i in range(keys // P):
                        last = pe.matmul(PS[:, 7, n * H:(n + 1) * H], values(n, i),
                                         PB[:, 0, i * P + n * H:i * P + (n + 1) * H],
                                         start=False, stop=True,
                                         skip_group_check=True)
                last.then_inc(sem("d_pv"), 1)

            plA, plB = plans["a"], plans["b"]
            pe.wait_ge(sem("a_dkv_in"), 32)
            pe.wait_ge(sem("a_mix"), PAIRS * plA["M"] + 1)
            pe.wait_ge(sem("a_oe"), PAIRS * plA["J"])
            decode_scores("a", WIN_A, 0)
            decode_values("a", WIN_A, lambda n, i: Hf[:, 1024 + n * P:1024 + (n + 1) * P], 0)

            pe.wait_ge(sem("d_out"), DN["a"])
            out_projection("b", slot, lambda c: (sem(f"w_full{c % 4}"), 16 * (W_AO[c % 4] + c // 4 + 1)))
            for k in range(8):
                pe.wait_ge(sem(f"w_full{k % 4}"), 16 * (W_KV[k % 4] + k // 4 + 1))
                if k:
                    pe.wait_ge(sem("lin_ev"), L_KV + k - 1)
                product(k % 2, slot(k % 4), HT, name=None if k else "kv")
            pe.wait_ge(sem("lin_ev"), L_KV + 8)
            turn_values(PB[:, 2, :], 0, "sel_vt")
            pe.wait_ge(sem("sel_vt_ev"), 2)
            turn_values(QT[:, :], 1, "win_vt")
            pe.wait_ge(sem("win_vt_ev"), 2)
            pe.wait_ge(sem("b_mod"), 1)
            pe.wait_ge(sem("b_mod_act"), 4)
            pe.wait_ge(sem("w_full3"), 16 * (W_GL + 1))
            product(0, slot(3), HT, 3 * H)
            pe.wait_ge(sem("lin_ev"), L_GL + 1)
            for i in range(QB):
                last = pe.transpose(PS[:, 6, i * 3 * H:(i + 1) * 3 * H], GL[0:3 * H, i * P:(i + 1) * P], CST[0:3 * H, C_ID:C_ID + 3 * H])
            pe.transpose(PS[0:DEC, 7, 0:3 * H], GL[0:3 * H, SEQ:TOK], CST[0:3 * H, C_ID:C_ID + 3 * H])\
              .then_inc(sem("gl_tr"), 1)
            pe.wait_ge(sem("gl_ev"), 2)
            pe.matmul(PS[:, 6, 0:3 * H], CST[0:DEC, C_EN:C_EN + P], SS[0:DEC, 0:3 * H], start=True, stop=True)\
              .then_inc(sem("gs_mm"), 1)
            pe.wait_ge(sem("w1_in"), 16)
            pe.wait_ge(sem("w2_in"), 16)
            for k in range(2):
                for b in range(16):
                    last = pe.matmul(PS[:, 3, k:k + 1], W1[:, k, b, :], VEC[:, V_POS + 16 * k + b:V_POS + 16 * k + b + 1],
                                     start=(b == 0), stop=(b == 15))
            last.then_inc(sem("pc_mm"), 1)
            for st in range(6):
                k, third_ = divmod(st, 3)
                for part in range(3):
                    loads_ = sum(8 if s % 3 < 2 else (6, 5, 5)[part] for s in range(st % 2, st + 1, 2))
                    pe.wait_ge(sem(f"cm_full{part}{st % 2}"), 16 * loads_)
                if third_ == 2:
                    pe.wait_ge(sem("cm_own"), k + 1)
                if st >= 2:
                    pe.wait_ge(sem("hid"), st - 1)
                for b in range(16):
                    last = pe.matmul(PS[:, st % 2, 0:CM_PAGES * 8], W1[:, k, b, :], CM[st % 2][:, b::16],
                                     start=(b == 0), stop=(b == 15))
                last.then_inc(sem("cm_mm"), 1)
                pe.wait_ge(sem("hid"), st + 1)
                if st:
                    pe.wait_ge(sem("ckv_ev"), min(st, 3))
                if k == 0:
                    for half in range(2):
                        last = pe.matmul(PS[half * HDIM:(half + 1) * HDIM, 2, 0:CM_PAGES * 8], W2[:, 0, :], HS[:, :],
                                         start=True, stop=True)
                else:
                    hs = HX.rearrange("p (n g c) -> p n g c", n=3, g=2)
                    for n in range(3):
                        for g in range(KVH):
                            q, at = (3 * third_ + n) % 4 * NCB, (3 * third_ + n) // 4 * P + g * HDIM
                            last = pe.matmul(PS[q:q + NCB, 2, at:at + HDIM], hs[:, n, g], W2[:, 1, :], start=True, stop=True)
                last.then_inc(sem("ckv_mm"), 1)
            pe.wait_ge(sem("ckv_ev"), 5)
            pe.wait_ge(sem("gs_ev"), 1)
            pe.wait_ge(sem("lin_ev"), L_B)
            pairs("b")
            pe.wait_ge(sem("b_mix"), PAIRS * plB["M"] + 1)
            pe.wait_ge(sem("b_oe"), PAIRS * plB["J"])
            decode_scores("cmp", NCB, None)
            pe.wait_ge(sem("d_p"), DN["cmp"])
            pe.matmul(PS[:, 1, 0:NCB], CST[:, C_GS:C_GS + P], PB[:, 1, 0:NCB], start=True, stop=True).then_inc(sem("imp_mm"), 1)
            pe.transpose(PS[:, 4, 0:P], PB[:, 2, 0:P], ident).then_inc(sem("d_tr"), 1)
            pe.wait_ge(sem("d_pt"), DPT["cmp"])
            for i in range(2):
                last = pe.matmul(PS[:, 7, i * 4 * H:(i + 1) * 4 * H], CV[:, i, :], PB[:, 0, i * 4 * H:(i + 1) * 4 * H],
                                 start=True, stop=True)
            last.then_inc(sem("d_pv"), 1)
            pe.wait_ge(sem("sel_k_in"), 16 * DEC * PAGES)
            pe.wait_ge(sem("imp_done"), 1)
            decode_scores("sel", PAST, 1)
            pe.wait_ge(sem("d_out"), DN["cmp"])
            pe.wait_ge(sem("sel_v_in"), 16 * DEC * PAGES)
            decode_values("sel", PAST, lambda n, i: WR[:, (n * PAGES + i) * P:(n * PAGES + i + 1) * P], 1)
            pe.wait_ge(sem("win_dkv_in"), 32)
            decode_scores("win", WIN_B, 2)
            pe.wait_ge(sem("d_out"), DN["sel"])
            decode_values("win", WIN_B, lambda n, i: Hf[:, 4096 + (n * 4 + i) * P:4096 + (n * 4 + i + 1) * P], 2)
            pe.wait_ge(sem("d_out"), DN["win"])
            out_projection("f", lambda i: slot(i, KDf), lambda c: (sem(f"wo_full{c % 4}"), 16 * (c // 4 + 1)))

        @block.scalar
        def _(act):
            act.wait_ge(sem("c_in"), 16)
            act.activation(CE[:, :, :], CT[:, :, :], ACT.Tanh, scale=0.5).then_inc(sem("tanh_c"), 1)

            def norm(name, ready):
                for c in range(NC):
                    ready(c)
                    act.activation(HT[:, c, :], XT[:, c, :], ACT.Square).then_inc(sem("sq"), 1)
                act.wait_ge(sem("ms"), NRM[name] + 1)
                act.activation(third(PB[:, 2, :]), PS[:, 5:8, 0:THIRD], ACT.Ln, bias=EPT[:, :]).then_inc(sem("ln_ms"), 1)
                act.wait_ge(sem("ln_ms"), NRM[name] + 1)
                act.activation(PB[:, 2, :], PB[:, 2, :], ACT.Exp, scale=-0.5).then_inc(sem("rstd"), 1)

            def modulate(name, src, part):
                act.wait_ge(sem(name + "_ag"), 1)
                for c in range(1 if name == "b" else 0, NC, 2 if name == "b" else 1):
                    if name != "b":
                        act.wait_ge(sem({"a": "a_y", "kv": "b_y"}[name]), c + 1)
                    act.activation(HT[:, c, 0:SEQ], src[:, c, 0:SEQ], ACT.Identity, scale=AG[:, part, c, 0:1],
                                   bias=ADA[:, ADA0[name] + c, 0:1]).then_inc(sem(name + "_mod_act"), 1)

            act.wait_ge(sem("ones"), 2)

            def first(c):
                if c == 0:
                    act.wait_ge(sem("x_in0"), 64)
                    act.wait_ge(sem("x_in1"), 64)

            norm("a", first)
            modulate("a", HT, 0)
            act.wait_ge(sem("a_vt"), 1)
            act.activation(VT[:, 0, :, :].rearrange("p b n -> p (b n)"), PSf[:, 2048:3072], ACT.Copy).then_inc(sem("a_vt_ev"), 1)

            def pairs(ph):
                pl, C = plans[ph], CHUNKS[ph]
                units, first = pl["units"], pl["first"]

                def third_out(fl, bank):
                    cols = slice(fl["third"] * THIRD, (fl["third"] + 1) * THIRD)
                    if fl["kind"] == "q":
                        act.activation(QN[ph][:, cols], PS[:, bank, 0:THIRD], ACT.Copy).then_inc(sem("q_ev"), 1)
                    else:
                        act.activation(SZ[fl["b"]][:, cols], PS[:, bank, 0:THIRD], ACT.Tanh, scale=0.5).then_inc(sem("fill_tanh"), 1)

                if ph == "b":
                    act.wait_ge(sem("kv_stored"), 64)
                for fl in first:
                    act.wait_ge(sem("fill_mm"), FM0[ph] + fl["mm"] + 1)
                    third_out(fl, fl["f"] % 8)
                    if fl["kind"] == "q" and fl["third"] == 2:
                        act.wait_ge(sem("q_ev"), (FQ if ph == "b" else 0) + 3)
                        act.activation(QT[:, :], QN[ph], ACT.Copy).then_inc(sem("q_ready"), 1)

                def pair(it, last_):
                    for what, x in pl["last_plan" if last_ else "plan"]:
                        if what == "ft" and x["kind"] in ("q", "gate"):
                            act.wait_ge(sem("fill_mm"), it * pl["FM"] + FM0[ph] + len(first) + x["mm"] + 1)
                            if x["kind"] == "gate" and x["third"] == 0:
                                m = {"a": 0, "win": 0, "cmp": 2, "sel": 4}[x["b"]]
                                act.wait_ge(sem(ph + "_mix"), it * pl["M"] + m + 1)
                            third_out(x, 7)
                        elif what == "qc":
                            act.wait_ge(sem(ph + "_qk"), it * pl["U"] + pl["U"])
                            act.wait_ge(sem("qs_set"), it * 2 + (2 * PAIRS if ph == "b" else 0) + 2)
                            act.wait_ge(sem("q_ev"), it * 3 + (FQ if ph == "b" else 0) + 6)
                            act.activation(QT[:, :], QN[ph], ACT.Copy).then_inc(sem("q_ready"), 1)
                        elif what == "ex":
                            un = units[x]
                            act.wait_ge(sem(ph + "_sm"), it * pl["U"] + x + 1)
                            if un["b"] == "cmp":
                                act.activation(PB[:, x % 3, 0:un["keys"]], PB[:, x % 3, 0:un["keys"]], ACT.Exp)\
                                   .then_inc(sem(ph + "_ex"), 1)
                            elif ph == "a":
                                act.activation(PB[:, x % 3, 512:513 + un["keys"]], PB[:, x % 3, 0:1 + un["keys"]], ACT.Exp,
                                               scale=-1.0, bias=NM[:, x % 3, 0:1],
                                               accum_out=DEN[:, un["job"], un["qb"]:un["qb"] + 1]).then_inc(sem(ph + "_ex"), 1)
                            else:
                                act.activation(PB[:, x % 3, 0:un["keys"]], PB[:, x % 3, 0:un["keys"]], ACT.Exp,
                                               scale=-1.0, bias=NM[:, x % 3, 0:1],
                                               accum_out=DEN[:, un["job"], un["qb"]:un["qb"] + 1]).then_inc(sem(ph + "_ex"), 1)
                        elif what == "ev" and x["c"] % 2 == 0:
                            c, un = x["c"], units[x["unit"]]
                            act.wait_ge(sem(ph + "_tr"), it * pl["N"] + x["n"] + 1)
                            if c > 1:
                                act.wait_ge(sem(ph + "_pv"), it * pl["C"] + c - 1)
                            m = NCB if un["b"] == "cmp" else P
                            n = 512 if un["b"] == "cmp" else min(512, un["keys"] - 512 * x["part"])
                            act.activation(PT[0:m, c % 2, 0:n], PS[0:m, 4 + x["n"] % 2, 0:n], ACT.Copy).then_inc(sem(ph + "_eva"), 1)
                    act.wait_ge(sem(ph + "_pv"), it * pl["C"] + pl["C"])

                with act.Fori(0, PAIRS - 1) as it:
                    pair(it, False)
                pair(PAIRS - 1, True)

            pairs("a")

            def decode(b, keys, extra):
                act.wait_ge(sem("d_sm"), DN[b])
                act.activation(PB[:, 1, 0:keys + extra], PB[:, 0, 0:keys + extra], ACT.Exp, scale=-1.0,
                               bias=SS[:, 200:201], accum_out=SS[:, 201:202]).then_inc(sem("d_ex"), 1)
                act.wait_ge(sem("d_tr"), DN[b])
                if b == "cmp":
                    act.activation(PB[:, 0, 0:P], PS[:, 4, 0:P], ACT.Copy).then_inc(sem("d_pt"), 1)
                else:
                    act.activation(PB[:, 0, 0:keys], PSf[:, 2048:2048 + keys], ACT.Copy).then_inc(sem("d_pt"), 1)

            decode("a", WIN_A, 2)
            norm("b", lambda c: act.wait_ge(sem("op_ev"), 3 * c + 3))
            modulate("kv", MT, 1)
            act.wait_ge(sem("sel_vt"), 1)
            act.activation(VT[:, 0, :, :].rearrange("p b n -> p (b n)"), PSf[:, 2048:3072], ACT.Copy).then_inc(sem("sel_vt_ev"), 1)
            act.wait_ge(sem("win_vt"), 1)
            act.activation(VT[:, 1, :, :].rearrange("p b n -> p (b n)"), PSf[:, 2048:3072], ACT.Copy).then_inc(sem("win_vt_ev"), 1)
            act.wait_ge(sem("lin_mm"), L_KV + 8)
            modulate("b", MT, 2)
            act.wait_ge(sem("lin_mm"), L_GL + 1)
            act.activation(third(GL[0:3 * H, :]), PS[0:3 * H, 0:3, 0:THIRD], ACT.Tanh, scale=0.5).then_inc(sem("gl_tanh"), 1)
            for st in range(2):
                compression_pages(act, 2, st)
            act.wait_ge(sem("pc_ev"), 2)
            for st in range(6):
                act.wait_ge(sem("cm_mm"), st + 1)
                if st:
                    act.wait_ge(sem("hid"), st)
                    act.wait_ge(sem("ckv_mm"), st)
                act.activation(HX[:, :], PS[:, st % 2, 0:CM_PAGES * 8], ACT.Tanh, scale=0.5, bias=PCH[:, st // 3:st // 3 + 1])\
                   .then_inc(sem("hid_tanh"), 1)
                if st < 4:
                    compression_pages(act, 2, st + 2)
            pairs("b")
            decode("cmp", NCB, 0)
            decode("sel", PAST, 1)
            decode("win", WIN_B, 1)
            norm("f", lambda c: act.wait_ge(sem("op_ev"), 3 * (NC + c) + 3))

        @block.vector
        def _(dve):
            chain = [0]

            def step(ins):
                chain[0] += 1
                ins.then_inc(sem("dve_step"), 1)
                dve.wait_ge(sem("dve_step"), chain[0])

            dve.memset(ONE[:, 0:1], 1.0)
            dve.memset(ONE[:, 1:2], 1.0 / DM).then_inc(sem("ones"), 1)
            dve.memset(EPT[:, :], EPS).then_inc(sem("ones"), 1)
            dve.memset(QS[:, :], 0.0).then_inc(sem("qs_zero"), 1)
            dve.wait_ge(sem("tanh_c"), 1)
            step(dve.scalar_tensor_tensor(CE[:, :, :].rearrange("p a b -> p (a b)"), CE[:, :, :].rearrange("p a b -> p (a b)"), 1.0,
                                          CT[:, :, :].rearrange("p a b -> p (a b)"), ALU.add, ALU.mult))
            dve.tensor_scalar(CE[:, :, :], CE[:, :, :], 0.5, None, ALU.mult).then_inc(sem("silu_c"), 1)
            dve.wait_ge(sem("row_mm"), 1)
            row = PB[:, 0:2, :].rearrange("p a n -> p (a n)")[:, 0:NBIAS]
            dve.scalar_tensor_tensor(row.rearrange("p (a n) -> p a n", a=3), PS[:, 5:8, 0:384], 1.0 / SCALE,
                                     Mf[:, 2048:2048 + NBIAS].rearrange("p (a n) -> p a n", a=3), ALU.mult, ALU.add)\
               .then_inc(sem("bias_row"), 1)
            dve.wait_ge(sem("bias_row"), 1)
            dve.wait_ge(sem("const_in"), 16)
            dve.wait_ge(sem("vec_in"), 16)
            dve.tensor_copy(IDB[:, :], ident)
            dve.tensor_copy(FARB[:, :], CST[:, C_FAR:C_FAR + P])
            dve.tensor_scalar(NSK[:, :], VEC[:, V_SINK:V_SINK + H + 1], -1.0, None, ALU.mult).then_inc(sem("row_ev"), 1)
            dve.wait_ge(sem("row_ev"), 1)
            for i in range(NADA0 // 4):
                dve.wait_ge(sem("ada_group"), i + 1)
                dve.tensor_copy(RA[:, i * 512:(i + 1) * 512], PS[0:NTOK1, i, :]).then_inc(sem("ada_rows"), 1)
            dve.wait_ge(sem("ada_turned"), 1)
            dve.tensor_tensor(ADA[:, 0:NADA0, :], PS[:, 4, 0:NADA0 * NTOK1].rearrange("p (a n) -> p a n", a=NADA0),
                              VEC[:, V_BIAS:V_BIAS + NADA0].unsqueeze(2).to_broadcast([P, NADA0, NTOK1]), ALU.add)\
               .then_inc(sem("ada_ev"), 1)
            dve.wait_ge(sem("ada_ev"), 1)

            def gains(name, part, g0):
                a0 = ADA0[name]
                dve.scalar_tensor_tensor(AG[:, part, :, :], ADA[:, a0 + NC:a0 + 2 * NC, :], 1.0,
                                         VEC[:, g0:g0 + NC].unsqueeze(2).to_broadcast([P, NC, NTOK1]), ALU.add, ALU.mult)\
                   .then_inc(sem(name + "_ag"), 1)
                dve.wait_ge(sem(name + "_ag"), 1)

            gains("a", 0, V_GA)

            def norm(name, dst):
                dve.wait_ge(sem("rstd"), NRM[name] + 1)
                for c in range(NC):
                    if dst is None:
                        dve.scalar_tensor_tensor(HT[:, c, :], XT[:, c, :], VEC[:, V_GF + c:V_GF + c + 1], PB[:, 2, :],
                                                 ALU.mult, ALU.mult).then_inc(sem("y_out"), 1)
                    else:
                        dve.tensor_tensor(dst[:, c, :], XT[:, c, :], PB[:, 2, :], ALU.mult).then_inc(sem(name + "_y"), 1)

            def modulate(name, src, part):
                a0 = ADA0[name]
                for c in range(0, NC if name == "b" else 0, 2):
                    dve.tensor_scalar(HT[:, c, 0:SEQ], src[:, c, 0:SEQ], AG[:, part, c, 0:1], ADA[:, a0 + c, 0:1],
                                      ALU.mult, ALU.add)
                step(dve.tensor_tensor(HT[:, :, SEQ:TOK], src[:, :, SEQ:TOK], AG[:, part, :, 1:NTOK1], ALU.mult))
                dve.tensor_tensor(HT[:, :, SEQ:TOK], HT[:, :, SEQ:TOK], ADA[:, a0:a0 + NC, 1:NTOK1], ALU.add)\
                   .then_inc(sem(name + "_mod"), 1)

            norm("a", HT)
            dve.wait_ge(sem("a_y"), NC)
            modulate("a", HT, 0)
            dve.wait_ge(sem("scratch"), 16 * COPIES // DEC)
            for k, dst in enumerate((KD[:, 0, 0, :], KD[:, 0, 1, :], PB[:, 0, :])):
                dve.wait_ge(sem("lin_mm"), L_A0 + k + 1)
                dve.tensor_copy(third(dst), lin_set(k)).then_inc(sem("lin_ev"), 1)
            dve.wait_ge(sem("lin_ev"), L_A)

            def new_keys(j, kd):
                for g in range(KVH):
                    rows = slice(g * HDIM, (g + 1) * HDIM)
                    dve.tensor_copy(KN[rows, j, :], KD[rows, kd, g, SEQ:TOK]).then_inc(sem("new_keys"), 1)

            new_keys(0, 0)
            dve.wait_ge(sem("a_vt"), 1)
            dve.tensor_copy(VN[:, 0, :], PS[0:DEC, 6, 0:P]).then_inc(sem("a_vt_ev"), 1)
            dve.wait_ge(sem("a_v_stored"), 16)
            dve.wait_ge(sem("qs_zero"), 1)

            def pairs(ph):
                pl, C = plans[ph], CHUNKS[ph]
                base = {"a": L_A, "b": L_B}[ph]
                units, jobs = pl["units"], pl["jobs"]
                RC = sum(1 if b == "a" else 3 if b == "cmp" else 2 for b, _ in jobs)
                CC = 4 * sum(1 for un in units if un["b"] == "cmp")
                first = pl["first"]

                def third_out(fl, bank, i):
                    cols = slice(fl["third"] * THIRD, (fl["third"] + 1) * THIRD)
                    tile = SZ[fl["b"]]
                    dve.scalar_tensor_tensor(tile[:, cols], tile[:, cols], 1.0, PS[:, bank, 0:THIRD], ALU.add, ALU.mult)\
                       .then_inc(sem("fill_ev"), 1)

                def decode_gate(b, i):
                    dve.tensor_copy(SZS[:, BR[b], bass.ds(i, 1), :].rearrange("p o n -> p (o n)"), SZ[b][:, SEQ:TOK])\
                       .then_inc(sem("szs_set"), 1)

                dve.memset(NM[:, 0, 1:2], 0.0).then_inc(sem(ph + "_mix"), 1)
                for fl in first:
                    if fl["kind"] == "gate":
                        dve.wait_ge(sem("fill_tanh"), FT0[ph] + fl["tanh"] + 1)
                        third_out(fl, fl["f"] % 8, 0)
                        if fl["third"] == 2:
                            dve.wait_ge(sem("fill_ev"), FV0[ph] + fl["ev"] + 1)
                            decode_gate(fl["b"], 0)

                def pair(g, it, last_):
                        dve.wait_ge(sem("q_ready"), it + (PAIRS if ph == "b" else 0) + 1)
                        for s in range(2):
                            dve.tensor_copy(QS[g * HDIM:(g + 1) * HDIM, :].rearrange("p (n x) -> p n x", x=144)
                                            [:, :, bass.ds(it * 2 + s, 1)].rearrange("p n o -> p (n o)"),
                                            QT[s * HDIM:(s + 1) * HDIM, SEQ:TOK]).then_inc(sem("qs_set"), 1)
                        if ph == "a":
                            for s in range(3):
                                dve.tensor_copy(PB[:, s, 0:1], NSK[:, bass.ds(it * 2, 1)]).then_inc(sem("sink_set"), 1)
                        for what, x in pl["last_plan" if last_ else "plan"]:
                            if what == "fe" and x["kind"] == "ada":
                                dve.wait_ge(sem("ada_mm"), it * 2 + x["third"] + 1)
                                dve.tensor_copy(RP[x["third"]], PS[0:NTOK1, 7, 0:3 * P]).then_inc(sem("fill_ev"), 1)
                            elif what == "fe" and x["kind"] == "turn":
                                dve.wait_ge(sem("ada_turned"), it * 2 + x["third"] + 2)
                                c0 = it * NPA + NADA0 + 3 * x["third"]
                                dve.tensor_tensor(ADA[:, bass.ds(c0, 3), :], PS[:, 7, 0:3 * NTOK1].rearrange("p (a n) -> p a n", a=3),
                                                  VEC[:, bass.ds(c0 + V_BIAS, 3)].unsqueeze(2).to_broadcast([P, 3, NTOK1]), ALU.add)\
                                   .then_inc(sem("fill_ev"), 1)
                            elif what == "fe" and x["kind"] == "gate":
                                dve.wait_ge(sem("fill_tanh"), it * pl["FT"] + FT0[ph] + sum(1 for fl in first if fl["kind"] == "gate") + x["tanh"] + 1)
                                third_out(x, 7, it)
                                if x["third"] == 2:
                                    dve.wait_ge(sem("fill_ev"), it * pl["FV"] + FV1[ph] + x["ev"] + 1)
                                    decode_gate(x["b"], it + x["after"])
                            elif what == "sm":
                                un = units[x]
                                L = un["keys"]
                                if un["b"] in ("a", "sel") and un["qb"] == 0:
                                    dve.wait_ge(sem(f"strip{un['s']}"), it * 64 + (64 * PAIRS if ph == "b" else 0) + 64)
                                if ph == "a" and x < 3:
                                    dve.wait_ge(sem("sink_set"), it * 6 + 3)
                                if x >= 3:
                                    dve.wait_ge(sem(ph + "_tr"), it * pl["N"] + units[x - 3]["trs"])
                                if ph == "a" and QB <= x < QB + 3:
                                    dve.tensor_scalar(PB[:, x % 3, 0:1], NSK[:, bass.ds(it * 2 + 1, 1)], 1.0, None, ALU.mult).then_inc(sem("sink_set"), 1)
                                    dve.wait_ge(sem("sink_set"), it * 6 + 3 + x - QB + 1)
                                if un["b"] == "cmp":
                                    cc = 3 * x
                                    dve.wait_ge(sem(ph + "_qk"), it * pl["U"] + x + 1)
                                    xx = PB[:, x % 3, 0:L]
                                    x3 = xx.rearrange("p (q c) -> p q c", q=QB)
                                    dve.scalar_tensor_tensor(xx, PS[:, 2 * (x % 2), 0:L], -SCALE, CST[:, C_CM:C_CM + L],
                                                             ALU.mult, ALU.add).then_inc(sem("cmp_step"), 1)
                                    dve.wait_ge(sem("cmp_step"), it * CC + cc + 1)
                                    dve.tensor_reduce(NM[:, x % 3, :], x3, AX, ALU.min).then_inc(sem("cmp_step"), 1)
                                    dve.wait_ge(sem("cmp_step"), it * CC + cc + 2)
                                    dve.tensor_scalar(NM[:, x % 3, :], NM[:, x % 3, :], BIG / 10, None, ALU.min).then_inc(sem("cmp_step"), 1)
                                    dve.wait_ge(sem("cmp_step"), it * CC + cc + 3)
                                    dve.scalar_tensor_tensor(x3, x3, -1.0, NM[:, x % 3, :].unsqueeze(2).to_broadcast([P, QB, NCB]),
                                                             ALU.mult, ALU.add).then_inc(sem(ph + "_sm"), 1)
                                else:
                                    at = 1 if ph == "a" else 0
                                    dve.wait_ge(sem(ph + "_qk"), it * pl["U"] + x + 1)
                                    dve.memset(NM[:, x % 3, 1:2], 0.0)
                                    dve.tensor_tensor_reduce(PB[:, x % 3, at:at + L], PSf[:, 1024 * (x % 2):1024 * (x % 2) + L],
                                                             STR[:, un["s"], SEQ - L:SEQ], -SCALE,
                                                             (PB[:, x % 3, 0:1] if ph == "a" else 3 * BIG), ALU.add, ALU.min,
                                                             NM[:, x % 3, 0:1]).then_inc(sem(ph + "_sm"), 1)
                            elif what == "ev" and x["c"] % 2:
                                c, un = x["c"], units[x["unit"]]
                                if un["b"] == "cmp" and x["part"] == 1:
                                    dve.wait_ge(sem(ph + "_ex"), it * pl["U"] + x["unit"] + 1)
                                    dve.tensor_reduce(DEN[:, un["job"], :], PB[:, x["unit"] % 3, 0:un["keys"]]
                                                      .rearrange("p (q c) -> p q c", q=QB), AX, ALU.add).then_inc(sem("cmp_step"), 1)
                                dve.wait_ge(sem(ph + "_tr"), it * pl["N"] + x["n"] + 1)
                                if c > 1:
                                    dve.wait_ge(sem(ph + "_pv"), it * pl["C"] + c - 1)
                                m = NCB if un["b"] == "cmp" else P
                                n = 512 if un["b"] == "cmp" else min(512, un["keys"] - 512 * x["part"])
                                dve.tensor_copy(PT[0:m, c % 2, 0:n], PS[0:m, 4 + x["n"] % 2, 0:n]).then_inc(sem(ph + "_evd"), 1)
                            elif what == "oe":
                                b, s = jobs[x]
                                rc0 = sum(1 if jobs[i][0] == "a" else 3 if jobs[i][0] == "cmp" else 2 for i in range(x))
                                lastg = [g_ for un in units if un["job"] == x for g_ in un["groups"]][-1]
                                if b == "cmp":
                                    dve.wait_ge(sem("cmp_step"), it * CC + 6 + x + 1)
                                    dve.tensor_scalar(DEN[:, x, :], DEN[:, x, :], 1.0 / BIG, None, ALU.max).then_inc(sem(ph + "_rc"), 1)
                                    rc0 += 1
                                    dve.wait_ge(sem(ph + "_rc"), it * RC + rc0)
                                if x:
                                    dve.wait_ge(sem(ph + "_oe"), it * pl["J"] + x)
                                dve.reciprocal(RG[:, :], DEN[:, x, :]).then_inc(sem(ph + "_rc"), 1)
                                rc0 += 1
                                dve.wait_ge(sem(ph + "_rc"), it * RC + rc0)
                                if ph == "b":
                                    dve.tensor_tensor(RG[:, :], RG[:, :],
                                                      SG[:, :, bass.ds(it * 2 + BR[b] * H + s, 1)].rearrange("p q o -> p (q o)"),
                                                      ALU.mult).then_inc(sem(ph + "_rc"), 1)
                                    rc0 += 1
                                    dve.wait_ge(sem(ph + "_rc"), it * RC + rc0)
                                dve.wait_ge(sem(ph + "_pv"), it * pl["C"] + lastg["c"] + 1)
                                if x >= 2 and s == 0:
                                    og = [o for o in pl["order"] if o["kind"] == "o" and o["b"] == jobs[x - 1][0]][-1]
                                    dve.wait_ge(sem(ph + "_tr"), it * pl["N"] + og["n"] + 1)
                                dve.tensor_tensor(OS[:, :, s * HDIM:(s + 1) * HDIM],
                                                  PS[:, 6, :].rearrange("p (q d) -> p q d", q=QB),
                                                  RG[:, :].unsqueeze(2).to_broadcast([P, QB, HDIM]), ALU.mult).then_inc(sem(ph + "_oe"), 1)
                            elif what == "mix":
                                half = slice(512 * x["part"], 512 * x["part"] + 512)
                                dve.wait_ge(sem(ph + "_tr"), it * pl["N"] + x["n"] + 1)
                                out = MT[:, bass.ds(it, 1), half].rearrange("p o n -> p (o n)")
                                if x["b"] == pl["branches"][0]:
                                    dve.scalar_tensor_tensor(out, PS[:, 4 + x["n"] % 2, :], 0.5, SZ[x["b"]][:, half],
                                                             ALU.mult, ALU.mult).then_inc(sem(ph + "_mix"), 1)
                                else:
                                    ms = x["m"] - 1
                                    dve.scalar_tensor_tensor(SS[:, :], PS[:, 4 + x["n"] % 2, :], 0.5, SZ[x["b"]][:, half],
                                                             ALU.mult, ALU.mult).then_inc(sem("mix_step"), 1)
                                    dve.wait_ge(sem("mix_step"), it * (pl["M"] - 2) + ms)
                                    dve.wait_ge(sem(ph + "_mix"), it * pl["M"] + x["m"])
                                    dve.tensor_tensor(out, out, SS[:, :], ALU.add).then_inc(sem(ph + "_mix"), 1)
                                    dve.wait_ge(sem(ph + "_mix"), it * pl["M"] + x["m"] + 2)
                        dve.wait_ge(sem(ph + "_oe"), it * pl["J"] + pl["J"])
                        dve.wait_ge(sem(ph + "_tr"), it * pl["N"] + pl["N"])

                for g, i0, i1 in ((0, 0, PAIRS // 2), (1, PAIRS // 2, PAIRS - 1)):
                    with dve.Fori(i0, i1) as it:
                        pair(g, it, False)
                pair(1, PAIRS - 1, True)

            pairs("a")
            dve.wait_ge(sem("szs_set"), 8)
            dve.wait_ge(sem("sink_set"), 48)

            def decode(b, keys, extra, new):
                dve.wait_ge(sem("d_qk"), DN[b])
                nm, den, r = SS[:, 200:201], SS[:, 201:202], SS[:, 202:203]
                if b == "cmp":
                    step(dve.tensor_scalar(PB[:, 0, 0:keys], PSf[:, 0:keys], -SCALE, None, ALU.mult))
                    dve.tensor_reduce(nm, PB[:, 0, 0:keys], AX, ALU.min).then_inc(sem("d_sm"), 1)
                else:
                    if b == "a":
                        dve.tensor_copy(PB[:, 0, keys + 1:keys + 2], NSK[:, H:H + 1])
                    dve.tensor_tensor_reduce(PB[:, 0, 0:keys + 1], PSf[:, 0:keys + 1],
                                             STR[:, :, :].rearrange("p a n -> p (a n)")[:, PAST - keys:PAST + 1], -SCALE,
                                             (NSK[:, H:H + 1] if b == "a" else 3 * BIG), ALU.add, ALU.min, nm)\
                       .then_inc(sem("d_sm"), 1)
                dve.wait_ge(sem("d_ex"), DN[b])
                step(dve.reciprocal(r, den))
                if b == "cmp":
                    step(dve.tensor_scalar(PB[:, 1, 0:keys], PB[:, 1, 0:keys], r, None, ALU.mult))
                    dve.scalar_tensor_tensor(PB[:, 2, 0:P].rearrange("p (r c) -> p r c", r=4),
                                             PB[:, 1, 0:keys].unsqueeze(1).to_broadcast([P, 4, keys]), SGS[:, 0:1],
                                             CST[:, C_M4:C_M4 + 4].unsqueeze(2).to_broadcast([P, 4, keys]), ALU.mult, ALU.mult)\
                       .then_inc(sem("d_p"), 1)
                    return
                gate = ONE[:, 0:1] if b == "a" else SGS[:, BR[b]:BR[b] + 1]
                step(dve.tensor_scalar(PB[:, 2, 0:keys + 1], PB[:, 1, 0:keys + 1], r, gate, ALU.mult, ALU.mult))
                dve.tensor_scalar(SS[:, 0:DEC], CST[:, C_DN:C_DN + DEC], PB[:, 2, keys:keys + 1], None, ALU.mult)\
                   .then_inc(sem("d_p"), 1)
                dve.wait_ge(sem("d_tr"), DN[b])
                dve.tensor_copy(SS[0:DEC, 16:16 + P], PS[0:DEC, 6, 0:P]).then_inc(sem("d_pt"), 1)

            def decode_out(b, first_):
                dve.wait_ge(sem("d_pv"), DN[b])
                os_ = SS[:, 256:320].rearrange("p (c n) -> p c n", c=NC)
                for g in range(KVH):
                    for s in range(2):
                        src = PS[g * HDIM:(g + 1) * HDIM, 7, 0:P].rearrange("p (n g c s) -> p g s c n", n=DEC, g=2, s=2)[:, g, s]
                        ins = dve.tensor_copy(os_[s * HDIM:(s + 1) * HDIM, 4 * g:4 * g + 4, :], src)
                step(ins)
                out = MT[:, :, SEQ:TOK]
                if first_:
                    dve.scalar_tensor_tensor(out, os_, 0.5, SZS[:, BR[b], :, :], ALU.mult, ALU.mult).then_inc(sem("d_out"), 1)
                else:
                    o2 = SS[:, 320:384].rearrange("p (c n) -> p c n", c=NC)
                    step(dve.scalar_tensor_tensor(o2, os_, 0.5, SZS[:, BR[b], :, :], ALU.mult, ALU.mult))
                    dve.tensor_tensor(out, out, o2, ALU.add).then_inc(sem("d_out"), 1)
                dve.wait_ge(sem("d_out"), DN[b])

            dve.wait_ge(sem("a_rows_in"), 16)
            dve.wait_ge(sem("new_keys"), 2)
            decode("a", WIN_A, 2, 0)
            decode_out("a", True)

            def residual(n0, a0):
                for c in range(NC):
                    gate, x = ADA[:, a0 + c, :], XT[:, c, :]
                    for a in range(3):
                        dve.wait_ge(sem("op_mm"), 3 * (n0 + c) + a + 1)
                        n = THIRD if a < 2 else THIRD - DEC
                        if a == 2:
                            dve.tensor_tensor(SS[:, 384:392], PS[:, a, n:THIRD], gate[:, 1:NTOK1], ALU.mult).then_inc(sem("res_step"), 1)
                        ins = dve.scalar_tensor_tensor(x[:, a * THIRD:a * THIRD + n], PS[:, a, 0:n], gate[:, 0:1],
                                                       x[:, a * THIRD:a * THIRD + n], ALU.mult, ALU.add)
                        if a < 2:
                            ins.then_inc(sem("op_ev"), 1)
                    dve.wait_ge(sem("res_step"), n0 + c + 1)
                    dve.tensor_tensor(x[:, SEQ:TOK], x[:, SEQ:TOK], SS[:, 384:392], ALU.add).then_inc(sem("op_ev"), 1)
                    dve.wait_ge(sem("op_ev"), 3 * (n0 + c) + 3)

            residual(0, 16)
            gains("kv", 1, V_GKV)
            gains("b", 2, V_GB)
            norm("b", MT)
            dve.wait_ge(sem("b_y"), NC)
            modulate("kv", MT, 1)
            kv_dst = (PB[:, 0, :], PB[:, 1, :], KD[:, 0, 0, :], KD[:, 0, 1, :], PB[:, 2, :], KD[:, 1, 0, :], KD[:, 1, 1, :], QT[:, :])
            for k, dst in enumerate(kv_dst):
                dve.wait_ge(sem("lin_mm"), L_KV + k + 1)
                dve.tensor_copy(third(dst), lin_set(k)).then_inc(sem("lin_ev"), 1)
            dve.wait_ge(sem("lin_ev"), L_KV + 8)
            new_keys(1, 0)
            new_keys(2, 1)
            for j, tag in ((1, "sel_vt"), (2, "win_vt")):
                dve.wait_ge(sem(tag), 1)
                dve.tensor_copy(VN[:, j, :], PS[0:DEC, 6, 0:P]).then_inc(sem(tag + "_ev"), 1)
            modulate("b", MT, 2)
            dve.wait_ge(sem("gl_tanh"), 1)
            dve.tensor_scalar(GL[0:3 * H, :], GL[0:3 * H, :], 1.0, 0.5, ALU.add, ALU.mult).then_inc(sem("lin_ev"), 1)
            dve.wait_ge(sem("gl_tr"), 1)
            dve.tensor_copy(SG[:, :, :].rearrange("p q c -> p (q c)"), PS[:, 6, 0:QB * 3 * H]).then_inc(sem("gl_ev"), 1)
            dve.tensor_copy(SS[0:DEC, 0:3 * H], PS[0:DEC, 7, 0:3 * H]).then_inc(sem("gl_ev"), 1)
            dve.wait_ge(sem("gs_mm"), 1)
            own = SS[:, 64:112].rearrange("p (b h) -> p b h", b=3)
            step(dve.tensor_tensor(own, PS[:, 6, 0:3 * H].rearrange("p (b h) -> p b h", b=3),
                                   CST[:, C_DH:C_DH + H].unsqueeze(1).to_broadcast([P, 3, H]), ALU.mult))
            dve.tensor_reduce(SGS[:, :], own, AX, ALU.add).then_inc(sem("gs_ev"), 1)
            dve.wait_ge(sem("gs_ev"), 1)
            dve.wait_ge(sem("pc_mm"), 1)
            dve.tensor_copy(PC[:, :], PS[:, 3, 0:2]).then_inc(sem("pc_ev"), 1)
            dve.tensor_scalar(PCH[:, :], PS[:, 3, 0:2], 0.5, None, ALU.mult).then_inc(sem("pc_ev"), 1)
            dve.wait_ge(sem("pc_ev"), 2)
            for st in range(6):
                k, third_ = divmod(st, 3)
                if third_ == 2:
                    if st >= 2:
                        dve.wait_ge(sem("cm_mm"), st - 1)
                    pages = CM[st % 2][:, 16 * P:24 * P].rearrange("p (j g x) -> p j g x", j=8, g=2)
                    for g in range(KVH):
                        for par in range(2):
                            src = PB[g * HDIM:(g + 1) * HDIM, k, 0:SEQ].rearrange("p (j x r) -> p r j x", j=8, r=2)[:, par]
                            ins = dve.tensor_copy(pages[par * HDIM:(par + 1) * HDIM, :, g, :], src)
                    ins.then_inc(sem("cm_own"), 1)
                dve.wait_ge(sem("hid_tanh"), st + 1)
                if st:
                    dve.wait_ge(sem("ckv_mm"), st)
                n = CM_PAGES * 8
                step(dve.tensor_scalar(HS[:, :], PS[:, st % 2, 0:n], PC[:, k:k + 1], None, ALU.add))
                last = dve.scalar_tensor_tensor(HS[:, :], HX[:, :], 1.0, HS[:, :], ALU.add, ALU.mult)
                if k == 1:
                    step(last)
                    for n_ in range(3):
                        last = dve.tensor_copy(HX.rearrange("p (n g j b) -> p n g j b", n=3, g=2, j=8)[:, n_],
                                               HS.rearrange("p (n j g b) -> p n g j b", n=3, j=8, g=2)[:, n_])
                last.then_inc(sem("hid"), 1)
                dve.wait_ge(sem("ckv_mm"), st + 1)
                if k == 0:
                    dve.tensor_scalar(CK[:, third_ * n:(third_ + 1) * n], PS[:, 2, 0:n], 0.5, None, ALU.mult).then_inc(sem("ckv_ev"), 1)
                elif third_ == 2:
                    dve.tensor_scalar(CV[:, 0:2, :].rearrange("p n c -> p (n c)"), PS[:, 2, 0:2 * P], 0.5, None, ALU.mult)\
                       .then_inc(sem("ckv_ev"), 1)
                    dve.tensor_scalar(CV[0:NCB, 2, :], PS[0:NCB, 2, 2 * P:3 * P], 0.5, None, ALU.mult).then_inc(sem("ckv_ev"), 1)
            dve.wait_ge(sem("ckv_ev"), 5)
            dve.tensor_copy(CKP[:, :], CK[:, 512:576]).then_inc(sem("cks"), 1)
            for g in range(KVH):
                rows = slice(g * HDIM, (g + 1) * HDIM)
                dve.tensor_copy(CKS[rows, :, :].rearrange("p n (j b) -> p (n j) b", b=4),
                                CK[rows, 0:512].rearrange("p (m g b) -> p m g b", g=2, b=4)[:, :, g, :]).then_inc(sem("cks"), 1)
            dve.wait_ge(sem("kv_stored"), 64)
            pairs("b")
            dve.wait_ge(sem("szs_set"), 32)
            dve.wait_ge(sem("qs_set"), 32)
            decode("cmp", NCB, 0, None)
            dve.wait_ge(sem("imp_mm"), 1)
            imp, eq, mn, dr = SS[:, 400:416], SS[:, 416:430], SS[:, 206:207], SS[:, 207:208]
            pen = SS[:, 432:448]
            step(dve.tensor_reduce(imp, PS[:, 1, 0:NCB].rearrange("p (j c) -> p j c", c=2), AX, ALU.add))
            step(dve.tensor_reduce(mn, imp[:, 1:15], AX, ALU.min))
            step(dve.scalar_tensor_tensor(eq, imp[:, 1:15], mn, CST[:, C_JW + 1:C_JW + 15], ALU.is_equal, ALU.mult))
            step(dve.tensor_reduce(dr, eq, AX, ALU.max))
            step(dve.tensor_scalar(pen, CST[:, C_JW:C_JW + 16], dr, -BIG / SCALE, ALU.is_equal, ALU.mult))
            dve.wait_ge(sem("b_rows_in"), 16)
            rowf = STR[:, :, :].rearrange("p a n -> p (a n)")
            row2 = QT
            dve.tensor_tensor(row2[:, 0:PAST].rearrange("p (j x) -> p j x", j=16), rowf[:, 0:PAST].rearrange("p (j x) -> p j x", j=16),
                              pen.unsqueeze(2).to_broadcast([P, 16, SB]), ALU.add)
            dve.tensor_copy(row2[:, PAST:PAST + 1], rowf[:, PAST:PAST + 1]).then_inc(sem("imp_done"), 1)
            dve.wait_ge(sem("imp_done"), 1)
            decode_out("cmp", True)
            dve.wait_ge(sem("d_qk"), DN["sel"])
            dve.wait_ge(sem("new_keys"), 6)
            nm, den, r = SS[:, 200:201], SS[:, 201:202], SS[:, 202:203]
            dve.tensor_tensor_reduce(PB[:, 0, 0:PAST + 1], PSf[:, 0:PAST + 1], row2[:, 0:PAST + 1], -SCALE, 3 * BIG,
                                     ALU.add, ALU.min, nm).then_inc(sem("d_sm"), 1)
            dve.wait_ge(sem("d_ex"), DN["sel"])
            step(dve.reciprocal(r, den))
            step(dve.tensor_scalar(PB[:, 2, 0:PAST + 1], PB[:, 1, 0:PAST + 1], r, SGS[:, 1:2], ALU.mult, ALU.mult))
            dve.tensor_scalar(SS[:, 0:DEC], CST[:, C_DN:C_DN + DEC], PB[:, 2, PAST:PAST + 1], None, ALU.mult).then_inc(sem("d_p"), 1)
            dve.wait_ge(sem("d_tr"), DN["sel"])
            dve.tensor_copy(SS[0:DEC, 16:16 + P], PS[0:DEC, 6, 0:P]).then_inc(sem("d_pt"), 1)
            decode_out("sel", False)
            decode("win", WIN_B, 1, 2)
            decode_out("win", False)
            residual(NC, 56)
            norm("f", None)


def kernel(**inputs):
    import concourse.bacc as _bacc
    from concourse.bass_utils import run_bass_kernel_spmd as _run

    f = {k: np.asarray(v) for k, v in inputs.items()}
    chunked = lambda a: np.ascontiguousarray(a.reshape(NC, P, -1).transpose(1, 0, 2))

    def tiles(w):
        return np.ascontiguousarray(w.reshape(NC, P, -1, P).transpose(2, 1, 0, 3))

    def vec(a):
        return a.reshape(-1, P).T

    x = np.concatenate([f["x_prompt"][0], f["x_sample"][:, 0]], 0).T
    c = np.concatenate([f["c_prompt"], f["c_sample"]], 0).T
    wa, wkv, wb = f["a_w_in"][0], f["kv_w_in"], f["b_w_in"][0]
    hd, kvd = H * HDIM, KVH * HDIM

    def both(w):
        return np.concatenate([w, w], 1)

    def kv_cols(w, at):
        return [both(w[:, at:at + HDIM]), both(w[:, at + HDIM:at + 2 * HDIM]), w[:, at + kvd:at + 2 * kvd]]

    w_a0 = np.concatenate(kv_cols(wa, hd), 1)
    pair = lambda w, at, i: w[:, at + i * P:at + (i + 1) * P]
    w_a = np.concatenate([pair(wa, at, i) for i in range(PAIRS) for at in (0, hd + 2 * kvd)], 1)
    w_kv = np.concatenate([wkv[:, 0:2 * kvd]] + kv_cols(wkv, 2 * kvd) + kv_cols(wkv, 4 * kvd), 1)
    w_b = np.concatenate([pair(wb, at, i) for i in range(PAIRS) for at in (0, hd, 2 * hd, 3 * hd)], 1)
    w_gl = np.concatenate([wb[:, 4 * hd:], np.zeros((DM, P - 3 * H), wb.dtype)], 1)
    w_ada = np.concatenate([tiles(f["a_w_ada"][0]), tiles(f["kv_w_ada"]), tiles(f["b_w_ada"][0])], 0)
    sink = f["a_sinks"][0]
    pos = f["cmp_pos"].reshape(16, 2, 2, HDIM).transpose(1, 3, 2, 0).reshape(P, 32)
    vecs = np.concatenate([vec(f["a_norm_g"][0]), vec(f["kv_norm_g"]), vec(f["b_norm_g"][0]), vec(f["final_norm_g"]),
                           vec(f["a_b_ada"][0]), vec(f["kv_b_ada"]), vec(f["b_b_ada"][0]),
                           np.tile(sink, (P, 1)), np.tile(sink, DEC)[:, None], pos], 1)
    w1 = f["cmp_w1"].reshape(2, 16, P, P).transpose(2, 0, 1, 3).reshape(P, 4096)
    w2 = f["cmp_w2"].transpose(1, 0, 2)
    pool = f["cache_cmp_kv"].reshape(-1, 4, 16, 2, 2, KVH, HDIM).transpose(0, 4, 3, 6, 5, 1, 2).reshape(-1, 2, P, P)
    sel, sa, sw = f["cache_sel_kv"], f["state_a_kv"][0], f["state_win_kv"]
    rows = lambda a, k: a[:, :, k].reshape(a.shape[0], a.shape[1], P)

    const = np.zeros((P, C_END), np.float32)
    const[:, C_ID:C_ID + P] = np.eye(P)
    q = np.arange(P)
    ends = np.arange(NCB) * CB + CB - 1
    for qb in range(QB):
        const[:, C_CM + qb * NCB:C_CM + (qb + 1) * NCB] = np.where(ends[None] <= qb * P + q[:, None], 0.0, BIG)
    const[q, C_DN + q // H] = 1.0
    const[q, C_DH + q % H] = 1.0
    const[:, C_GS:C_GS + P] = (q[:, None] // 8 == q[None] // 8)
    const[:, C_FAR:C_FAR + P] = np.where(q[:, None] <= q[None], 0.0, -BIG / SCALE)
    for n in range(DEC):
        const[n, C_EN + n * H:C_EN + (n + 1) * H] = 1.0
    const[:, C_JW:C_JW + 16] = np.arange(1, 17)
    const[q, C_M4 + q // H % 4] = 1.0
    dist = PAST - np.arange(NBIAS)
    n_ = np.maximum(dist, 0)
    large = 16 + (np.log(np.maximum(n_, 16).astype(np.float32) / np.float32(16)) / np.float32(np.log(8.0)) * np.float32(16)).astype(np.int32)
    bucket = np.where(n_ < 16, n_, np.minimum(large, 31))
    onehot = (np.arange(32)[:, None] == bucket[None]).astype(np.float32)
    causal = np.tile(np.where(dist < 0, -BIG / SCALE, 0.0).astype(np.float32), (P, 1))

    ins = dict(
        c=chunked(c), const=const, vec=vecs, w_ada=w_ada, table=np.tile(f["rel_bias_table"], (1, DEC)), onehot=onehot, causal=causal,
        pages=f["page_table"].reshape(1, -1).astype(np.int32), w2=w2, x=chunked(x),
        sa_kT=rows(sa, 0).transpose(0, 2, 1), sa_v=rows(sa, 1), sw_kT=rows(sw, 0).transpose(0, 2, 1), sw_v=rows(sw, 1),
        w_a0=tiles(w_a0), w_a=tiles(w_a), w_ao=tiles(f["a_w_out"][0]), w_kv=tiles(w_kv), w1=w1, w_gl=tiles(w_gl)[0],
        cmp_pool=pool, w_b=tiles(w_b), sel_kT=rows(sel, 0).transpose(0, 2, 1), sel_v=rows(sel, 1), w_bo=tiles(f["b_w_out"][0]),
    )
    outs = dict(o_sa_k=(DEC, P, WIN_A - 1), o_sa_v=(DEC, WIN_A - 1, P), o_sw_k=(DEC, P, WIN_B - 1), o_sw_v=(DEC, WIN_B - 1, P),
                o_kv_a=(2, P, WIN_A + DEC), o_kv=(6, P, TOK), o_y=(P, NC, TOK))
    nc = _bacc.Bacc("TRN2", target_bir_lowering=False, num_devices=1)
    t, arrays = {}, {}
    for name, a in ins.items():
        a = np.ascontiguousarray(a)
        arrays[name] = a
        t[name] = nc.dram_tensor(name, a.shape, mybir.dt.from_np(a.dtype), kind="ExternalInput").ap()
    for name, shape in outs.items():
        t[name] = nc.dram_tensor(name, shape, F32, kind="ExternalOutput").ap()
    t["scratch"] = nc.dram_tensor("scratch", (COPIES * H, NBIAS), F32, kind="Internal").ap()
    build(nc, t)
    r = _run(nc, [arrays], core_ids=[0]).results[0]
    o = {name: np.asarray(r[name]) for name in outs}

    kvr = lambda k, v: np.stack([k, v], 0).reshape(2, KVH, HDIM, -1).transpose(3, 0, 1, 2)
    y = o["o_y"].transpose(1, 0, 2).reshape(DM, TOK).T
    a_new = kvr(o["o_kv_a"][0], o["o_kv_a"][1])
    cmp_r, sel_r, win_r = (kvr(o["o_kv"][2 * i], o["o_kv"][2 * i + 1]) for i in range(3))

    def shifted(k, v, new):
        old = np.stack([k.transpose(0, 2, 1), v], 2).reshape(DEC, -1, 2, KVH, HDIM)
        return np.concatenate([old, new[:, None]], 1)

    return (y[None, :SEQ], y[SEQ:, None],
            a_new[None, None, :WIN_A], shifted(o["o_sa_k"], o["o_sa_v"], a_new[WIN_A:])[None],
            cmp_r[None, :SEQ], cmp_r[SEQ:, None], sel_r[None, :SEQ], sel_r[SEQ:, None],
            win_r[None, SEQ - WIN_B:SEQ], shifted(o["o_sw_k"], o["o_sw_v"], win_r[SEQ:]))
```

```python
from contextlib import ExitStack

import numpy as np
import concourse.bass as bass
from concourse import mybir

F32 = mybir.dt.float32
F32R = mybir.dt.float32r
BF16 = mybir.dt.bfloat16
I32 = mybir.dt.int32
ALU = mybir.AluOpType
ACT = mybir.ActivationFunctionType
AX = mybir.AxisListType.X

P = 128
SEQ, DEC, PAST = 1024, 8, 1024
TOK = SEQ + DEC
DM = 1024
NC = DM // P
H, HDIM, KVH = 16, 64, 2
PAIRS = H // 2
QB = SEQ // P
WIN_A, WIN_B = 128, 512
CB, SB = 32, 64
NCB = PAST // CB
PAGES = PAST // P
NPA = 6
THIRD = TOK // 3
NBIAS = PAST + P
NADA0, NADA = 16, 64
NTOK1 = DEC + 1
COPIES = 32
BIG = 1e30
SCALE = HDIM ** -0.5
EPS = 1e-6
CM_PAGES = 24

C_ID, C_CM, C_DN, C_DH, C_GS, C_FAR, C_EN, C_JW, C_M4, C_END = 0, 128, 384, 392, 408, 536, 664, 792, 808, 812
V_GA, V_GKV, V_GB, V_GF, V_BIAS, V_SINK, V_SINKS, V_POS, V_END = 0, 8, 16, 24, 32, 96, 112, 113, 145


def pair_plan(phase):
    branches = ["a"] if phase == "a" else ["cmp", "sel", "win"]
    jobs = [(b, s) for b in branches for s in range(2)]
    units, groups, plan = [], [], []
    for j, (b, s) in enumerate(jobs):
        if b == "cmp":
            units.append(dict(job=j, b=b, s=s, qb=None, keys=QB * NCB, first=0))
            continue
        for qb in range(QB):
            blocks = {"a": min(qb + 1, 2), "sel": qb + 1, "win": min(qb + 1, 5)}[b]
            units.append(dict(job=j, b=b, s=s, qb=qb, keys=blocks * P, first=qb + 1 - blocks))
    copies = 0
    for u, un in enumerate(units):
        un["groups"] = []
        n = 2 if un["b"] == "cmp" else -(-un["keys"] // 512)
        for i in range(n):
            groups.append(dict(kind="p", unit=u, part=i, last=(i == n - 1 and (u + 1 == len(units) or units[u + 1]["job"] != un["job"]))))
            un["groups"].append(groups[-1])
    pending, ended, turned = None, [], []

    def flush():
        nonlocal pending
        if pending is not None:
            plan.append(("pv", pending))
            if pending["last"]:
                ended.append(units[pending["unit"]]["job"])
            pending = None

    def turn(b):
        for half in range(2):
            g = dict(kind="o", b=b, part=half)
            plan.append(("tr", g))
            plan.append(("mix", g))

    for u in range(min(2, len(units))):
        plan += [("qk", u), ("sm", u), ("ex", u)]
    plan += [("slot", 0), ("slot_end", 0)]
    for u, un in enumerate(units):
        if u + 2 < len(units):
            plan.append(("qk", u + 2))
        for g in un["groups"]:
            plan.append(("tr", g))
            plan.append(("ev", g))
            flush()
            pending = g
            if g is un["groups"][0]:
                plan.append(("slot", u + 1))
        if turned:
            turn(turned.pop())
        while ended:
            j = ended.pop()
            plan.append(("oe", j))
            if j % 2:
                turned.append(jobs[j][0])
        if u + 2 < len(units):
            plan += [("sm", u + 2), ("ex", u + 2)]
        if u + 3 == len(units):
            plan.append(("qc", None))
        plan.append(("slot_end", u + 1))
    flush()
    plan.append(("oe", ended.pop()))
    plan.append(("slot", len(units) + 1))
    turn(jobs[-1][0])
    plan.append(("slot_end", len(units) + 1))
    n = c = m = 0
    order = []
    for what, g in plan:
        if what == "tr":
            g["n"] = n
            n += 1
            order.append(g)
            if g["kind"] == "p":
                g["c"] = c
                c += 1
            else:
                g["m"] = m
                m += 1
    for u, un in enumerate(units):
        un["trs"] = max(g["n"] for g in un["groups"]) + 1
    if phase == "a":
        runs = [("ada0", None, 0, (2,)), ("gate", "a", 0, (2, 2, 1)), ("ada1", None, 0, (3,)), ("q", None, 1, (2, 1, 2)),
                ("turn", None, 0, (1, 1))]
    else:
        runs = [("gate", "win", 0, (3, 3, 3)), ("gate", "cmp", 1, (3, 3, 3)), ("q", None, 1, (3, 3, 3)), ("gate", "sel", 1, (3, 3, 3))]

    def filled(last):
        fills, slots, at = [], {}, 0
        for kind, b, after, spans in runs:
            if last and phase == "b":
                spans = (1, 1, 1)
            for a, span in enumerate(spans):
                if not (last and after):
                    fl = dict(kind=kind[:3] if kind[:3] == "ada" else kind, b=b, after=after, third=int(kind[3]) if kind[:3] == "ada" else a, f=len(fills), mm=sum(1 for x in fills if x["kind"] in ("q", "gate")),
                              tanh=sum(1 for x in fills if x["kind"] == "gate"),
                              ev=sum(1 for x in fills if (x["kind"] == "q") == (kind == "q")), before=fills[-1] if fills else None)
                    fills.append(fl)
                    steps = NC
                    for i in range(span):
                        slots[at + i] = (fl, i * steps // span, (i + 1) * steps // span, i == span - 1)
                at += span
        assert at <= len(units) + 2
        out = []
        for what, g in plan:
            if what == "slot":
                if g in slots:
                    fl, k0, k1, end = slots[g]
                    out.append(("fill", (fl, k0, k1)))
                    if end:
                        out.append(("ft", fl))
            elif what == "slot_end":
                if g in slots and slots[g][3]:
                    out.append(("fe", slots[g][0]))
            elif not (what == "qc" and last):
                out.append((what, g))
        return fills, out

    fills, loop_plan = filled(False)
    _, last_plan = filled(True)
    first = [dict(kind=kind, b=b, after=0, third=a, tanh=3 * sum(1 for r in runs[:i] if r[2] and r[0] == "gate") + a)
             for i, (kind, b, after, _) in enumerate(runs) if after for a in range(3)]
    for i, fl in enumerate(first):
        fl["f"] = fl["mm"] = i
        fl["ev"] = fl["third"] if fl["kind"] == "q" else fl["tanh"]
    return dict(branches=branches, jobs=jobs, units=units, plan=loop_plan, last_plan=last_plan, order=order, first=first,
                U=len(units), N=n, C=c, M=m, J=len(jobs), FV=sum(1 for x in fills if x["kind"] != "q"), FM=sum(1 for x in fills if x["kind"] in ("q", "gate")),
                FT=sum(1 for x in fills if x["kind"] == "gate"))


def build(nc, t):
    ctx = ExitStack()
    with ctx:
        def sb(name, shape, dt=F32):
            return ctx.enter_context(nc.sbuf_tensor(name, shape, dt))

        def sb_rounded(name, shape):
            at = -(-nc.sbuf_base // 32) * 32
            tile = sb(name, shape)
            return tile, nc.alloc_sbuf_tensor_at(name + "_r", shape, F32R, offset=at)

        sems = {}

        def sem(name):
            if name not in sems:
                sems[name] = ctx.enter_context(nc.semaphore(name))
            return sems[name]

        XT, XTR = sb_rounded("XT", [P, NC, TOK])
        HT, HTR = sb_rounded("HT", [P, NC, TOK])
        MT, MTR = sb_rounded("MT", [P, NC, TOK])
        KD, KDR = sb_rounded("KD", [P, 2, KVH, TOK])
        VT = sb("VT", [P, 2, QB, P])
        STR = sb("STR", [P, 2, SEQ])
        WR, WRR = sb_rounded("WR", [P, 8 * 1024 + 64])
        PB = sb("PB", [P, 3, TOK])
        PT = sb("PT", [P, 2, 512])
        QT = sb("QT", [P, TOK])
        OS = sb("OS", [P, QB, P])
        QS = sb("QS", [P, DEC * 144])
        ADA = sb("ADA", [P, NADA, NTOK1])
        AG = sb("AG", [P, 3, NC, NTOK1])
        CST = sb("CST", [P, C_END])
        VEC = sb("VEC", [P, V_END])
        CE = sb("CE", [P, NC, NTOK1])
        IDB = sb("IDB", [P, P], BF16)
        FARB = sb("FARB", [P, P], BF16)
        ONE = sb("ONE", [P, 2])
        EPT = sb("EPT", [P, 1])
        NM = sb("NM", [P, 3, QB])
        DEN = sb("DEN", [P, 6, QB])
        RG = sb("RG", [P, QB])
        NSK = sb("NSK", [P, H + 1])
        SZS = sb("SZS", [P, 3, NC, DEC])
        SG = sb("SG", [P, QB, 3 * H])
        SGS = sb("SGS", [P, 3])
        CKP = sb("CKP", [P, 8 * 8])
        CKS = sb("CKS", [P, DEC, NCB])
        CV = sb("CV", [P, 3, P])
        W2 = sb("W2", [P, 2, HDIM])
        PC = sb("PC", [P, 2])
        PCH = sb("PCH", [P, 2])
        KN = sb("KN", [P, 3, DEC])
        VN = sb("VN", [DEC, 3, P])
        PGT = sb("PGT", [1, DEC * PAGES], I32)
        SS = sb("SS", [P, 512])
        PS = ctx.enter_context(nc.psum_tensor("PS", [P, 8, 512], F32))
        PSf = PS[:, :, :].rearrange("p b n -> p (b n)")

        ident = CST[:, C_ID:C_ID + P]
        GL = STR[:, :, :].rearrange("p a n -> p (a n)")[:, 0:TOK]
        Hf = HT[:, :, :].rearrange("p c n -> p (c n)")
        Mf = MT[:, :, :].rearrange("p c n -> p (c n)")
        CM = [Mf[:, i * CM_PAGES * P:(i + 1) * CM_PAGES * P] for i in range(2)]
        TAB = QT[0:32, 0:DEC * H]
        CT = QT[:, P:P + NC * NTOK1].rearrange("p (c n) -> p c n", c=NC)
        OSf = OS[:, :, :].rearrange("p b n -> p (b n)")
        RA = KD[0:NTOK1, 0, :, :].rearrange("p a n -> p (a n)")
        HS, HX, CK = OSf[:, 0:192], OSf[:, 192:384], OSf[:, 384:960]
        W1 = WR[:, 4096:8192].rearrange("p (k b h) -> p k b h", k=2, b=16)
        KDf = KD[:, :, :, :].rearrange("p a b n -> p (a b n)")

        def slot(i, base=None):
            w = WR if base is None else base
            return w[:, i * 1024:(i + 1) * 1024].rearrange("p (k m) -> p k m", m=P)

        def rounded(base):
            return WRR if base is None else KDRf

        SZ = {"a": KD[:, 1, 1, :], "cmp": WR[:, 5160:6192], "sel": WR[:, 6192:7224], "win": WR[:, 7224:8256]}
        BR = {"a": 0, "cmp": 0, "sel": 1, "win": 2}
        KSRC = {"a": 0, "sel": 0, "win": 1}
        DN = {"a": 1, "cmp": 2, "sel": 3, "win": 4}
        DPT = {"a": 2, "cmp": 3, "sel": 5, "win": 7}
        NRM = {"a": 0, "b": 1, "f": 2}
        ADA0 = {"a": 0, "kv": 24, "b": 40}
        plans = {ph: pair_plan(ph) for ph in "ab"}
        CHUNKS = {"a": 2, "b": 4}
        N_Q0, N_AO, N_KV, N_GL, N_B0, N_B, N_BO = 3, 19, 27, 35, 36, 39, 68
        ORDER = {"a": ("a", "q"), "b": ("win", "cmp", "q", "sel")}
        QN = {"a": KD[:, 1, 0, :], "b": WR[:, 4096:5128]}
        pa = plans["a"]
        FQ = 3 * PAIRS
        FV0 = {"a": 0, "b": PAIRS * 7}
        FV1 = {"a": 0, "b": PAIRS * 7 + 6}
        FM0 = {"a": 0, "b": 3 + (PAIRS - 1) * pa["FM"] + 3}
        FT0 = {"a": 0, "b": PAIRS * 3}
        FM_ALL = FM0["b"] + 3 * 4 * PAIRS
        L_A0, L_A, L_KV, L_GL, L_B = 0, 3, 3, 11, 12

        def done(n):
            if n < N_Q0:
                return sem("lin_mm"), n + 1
            if n < N_AO:
                return sem("fill_mm"), 3 * (n - N_Q0 + 1)
            if n < N_KV:
                return sem("op_mm"), 3 * (n - N_AO + 1)
            if n < N_B0:
                return sem("lin_mm"), L_KV + n - N_KV + 1
            if n < N_BO:
                return sem("fill_mm"), 3 * (N_AO - N_Q0) + 3 * (n - N_B0 + 1)
            return sem("op_mm"), 3 * NC + 3 * (n - N_BO + 1)

        KDRf = KDR[:, :, :, :].rearrange("p a b n -> p (a b n)")

        w_slots = WR[:, 0:8192].rearrange("p (s k m) -> p s k m", s=8, k=NC)
        RP = [CV[:, :, :].rearrange("p n c -> p (n c)")[0:NTOK1, :], SS[0:NTOK1, 0:3 * P]]

        def first_bank(ph, f):
            return f if ph == "a" else 4 + f if f < 4 else f - 4

        EARLY = (3, 2, 1)

        def lin_set(i):
            return PS[:, 3 * (i % 2):3 * (i % 2) + 3, 0:THIRD]

        def third(ap):
            return ap.rearrange("p (a n) -> p a n", a=3)

        block = ctx.enter_context(nc.Block())

        def compression_pages(eng, part, st):
            if st == 0:
                eng.wait_ge(sem("pages_in"), 16)
                eng.wait_ge(sem("mod_dec"), 3)
            if st < 2:
                eng.wait_ge(sem("mod_t"), 2 * NC + -(-(st + 1) * CM_PAGES * P // TOK))
            k, third_ = divmod(st, 3)
            if st >= 2:
                eng.wait_ge(sem("cm_mm"), st - 1)
            first, n = ((0, 8), (8, 8), (16, 8))[part] if third_ < 2 else ((0, 6), (6, 6), (12, 4))[part]
            with eng.Fori(0, n // 2) as i:
                pages = [eng.value_load(PGT[0:1, bass.ds(i * 2 + third_ * CM_PAGES + first + j, 1)], min_val=0, max_val=79) for j in range(2)]
                for j, page in enumerate(pages):
                    eng.dma_start(CM[st % 2][:, bass.ds(i * 2 * P + (first + j) * P, P)],
                                  t["cmp_pool"][bass.ds(page, 1), k].rearrange("o p n -> (o p) n"))\
                       .then_inc(sem(f"cm_full{part}{st % 2}"), 16)

        def selected_pages(eng, i0, i1, dst, src, loaded):
            with eng.Fori(i0 // 4, i1 // 4) as i:
                pages = [eng.value_load(PGT[0:1, bass.ds(i * 4 + j, 1)], min_val=0, max_val=79) for j in range(4)]
                for j, page in enumerate(pages):
                    eng.dma_start(dst[:, bass.ds(i * 4 * P + j * P, P)], t[src][bass.ds(page, 1)].rearrange("o p n -> (o p) n"))\
                       .then_inc(sem(loaded), 16)

        @block.gpsimd
        def _(pool):
            def split_chunk(full, count, j, base=None):
                raw = slot(j, base)
                high_r, raw_r = slot(2 + j, rounded(base)), slot(j, rounded(base))
                pool.wait_ge(sem(f"w_full{j}"), full)
                pool.tensor_tensor(high_r, raw, ONE[:, 0:1].unsqueeze(2).to_broadcast([P, NC, P]), ALU.mult).then_inc(sem("w_split"), 1)
                pool.wait_ge(sem("w_split"), count + 1)
                pool.tensor_tensor(raw_r, raw, high_r, ALU.subtract).then_inc(sem("w_split"), 1)

            def splits(n0, n1, base=None):
                for n in range(n0, n1):
                    split_chunk(16 * (n // 2 + 3), 2 * n, n % 2, base)

            def split_output(ph, c):
                n = {"a": 0, "b": 2 * NC}[ph] + 2 * c
                pool.tensor_tensor(XTR[:, c, 0:SEQ], MT[:, c, 0:SEQ], ONE[:, 0:1].to_broadcast([P, SEQ]), ALU.mult).then_inc(sem("mt_split"), 1)
                pool.wait_ge(sem("mt_split"), n + 1)
                pool.tensor_tensor(MTR[:, c, 0:SEQ], MT[:, c, 0:SEQ], XTR[:, c, 0:SEQ], ALU.subtract).then_inc(sem("mt_split"), 1)

            pool.wait_ge(sem("ones"), 2)
            splits(0, N_Q0 + 2)
            with pool.Fori(0, PAIRS - 1) as it:
                for i in range(2):
                    n = N_Q0 + 2 + i
                    split_chunk(it * 16 + 16 * (n // 2 + 3), it * 4 + 2 * n, n % 2)
            pool.wait_ge(sem("fill_mm"), FM0["b"])
            for c in range(NC):
                pool.wait_ge(sem("a_mix"), (c + 1) * plans["a"]["M"] + 1)
                split_output("a", c)
            splits(N_AO, N_B0 + 1)
            for st in range(6):
                compression_pages(pool, 1, st)
            splits(N_B0 + 1, N_B + 1)
            with pool.Fori(0, PAIRS - 1) as it:
                for i in range(4):
                    n = N_B + 1 + i
                    split_chunk(it * 32 + 16 * (n // 2 + 3), it * 8 + 2 * n, n % 2)
            pool.wait_ge(sem("fill_mm"), FM_ALL)
            selected_pages(pool, 0, 40, WR, "sel_v", "sel_v_in")
            last = (PAIRS - 1) * plans["b"]["M"]
            for i, m in enumerate((2, 4)):
                pool.wait_ge(sem("b_mix"), last + m + 1)
                selected_pages(pool, 40 + 8 * i, 48 + 8 * i, WR, "sel_v", "sel_v_in")
            for c in range(NC - 2):
                split_output("b", c)
            pool.wait_ge(sem("b_mix"), last + 7)
            selected_pages(pool, 56, 64, WR, "sel_v", "sel_v_in")
            for c in range(NC - 2, NC):
                split_output("b", c)
            splits(N_BO, N_BO + NC, KDf)

        @block.sync
        def _(sp):
            sp.dma_start(CT[:, :, :], t["c"]).then_inc(sem("c_in"), 16)
            sp.dma_start(CST[:, :], t["const"]).then_inc(sem("const_in"), 16)
            sp.dma_start(VEC[:, :], t["vec"]).then_inc(sem("vec_in"), 16)
            for s in range(8):
                sp.dma_start(slot(s), t["w_ada"][s]).then_inc(sem(f"w_full{s}"), 16)
            sp.dma_start(TAB[:, :], t["table"]).then_inc(sem("table_in"), 16)
            sp.dma_start(Mf[0:32, 0:NBIAS], t["onehot"]).then_inc(sem("table_in"), 16)
            sp.dma_start(Mf[:, 2048:2048 + NBIAS], t["causal"]).then_inc(sem("table_in"), 16)
            sp.dma_start(PGT[:, :], t["pages"]).then_inc(sem("pages_in"), 16)
            sp.dma_start(W2[:, :, :], t["w2"]).then_inc(sem("w2_in"), 16)
            for c in range(NC):
                sp.dma_start(XT[:, c, :], t["x"][:, c, :]).then_inc(sem(f"x_in{c % 2}"), 16)
            for s in range(8):
                sp.wait_ge(sem("ada_group"), s // 4 + 1)
                sp.dma_start(slot(s), t["w_ada"][8 + s]).then_inc(sem(f"w_full{s}"), 16)
            sp.wait_ge(sem("bias_row"), 1)
            for m in range(COPIES // DEC):
                sp.dma_start(t["scratch"][m * P:(m + 1) * P], PB[:, 0:2, :].rearrange("p a n -> p (a n)")[:, 0:NBIAS])\
                  .then_inc(sem("scratch"), 16)
            def weights(n, src, base=None):
                if n >= 2:
                    sp.wait_ge(*done(n - 2))
                sp.dma_start(slot(n % 2, base), src).then_inc(sem(f"w_full{n % 2}"), 16)

            sp.wait_ge(sem("ada_group"), 4)
            for k in range(3):
                weights(k, t["w_a0"][k])
            for k in range(2):
                weights(N_Q0 + k, t["w_a"][k])
            sp.wait_ge(sem("lin_ev"), L_A)
            for g in range(KVH):
                rows = slice(g * HDIM, (g + 1) * HDIM)
                sp.dma_start(t["o_kv_a"][0, rows, :], KD[rows, 0, g, SEQ - WIN_A:TOK]).then_inc(sem("stored"), 16)
            sp.dma_start(t["o_kv_a"][1], PB[:, 0, SEQ - WIN_A:TOK]).then_inc(sem("a_v_stored"), 16)
            sp.wait_ge(sem("a_v_stored"), 16)
            sp.wait_ge(sem("scratch"), 16 * COPIES // DEC)

            def loads(ph):
                pl, C = plans[ph], CHUNKS[ph]
                FM, U = FM0[ph] + len(pl["first"]), pl["U"]

                def chunk(i, k, j):
                    sp.dma_start(slot(j), t["w_" + ph][bass.ds(i * C + k, 1)].rearrange("o p k m -> (o p) k m"))\
                      .then_inc(sem(f"w_full{j}"), 16)

                def ada_chunks(i, g):
                    for k in range(3):
                        sp.dma_start(slot(4 + k), t["w_ada"][bass.ds(i * NPA + NADA0 + 3 * g + k, 1)].rearrange("o p k m -> (o p) k m"))\
                          .then_inc(sem(f"ada_full{k}"), 16)

                def strip(i, s):
                    for a in range(P // COPIES):
                        rows = bass.AP(t["scratch"].tensor, P - a * COPIES, [[NBIAS, H], [H * NBIAS - 1, COPIES], [1, SEQ]])
                        sp.dma_start(STR[a * COPIES:(a + 1) * COPIES, s, :],
                                     rows[bass.ds(i * 2 + s, 1)].rearrange("s p n -> (s p) n")).then_inc(sem(f"strip{s}"), 16)

                for s in range(2):
                    strip(0, s)
                if ph == "a":
                    ada_chunks(0, 0)
                else:
                    for i, k in ((1, 0), (2, 2), (3, 3)):
                        weights(N_B0 + i, t["w_b"][k])
                if ph == "a":
                    sp.dma_start(t["o_sa_k"], t["sa_kT"][:, :, 1:WIN_A]).then_inc(sem("stored"), 16)
                    sp.dma_start(t["o_sa_v"], t["sa_v"][:, 1:WIN_A, :]).then_inc(sem("stored"), 16)
                    sp.dma_start(t["o_sw_k"], t["sw_kT"][:, :, 1:WIN_B]).then_inc(sem("stored"), 16)
                    sp.dma_start(t["o_sw_v"], t["sw_v"][:, 1:WIN_B, :]).then_inc(sem("stored"), 16)
                with sp.Fori(0, PAIRS - 1) as it:
                    if ph == "a":
                        sp.wait_ge(sem("fill_mm"), it * 6 + FM)
                        chunk(it + 1, 0, 1)
                        sp.wait_ge(sem("ada_mm"), it * 2 + 1)
                        ada_chunks(it, 1)
                        sp.wait_ge(sem("fill_mm"), it * 6 + FM + 3)
                        chunk(it + 1, 1, 0)
                    else:
                        sp.wait_ge(sem("fill_mm"), it * 12 + FM)
                        chunk(it + 1, 1, 0)
                        sp.wait_ge(sem("fill_mm"), it * 12 + FM + 3)
                        chunk(it + 1, 0, 1)
                        sp.wait_ge(sem("fill_mm"), it * 12 + FM + 6)
                        chunk(it + 1, 2, 0)
                    sp.wait_ge(sem(ph + "_sm"), it * U + U - QB)
                    strip(it + 1, 0)
                    if ph == "a":
                        sp.wait_ge(sem("ada_mm"), it * 2 + 2)
                        ada_chunks(it + 1, 0)
                    else:
                        sp.wait_ge(sem("fill_mm"), it * 12 + FM + 9)
                        chunk(it + 1, 3, 1)
                    sp.wait_ge(sem(ph + "_sm"), it * U + U)
                    strip(it + 1, 1)
                if ph == "a":
                    sp.wait_ge(sem("ada_mm"), 2 * PAIRS - 1)
                    ada_chunks(PAIRS - 1, 1)

            def bring_back(src, times, after):
                sp.wait_ge(*after)
                for c in range(NC):
                    if c >= 2:
                        sp.wait_ge(sem(f"x_in{c % 2}"), 64 * times + 16 * (c // 2))
                    sp.dma_start(HT[:, c, :], t[src][:, c, :]).then_inc(sem(f"x_in{c % 2}"), 16)

            loads("a")
            sp.wait_ge(sem("fill_mm"), FM0["b"])
            sp.dma_start(Hf[:, 0:1024].rearrange("p (n k) -> p n k", n=DEC), t["sa_kT"].rearrange("n d k -> d n k"))\
              .then_inc(sem("a_dkv_in"), 16)
            sp.dma_start(Hf[:, 1024:2048].rearrange("p (n k) -> p n k", n=DEC), t["sa_v"].rearrange("n k d -> k n d"))\
              .then_inc(sem("a_dkv_in"), 16)
            sp.wait_ge(sem("a_sm"), PAIRS * plans["a"]["U"])

            def bias_rows(name):
                sp.dma_start(STR[:, :, :].rearrange("p a n -> p (a n)")[:, 0:NBIAS], t["scratch"][0:P]).then_inc(sem(name), 16)

            bias_rows("a_rows_in")
            for c in range(2):
                weights(N_AO + c, t["w_ao"][c])
            bring_back("x", 1, (sem("d_pv"), DN["a"]))
            for c in range(2, NC):
                weights(N_AO + c, t["w_ao"][c])
            for c in range(NC):
                sp.wait_ge(sem("op_ev"), 3 * c + 3)
                sp.dma_start(t["x_mid"][:, c, :], HT[:, c, :]).then_inc(sem("x_spilled"), 16)
            for k in range(NC):
                weights(N_KV + k, t["w_kv"][k])
            sp.wait_ge(sem("ada_mm"), 2 * PAIRS)
            sp.wait_ge(sem("a_mix"), PAIRS * plans["a"]["M"] + 1)
            sp.dma_start(WR[:, 4096:8192], t["w1"]).then_inc(sem("w1_in"), 16)
            sp.wait_ge(sem("lin_ev"), L_KV + 8)
            for j, part in ((0, KD[:, 0]), (1, KD[:, 1])):
                for g in range(KVH):
                    rows = slice(g * HDIM, (g + 1) * HDIM)
                    sp.dma_start(t["o_kv"][2 + 2 * j, rows, :], KD[rows, j, g, :]).then_inc(sem("stored"), 16)
            sp.dma_start(t["o_kv"][0], PB[:, 0, :]).then_inc(sem("kv_stored"), 16)
            sp.dma_start(t["o_kv"][1], PB[:, 1, :]).then_inc(sem("kv_stored"), 16)
            sp.dma_start(t["o_kv"][3], PB[:, 2, :]).then_inc(sem("kv_stored"), 16)
            sp.dma_start(t["o_kv"][5], QT[:, :]).then_inc(sem("kv_stored"), 16)
            weights(N_GL, t["w_gl"])
            weights(N_B0, t["w_b"][1])
            for st in range(6):
                compression_pages(sp, 0, st)
            sp.wait_ge(sem("kv_stored"), 64)
            sp.wait_ge(sem("gl_ev"), 2)
            loads("b")
            sp.wait_ge(sem("fill_mm"), FM_ALL)
            selected_pages(sp, 0, DEC * PAGES, Hf, "sel_kT", "sel_k_in")
            sp.wait_ge(sem("b_sm"), PAIRS * plans["b"]["U"])
            bias_rows("b_rows_in")
            sp.wait_ge(sem("b_qk"), PAIRS * plans["b"]["U"])
            for c in range(2):
                weights(N_BO + c, t["w_bo"][c], KDf)
            sp.wait_ge(sem("d_qk"), DN["sel"])
            sp.dma_start(Hf[:, 0:4096].rearrange("p (n k) -> p n k", n=DEC), t["sw_kT"].rearrange("n d k -> d n k"))\
              .then_inc(sem("win_dkv_in"), 16)
            sp.dma_start(Hf[:, 4096:8192].rearrange("p (n j k) -> p n j k", n=DEC, j=4),
                         t["sw_v"].rearrange("n (j k) d -> k n j d", j=4)).then_inc(sem("win_dkv_in"), 16)
            sp.wait_ge(sem("x_spilled"), 16 * NC)
            bring_back("x_mid", 2, (sem("d_pv"), DN["win"]))
            for c in range(2, NC):
                weights(N_BO + c, t["w_bo"][c], KDf)
            for c in range(NC):
                sp.wait_ge(sem("y_out"), c + 1)
                sp.dma_start(t["o_y"][:, c, :], XT[:, c, :]).then_inc(sem("stored"), 16)
            sp.wait_ge(sem("stored"), 16 * (4 + 2 + 4 + NC))

        @block.tensor
        def _(pe):
            def three_passes(out, w, high, low, k):
                hw, lw = w
                pe.matmul(out, hw[:, k, :], high, start=(k == 0), stop=False)
                pe.matmul(out, hw[:, k, :], low, start=False, stop=False)
                return pe.matmul(out, lw[:, k, :], high, start=False, stop=(k == NC - 1))

            def parts(j, base=None):
                return slot(2 + j, rounded(base)), slot(j, rounded(base))

            def product(set_, n, first=None):
                pe.wait_ge(sem("w_split"), 2 * n + 2)
                steps = [(k, a) for k in range(NC) for a in range(3)] if first is not None else [(k, a) for a in range(3) for k in range(NC)]
                if first is not None:
                    pe.wait_ge(sem("mod_dec"), first + 1)
                for k, a in steps:
                    if first is not None and a == 0:
                        pe.wait_ge(sem("mod_lo"), first * NC + k + 1)
                    cols = slice(a * THIRD, (a + 1) * THIRD)
                    last = three_passes(PS[:, 3 * set_ + a, 0:THIRD], parts(n % 2), HTR[:, k, cols], XTR[:, k, cols], k)
                last.then_inc(sem("lin_mm"), 1)

            def mean_square(name, c):
                sq = HT[:, c, :] if name == "a" else PB[:, c % 2, :]
                pe.wait_ge(sem("sq"), NRM[name] * NC + c + 1)
                for a in range(3):
                    last = pe.matmul(PS[:, 5 + a, 0:THIRD], ONE[:, 1:2].to_broadcast([P, P]), sq[:, a * THIRD:(a + 1) * THIRD],
                                     start=(c == 0), stop=(c == NC - 1))
                last.then_inc(sem("ms"), 1)

            def early_third(a):
                pe.wait_ge(sem("mt_split"), 4 * NC)
                pe.wait_ge(sem("w_split"), 2 * N_BO + 2)
                cols = slice(a * THIRD, (a + 1) * THIRD)
                for k in range(NC):
                    last = three_passes(PS[:, EARLY[a], 0:THIRD], parts(N_BO % 2, KDf), XTR[:, k, cols], MTR[:, k, cols], k)
                last.then_inc(sem("op_mm"), 1)

            def out_projection(name, n0, base=None):
                e0 = 0 if name == "b" else 3 * NC
                pe.wait_ge(sem("mt_split"), {"b": 2 * NC, "f": 4 * NC}[name])
                pe.wait_ge(sem("mt_dec"), NRM[name])
                for c in range(NC):
                    pe.wait_ge(sem("w_split"), 2 * (n0 + c) + 2)
                    for a in range(3):
                        early = name == "f" and c == 0
                        if early and a < 2:
                            continue
                        if c:
                            pe.wait_ge(sem("op_ev"), e0 + 3 * (c - 1) + (3 if c == 1 and a else a + 1))
                        cols = slice(a * THIRD, (a + 1) * THIRD)
                        for k in range(NC):
                            last = three_passes(PS[:, EARLY[a] if early else a, 0:THIRD], parts((n0 + c) % 2, base), XTR[:, k, cols], MTR[:, k, cols], k)
                        last.then_inc(sem("op_mm"), 1)
                    if c:
                        mean_square(name, c - 1)
                mean_square(name, NC - 1)

            pe.wait_ge(sem("table_in"), 48)
            for a in range(3):
                last = pe.matmul(PS[:, 5 + a, 0:384], TAB[:, :],
                                 Mf[0:32, a * 384:(a + 1) * 384], start=True, stop=True)
            last.then_inc(sem("row_mm"), 1)
            pe.wait_ge(sem("silu_c"), 1)
            for i in range(NADA0 // 4):
                for s in range(4):
                    pe.wait_ge(sem(f"w_full{4 * (i % 2) + s}"), i // 2 * 16 + 16)
                w4 = w_slots[:, 4 * (i % 2):4 * (i % 2) + 4]
                for k in range(NC):
                    last = pe.matmul(PS[0:NTOK1, i, :], CE[:, k, :], w4[:, :, k, :], start=(k == 0), stop=(k == NC - 1))
                last.then_inc(sem("ada_group"), 1)
            pe.wait_ge(sem("ones"), 1)
            pe.wait_ge(sem("const_in"), 16)
            for c in range(NC):
                if c == 0:
                    pe.wait_ge(sem("bias_row"), 1)
                mean_square("a", c)
            pe.wait_ge(sem("ada_rows"), NADA0 // 4)
            for i in range(NADA0):
                last = pe.transpose(PS[:, 4, i * NTOK1:(i + 1) * NTOK1], RA[:, i * P:(i + 1) * P], CST[0:NTOK1, C_ID:C_ID + NTOK1])
            last.then_inc(sem("ada_turned"), 1)
            for k in range(3):
                if k == 2:
                    pe.wait_ge(sem("lin_ev"), 1)
                product(k % 2, k, None if k else 0)
            pe.wait_ge(sem("lin_ev"), L_A)

            def turn_values(src, new, tag):
                for i in range(QB):
                    last = pe.transpose(PS[:, 4 + i // 4, (i % 4) * P:(i % 4 + 1) * P], src[:, i * P:(i + 1) * P], ident)
                pe.transpose(PS[0:DEC, 6, 0:P], src[:, SEQ:TOK], ident).then_inc(sem(tag), 1)

            turn_values(PB[:, 0, :], 0, "a_vt")
            pe.wait_ge(sem("a_vt_ev"), 2)

            def pairs(ph):
                pl, C = plans[ph], CHUNKS[ph]
                units, jobs, first = pl["units"], pl["jobs"], pl["first"]

                def third_product(fl, k0, k1, bank, n, splits):
                    if k0 == 0 and fl["third"] == 0:
                        pe.wait_ge(sem("w_split"), splits)
                    cols = slice(fl["third"] * THIRD, (fl["third"] + 1) * THIRD)
                    for k in range(k0, k1):
                        last = three_passes(PS[:, bank, 0:THIRD], parts(n % 2), HTR[:, k, cols], XTR[:, k, cols], k)
                    if k1 == NC:
                        last.then_inc(sem("fill_mm"), 1)

                for fl in first[3 if ph == "b" else 0:]:
                    if fl["f"] >= 8:
                        pe.wait_ge(sem("fill_ev"), FV0[ph] + 1)
                    n = {"a": N_Q0, "b": N_B0}[ph] + fl["f"] // 3
                    third_product(fl, 0, NC, first_bank(ph, fl["f"]), n, 2 * n + 2)
                pe.wait_ge(sem("q_ev"), (FQ if ph == "b" else 0) + 3)
                if ph == "b":
                    pe.wait_ge(sem("fill_ev"), FV1[ph])

                def pair(g, it, last_):
                        for what, x in pl["last_plan" if last_ else "plan"]:
                            if what == "fill":
                                fl, k0, k1 = x
                                if k0 == 0:
                                    b_ = fl["before"]
                                    if b_ is None:
                                        if ph == "b":
                                            pe.wait_ge(sem("fill_ev"), it * pl["FV"] + FV1[ph])
                                    elif b_["kind"] == "q":
                                        pe.wait_ge(sem("q_ev"), it * 3 + (FQ if ph == "b" else 0) + 3 + b_["ev"] + 1)
                                    else:
                                        pe.wait_ge(sem("fill_ev"), it * pl["FV"] + FV1[ph] + b_["ev"] + 1)
                                if fl["kind"] == "ada":
                                    for k in range(k0, k1):
                                        if k == 0:
                                            for i in range(3):
                                                pe.wait_ge(sem(f"ada_full{i}"), it * 32 + 16 * fl["third"] + 16)
                                        last = pe.matmul(PS[0:NTOK1, 7, 0:3 * P], CE[:, k, :], w_slots[:, 4:7, k, :],
                                                         start=(k == 0), stop=(k == NC - 1))
                                    if k1 == NC:
                                        last.then_inc(sem("ada_mm"), 1)
                                elif fl["kind"] == "turn":
                                    for i in range(3):
                                        last = pe.matmul(PS[:, 7, i * NTOK1:(i + 1) * NTOK1], RP[fl["third"]][:, i * P:(i + 1) * P],
                                                         CST[0:NTOK1, C_ID:C_ID + NTOK1], start=True, stop=True)
                                    last.then_inc(sem("ada_turned"), 1)
                                else:
                                    o = ORDER[ph]
                                    n = {"a": N_Q0 + 1, "b": N_B}[ph] + o.index(fl["b"] or "q")
                                    third_product(fl, k0, k1, 7, n, it * 2 * len(o) + 2 * n + 2)
                            elif what == "qk":
                                un = units[x]
                                if x == 0:
                                    pe.wait_ge(sem("q_ready"), it + (PAIRS if ph == "b" else 0) + 1)
                                if x >= 2:
                                    pe.wait_ge(sem(ph + "_sm"), it * pl["U"] + x - 1)
                                rows = slice(un["s"] * HDIM, (un["s"] + 1) * HDIM)
                                if un["b"] == "cmp":
                                    for qb in range(QB):
                                        keys = CKP[rows, :].rearrange("p (j g b) -> p j g b", j=8, g=2)[:, :, g, :]
                                        last = pe.matmul(PS[:, 2 * (x % 2), qb * NCB:(qb + 1) * NCB],
                                                         QT[rows, qb * P:(qb + 1) * P], keys, start=True, stop=True)
                                else:
                                    far = (un["b"] == "a" and un["qb"] >= 1) or (un["b"] == "win" and un["qb"] >= 4)
                                    for k0 in range(0, un["keys"], 512):
                                        n = min(512, un["keys"] - k0)
                                        key0 = un["first"] * P + k0
                                        last = pe.matmul(PS[:, 2 * (x % 2) + k0 // 512, 0:n],
                                                         QT[rows, un["qb"] * P:(un["qb"] + 1) * P],
                                                         KD[rows, KSRC[un["b"]], g, key0:key0 + n],
                                                         start=True, stop=not (far and k0 == 0))
                                        if far and k0 == 0:
                                            last = pe.matmul(PS[:, 2 * (x % 2), 0:P], IDB[:, :], FARB[:, :],
                                                             start=False, stop=True)
                                last.then_inc(sem(ph + "_qk"), 1)
                            elif what == "tr":
                                if x["n"] < 2:
                                    pe.wait_ge(sem(ph + "_mix"), it * pl["M"] + 1)
                                else:
                                    before = pl["order"][x["n"] - 2]
                                    if before["kind"] == "o":
                                        pe.wait_ge(sem(ph + "_mix"), it * pl["M"] + before["m"] + 2)
                                    elif before["c"] % 2:
                                        pe.wait_ge(sem(ph + "_evd"), it * (pl["C"] // 2) + before["c"] // 2 + 1)
                                    else:
                                        pe.wait_ge(sem(ph + "_eva"), it * ((pl["C"] + 1) // 2) + before["c"] // 2 + 1)
                                bank = 4 + x["n"] % 2
                                if x["kind"] == "o":
                                    job = 2 * pl["branches"].index(x["b"]) + 1
                                    pe.wait_ge(sem(ph + "_oe"), it * pl["J"] + job + 1)
                                    for i in range(4):
                                        last = pe.transpose(PS[:, bank, i * P:(i + 1) * P], OS[:, 4 * x["part"] + i, :], ident)
                                else:
                                    u = x["unit"]
                                    un = units[u]
                                    pe.wait_ge(sem(ph + "_ex"), it * pl["U"] + u + 1)
                                    if un["b"] == "cmp":
                                        for i in range(4):
                                            qb = 4 * x["part"] + i
                                            last = pe.transpose(PS[0:NCB, bank, i * P:(i + 1) * P],
                                                                PB[:, u % 3, qb * NCB:(qb + 1) * NCB], ident)
                                    else:
                                        at = 513 if ph == "a" else 0
                                        for i in range(min(4, un["keys"] // P - 4 * x["part"])):
                                            k0 = at + (4 * x["part"] + i) * P
                                            last = pe.transpose(PS[:, bank, i * P:(i + 1) * P], PB[:, u % 3, k0:k0 + P], ident)
                                last.then_inc(sem(ph + "_tr"), 1)
                            elif what == "pv":
                                u = x["unit"]
                                un = units[u]
                                c = x["c"]
                                if c % 2:
                                    pe.wait_ge(sem(ph + "_evd"), it * (pl["C"] // 2) + c // 2 + 1)
                                else:
                                    pe.wait_ge(sem(ph + "_eva"), it * ((pl["C"] + 1) // 2) + c // 2 + 1)
                                j = un["job"]
                                if j >= 1 and un["qb"] in (None, 0) and x["part"] == 0:
                                    pe.wait_ge(sem(ph + "_oe"), it * pl["J"] + j)
                                if un["b"] == "cmp":
                                    for i in range(4):
                                        qb = 4 * x["part"] + i
                                        last = pe.matmul(PS[:, 6, qb * HDIM:(qb + 1) * HDIM],
                                                         PT[0:NCB, c % 2, i * P:(i + 1) * P],
                                                         CV[0:NCB, 2, g * HDIM:(g + 1) * HDIM], start=True, stop=True)
                                else:
                                    blocks = un["keys"] // P
                                    for i in range(min(4, blocks - 4 * x["part"])):
                                        b = 4 * x["part"] + i
                                        last = pe.matmul(PS[:, 6, un["qb"] * HDIM:(un["qb"] + 1) * HDIM],
                                                         PT[:, c % 2, i * P:(i + 1) * P],
                                                         VT[:, KSRC[un["b"]], un["first"] + b, g * HDIM:(g + 1) * HDIM],
                                                         start=(b == 0), stop=(b == blocks - 1))
                                last.then_inc(sem(ph + "_pv"), 1)
                        if ph == "a":
                            pe.wait_ge(sem("fill_ev"), it * pl["FV"] + pl["FV"])

                for g, i0, i1 in ((0, 0, PAIRS // 2), (1, PAIRS // 2, PAIRS - 1)):
                    with pe.Fori(i0, i1) as it:
                        pair(g, it, False)
                pair(1, PAIRS - 1, True)

            pairs("a")

            def decode_scores(b, keys, new):
                for k0 in range(0, keys, 512):
                    n_ = min(512, keys - k0)
                    for n in range(DEC):
                        last = pe.matmul(PSf[:, k0:k0 + n_], QS[:, n * P:(n + 1) * P],
                                         (CKS[:, n, :] if b == "cmp" else Hf[:, n * keys + k0:n * keys + k0 + n_]),
                                         start=(n == 0), stop=(n == DEC - 1))
                if new is not None:
                    for n in range(DEC):
                        last = pe.matmul(PSf[:, keys:keys + 1], QS[:, n * P:(n + 1) * P], KN[:, new, n:n + 1],
                                         start=(n == 0), stop=(n == DEC - 1))
                last.then_inc(sem("d_qk"), 1)

            def decode_values(b, keys, values, new):
                pe.wait_ge(sem("d_p"), DN[b])
                for i in range(keys // P):
                    pe.transpose(PSf[:, 2048 + i * P:2048 + (i + 1) * P], PB[:, 2, i * P:(i + 1) * P], ident)
                pe.transpose(PS[0:DEC, 6, 0:P], SS[:, 0:DEC], ident).then_inc(sem("d_tr"), 1)
                pe.wait_ge(sem("d_pt"), DPT[b])
                pe.matmul(PS[:, 7, 0:P], VN[:, new, :], SS[0:DEC, 16:16 + P], start=True, stop=True)
                for n in range(DEC):
                    for i in range(keys // P):
                        last = pe.matmul(PS[:, 7, n * H:(n + 1) * H], values(n, i),
                                         PB[:, 0, i * P + n * H:i * P + (n + 1) * H],
                                         start=False, stop=True,
                                         skip_group_check=True)
                last.then_inc(sem("d_pv"), 1)

            plA, plB = plans["a"], plans["b"]
            pe.wait_ge(sem("a_dkv_in"), 32)
            pe.wait_ge(sem("a_mix"), PAIRS * plA["M"] + 1)
            pe.wait_ge(sem("a_oe"), PAIRS * plA["J"])
            decode_scores("a", WIN_A, 0)
            decode_values("a", WIN_A, lambda n, i: Hf[:, 1024 + n * P:1024 + (n + 1) * P], 0)

            pe.wait_ge(sem("d_out"), DN["a"])
            out_projection("b", N_AO)
            for k in range(8):
                if k:
                    pe.wait_ge(sem("lin_ev"), L_KV + k - 1)
                product(k % 2, N_KV + k, None if k else 1)
            pe.wait_ge(sem("lin_ev"), L_KV + 8)
            turn_values(PB[:, 2, :], 0, "sel_vt")
            pe.wait_ge(sem("sel_vt_ev"), 2)
            turn_values(QT[:, :], 1, "win_vt")
            pe.wait_ge(sem("w1_in"), 16)
            pe.wait_ge(sem("w2_in"), 16)
            for k in range(2):
                for b in range(16):
                    last = pe.matmul(PS[:, 3, k:k + 1], W1[:, k, b, :], VEC[:, V_POS + 16 * k + b:V_POS + 16 * k + b + 1],
                                     start=(b == 0), stop=(b == 15))
            last.then_inc(sem("pc_mm"), 1)
            pe.wait_ge(sem("win_vt_ev"), 2)
            product(0, N_GL, 2)
            pe.wait_ge(sem("lin_ev"), L_GL + 1)
            for i in range(QB):
                last = pe.transpose(PS[:, 6, i * 3 * H:(i + 1) * 3 * H], GL[0:3 * H, i * P:(i + 1) * P], CST[0:3 * H, C_ID:C_ID + 3 * H])
            pe.transpose(PS[0:DEC, 7, 0:3 * H], GL[0:3 * H, SEQ:TOK], CST[0:3 * H, C_ID:C_ID + 3 * H])\
              .then_inc(sem("gl_tr"), 1)
            pe.wait_ge(sem("gl_ev"), 2)
            pe.matmul(PS[:, 6, 0:3 * H], CST[0:DEC, C_EN:C_EN + P], SS[0:DEC, 0:3 * H], start=True, stop=True)\
              .then_inc(sem("gs_mm"), 1)
            for st in range(6):
                k, third_ = divmod(st, 3)
                for part in range(3):
                    loads_ = sum(8 if s % 3 < 2 else (6, 6, 4)[part] for s in range(st % 2, st + 1, 2))
                    pe.wait_ge(sem(f"cm_full{part}{st % 2}"), 16 * loads_)
                if third_ == 2:
                    pe.wait_ge(sem("cm_own"), k + 1)
                if st >= 2:
                    pe.wait_ge(sem("hid"), st - 1)
                for b in range(16):
                    last = pe.matmul(PS[:, st % 2, 0:CM_PAGES * 8], W1[:, k, b, :], CM[st % 2][:, b::16],
                                     start=(b == 0), stop=(b == 15))
                last.then_inc(sem("cm_mm"), 1)
                if st < 3:
                    if st == 0:
                        pe.wait_ge(sem("w_split"), 2 * N_B0 + 2)
                        pe.wait_ge(sem("lin_ev"), L_B)
                    cols = slice(st * THIRD, (st + 1) * THIRD)
                    for kc in range(NC):
                        last = three_passes(PS[:, 4 + st, 0:THIRD], parts(N_B0 % 2), HTR[:, kc, cols], XTR[:, kc, cols], kc)
                    last.then_inc(sem("fill_mm"), 1)
                pe.wait_ge(sem("hid"), st + 1)
                if st:
                    pe.wait_ge(sem("ckv_ev"), min(st, 3))
                if k == 0:
                    for half in range(2):
                        last = pe.matmul(PS[half * HDIM:(half + 1) * HDIM, 2, 0:CM_PAGES * 8], W2[:, 0, :], HS[:, :],
                                         start=True, stop=True)
                else:
                    hs = HX.rearrange("p (n g c) -> p n g c", n=3, g=2)
                    for n in range(3):
                        for g in range(KVH):
                            q, at = (3 * third_ + n) % 4 * NCB, (3 * third_ + n) // 4 * P + g * HDIM
                            last = pe.matmul(PS[q:q + NCB, 2, at:at + HDIM], hs[:, n, g], W2[:, 1, :], start=True, stop=True)
                last.then_inc(sem("ckv_mm"), 1)
            pe.wait_ge(sem("ckv_ev"), 5)
            pe.wait_ge(sem("gs_ev"), 1)
            pe.wait_ge(sem("lin_ev"), L_B)
            pairs("b")
            pe.wait_ge(sem("b_mix"), PAIRS * plB["M"] + 1)
            pe.wait_ge(sem("b_oe"), PAIRS * plB["J"])
            decode_scores("cmp", NCB, None)
            pe.wait_ge(sem("d_p"), DN["cmp"])
            pe.matmul(PS[:, 1, 0:NCB], CST[:, C_GS:C_GS + P], PB[:, 1, 0:NCB], start=True, stop=True).then_inc(sem("imp_mm"), 1)
            pe.transpose(PS[:, 4, 0:P], PB[:, 2, 0:P], ident).then_inc(sem("d_tr"), 1)
            pe.wait_ge(sem("d_pt"), DPT["cmp"])
            for i in range(2):
                last = pe.matmul(PS[:, 7, i * 4 * H:(i + 1) * 4 * H], CV[:, i, :], PB[:, 0, i * 4 * H:(i + 1) * 4 * H],
                                 start=True, stop=True)
            last.then_inc(sem("d_pv"), 1)
            pe.wait_ge(sem("sel_k_in"), 16 * DEC * PAGES)
            pe.wait_ge(sem("imp_done"), 1)
            decode_scores("sel", PAST, 1)
            early_third(0)
            pe.wait_ge(sem("d_out"), DN["cmp"])
            pe.wait_ge(sem("sel_v_in"), 16 * DEC * PAGES)
            decode_values("sel", PAST, lambda n, i: WR[:, (n * PAGES + i) * P:(n * PAGES + i + 1) * P], 1)
            pe.wait_ge(sem("win_dkv_in"), 32)
            decode_scores("win", WIN_B, 2)
            early_third(1)
            pe.wait_ge(sem("d_out"), DN["sel"])
            decode_values("win", WIN_B, lambda n, i: Hf[:, 4096 + (n * 4 + i) * P:4096 + (n * 4 + i + 1) * P], 2)
            pe.wait_ge(sem("d_out"), DN["win"])
            out_projection("f", N_BO, KDf)

        @block.scalar
        def _(act):
            act.wait_ge(sem("c_in"), 16)
            act.activation(CE[:, :, :], CT[:, :, :], ACT.Tanh, scale=0.5).then_inc(sem("tanh_c"), 1)

            def norm(name, ready):
                for c in range(NC):
                    ready(c)
                    if name == "a":
                        act.activation(HT[:, c, :], XT[:, c, :], ACT.Square).then_inc(sem("sq"), 1)
                    else:
                        if c >= 2:
                            act.wait_ge(sem("ms"), NRM[name] * NC + c - 1)
                        act.activation(PB[:, c % 2, :], HT[:, c, :], ACT.Square).then_inc(sem("sq"), 1)
                act.wait_ge(sem("ms"), NRM[name] * NC + NC)
                act.activation(third(PB[:, 2, :]), PS[:, 5:8, 0:THIRD], ACT.Ln, bias=EPT[:, :]).then_inc(sem("ln_ms"), 1)
                act.wait_ge(sem("ln_ms"), NRM[name] + 1)
                act.activation(PB[:, 2, :], PB[:, 2, :], ACT.Exp, scale=-0.5).then_inc(sem("rstd"), 1)

            def modulate(name, part):
                act.wait_ge(sem(name + "_ag"), 1)
                for c in range(NC):
                    act.wait_ge(sem("a_y" if name == "a" else "b_y"), c + 1)
                    act.activation(XT[:, c, 0:SEQ], MT[:, c, 0:SEQ], ACT.Identity, scale=AG[:, part, c, 0:1],
                                   bias=ADA[:, ADA0[name] + c, 0:1]).then_inc(sem("mod_t"), 1)
                    act.wait_ge(sem("mod_t"), part * NC + c + 1)
                    act.activation(HTR[:, c, 0:SEQ], XT[:, c, 0:SEQ], ACT.Copy).then_inc(sem("mod_hi"), 1)

            act.wait_ge(sem("ones"), 2)

            def first(c):
                if c == 0:
                    act.wait_ge(sem("x_in0"), 64)
                    act.wait_ge(sem("x_in1"), 64)

            norm("a", first)
            modulate("a", 0)
            act.wait_ge(sem("a_vt"), 1)
            act.activation(VT[:, 0, :, :].rearrange("p b n -> p (b n)"), PSf[:, 2048:3072], ACT.Copy).then_inc(sem("a_vt_ev"), 1)

            def pairs(ph):
                pl, C = plans[ph], CHUNKS[ph]
                units, first = pl["units"], pl["first"]

                def third_out(fl, bank):
                    cols = slice(fl["third"] * THIRD, (fl["third"] + 1) * THIRD)
                    if fl["kind"] == "q":
                        act.activation(QN[ph][:, cols], PS[:, bank, 0:THIRD], ACT.Copy).then_inc(sem("q_ev"), 1)
                    else:
                        act.activation(SZ[fl["b"]][:, cols], PS[:, bank, 0:THIRD], ACT.Tanh, scale=0.5).then_inc(sem("fill_tanh"), 1)

                if ph == "b":
                    act.wait_ge(sem("kv_stored"), 64)
                for fl in first:
                    act.wait_ge(sem("fill_mm"), FM0[ph] + fl["mm"] + 1)
                    third_out(fl, first_bank(ph, fl["f"]))
                    if fl["kind"] == "q" and fl["third"] == 2:
                        act.wait_ge(sem("q_ev"), (FQ if ph == "b" else 0) + 3)
                        act.activation(QT[:, :], QN[ph], ACT.Copy).then_inc(sem("q_ready"), 1)

                def pair(it, last_):
                    for what, x in pl["last_plan" if last_ else "plan"]:
                        if what == "ft" and x["kind"] in ("q", "gate"):
                            act.wait_ge(sem("fill_mm"), it * pl["FM"] + FM0[ph] + len(first) + x["mm"] + 1)
                            if x["kind"] == "gate" and x["third"] == 0:
                                m = {"a": 0, "win": 0, "cmp": 2, "sel": 4}[x["b"]]
                                act.wait_ge(sem(ph + "_mix"), it * pl["M"] + m + 1)
                            third_out(x, 7)
                        elif what == "qc":
                            act.wait_ge(sem(ph + "_qk"), it * pl["U"] + pl["U"])
                            act.wait_ge(sem("qs_set"), it * 2 + (2 * PAIRS if ph == "b" else 0) + 2)
                            act.wait_ge(sem("q_ev"), it * 3 + (FQ if ph == "b" else 0) + 6)
                            act.activation(QT[:, :], QN[ph], ACT.Copy).then_inc(sem("q_ready"), 1)
                        elif what == "ex":
                            un = units[x]
                            act.wait_ge(sem(ph + "_sm"), it * pl["U"] + x + 1)
                            if un["b"] == "cmp":
                                act.activation(PB[:, x % 3, 0:un["keys"]], PB[:, x % 3, 0:un["keys"]], ACT.Exp)\
                                   .then_inc(sem(ph + "_ex"), 1)
                            elif ph == "a":
                                act.activation(PB[:, x % 3, 512:513 + un["keys"]], PB[:, x % 3, 0:1 + un["keys"]], ACT.Exp,
                                               scale=-1.0, bias=NM[:, x % 3, 0:1],
                                               accum_out=DEN[:, un["job"], un["qb"]:un["qb"] + 1]).then_inc(sem(ph + "_ex"), 1)
                            else:
                                act.activation(PB[:, x % 3, 0:un["keys"]], PB[:, x % 3, 0:un["keys"]], ACT.Exp,
                                               scale=-1.0, bias=NM[:, x % 3, 0:1],
                                               accum_out=DEN[:, un["job"], un["qb"]:un["qb"] + 1]).then_inc(sem(ph + "_ex"), 1)
                        elif what == "ev" and x["c"] % 2 == 0:
                            c, un = x["c"], units[x["unit"]]
                            act.wait_ge(sem(ph + "_tr"), it * pl["N"] + x["n"] + 1)
                            if c > 1:
                                act.wait_ge(sem(ph + "_pv"), it * pl["C"] + c - 1)
                            m = NCB if un["b"] == "cmp" else P
                            n = 512 if un["b"] == "cmp" else min(512, un["keys"] - 512 * x["part"])
                            act.activation(PT[0:m, c % 2, 0:n], PS[0:m, 4 + x["n"] % 2, 0:n], ACT.Copy).then_inc(sem(ph + "_eva"), 1)
                    act.wait_ge(sem(ph + "_pv"), it * pl["C"] + pl["C"])

                with act.Fori(0, PAIRS - 1) as it:
                    pair(it, False)
                pair(PAIRS - 1, True)

            pairs("a")

            def decode(b, keys, extra):
                act.wait_ge(sem("d_sm"), DN[b])
                act.activation(PB[:, 1, 0:keys + extra], PB[:, 0, 0:keys + extra], ACT.Exp, scale=-1.0,
                               bias=SS[:, 200:201], accum_out=SS[:, 201:202]).then_inc(sem("d_ex"), 1)
                act.wait_ge(sem("d_tr"), DN[b])
                if b == "cmp":
                    act.activation(PB[:, 0, 0:P], PS[:, 4, 0:P], ACT.Copy).then_inc(sem("d_pt"), 1)
                else:
                    act.activation(PB[:, 0, 0:keys], PSf[:, 2048:2048 + keys], ACT.Copy).then_inc(sem("d_pt"), 1)

            decode("a", WIN_A, 2)
            norm("b", lambda c: act.wait_ge(sem("op_ev"), 3 * c + 3))
            act.wait_ge(sem("x_spilled"), 16 * NC)
            modulate("kv", 1)
            act.wait_ge(sem("sel_vt"), 1)
            act.activation(VT[:, 0, :, :].rearrange("p b n -> p (b n)"), PSf[:, 2048:3072], ACT.Copy).then_inc(sem("sel_vt_ev"), 1)
            act.wait_ge(sem("win_vt"), 1)
            act.activation(VT[:, 1, :, :].rearrange("p b n -> p (b n)"), PSf[:, 2048:3072], ACT.Copy).then_inc(sem("win_vt_ev"), 1)
            act.wait_ge(sem("lin_mm"), L_KV + 8)
            modulate("b", 2)
            compression_pages(act, 2, 0)
            act.wait_ge(sem("lin_mm"), L_GL + 1)
            act.activation(third(GL[0:3 * H, :]), PS[0:3 * H, 0:3, 0:THIRD], ACT.Tanh, scale=0.5).then_inc(sem("gl_tanh"), 1)
            compression_pages(act, 2, 1)
            act.wait_ge(sem("pc_ev"), 2)
            for st in range(6):
                act.wait_ge(sem("cm_mm"), st + 1)
                if st:
                    act.wait_ge(sem("hid"), st)
                    act.wait_ge(sem("ckv_mm"), st)
                act.activation(HX[:, :], PS[:, st % 2, 0:CM_PAGES * 8], ACT.Tanh, scale=0.5, bias=PCH[:, st // 3:st // 3 + 1])\
                   .then_inc(sem("hid_tanh"), 1)
                if st < 4:
                    compression_pages(act, 2, st + 2)
            pairs("b")
            decode("cmp", NCB, 0)
            decode("sel", PAST, 1)
            decode("win", WIN_B, 1)
            norm("f", lambda c: act.wait_ge(sem("op_ev"), 3 * (NC + c) + 3))

        @block.vector
        def _(dve):
            chain = [0]

            def step(ins):
                chain[0] += 1
                ins.then_inc(sem("dve_step"), 1)
                dve.wait_ge(sem("dve_step"), chain[0])

            dve.memset(ONE[:, 0:1], 1.0)
            dve.memset(ONE[:, 1:2], 1.0 / DM).then_inc(sem("ones"), 1)
            dve.memset(EPT[:, :], EPS).then_inc(sem("ones"), 1)
            dve.memset(QS[:, :], 0.0).then_inc(sem("qs_zero"), 1)
            dve.wait_ge(sem("tanh_c"), 1)
            step(dve.scalar_tensor_tensor(CE[:, :, :].rearrange("p a b -> p (a b)"), CE[:, :, :].rearrange("p a b -> p (a b)"), 1.0,
                                          CT[:, :, :].rearrange("p a b -> p (a b)"), ALU.add, ALU.mult))
            dve.tensor_scalar(CE[:, :, :], CE[:, :, :], 0.5, None, ALU.mult).then_inc(sem("silu_c"), 1)
            dve.wait_ge(sem("row_mm"), 1)
            row = PB[:, 0:2, :].rearrange("p a n -> p (a n)")[:, 0:NBIAS]
            dve.scalar_tensor_tensor(row.rearrange("p (a n) -> p a n", a=3), PS[:, 5:8, 0:384], 1.0 / SCALE,
                                     Mf[:, 2048:2048 + NBIAS].rearrange("p (a n) -> p a n", a=3), ALU.mult, ALU.add)\
               .then_inc(sem("bias_row"), 1)
            dve.wait_ge(sem("bias_row"), 1)
            dve.wait_ge(sem("const_in"), 16)
            dve.wait_ge(sem("vec_in"), 16)
            dve.tensor_copy(IDB[:, :], ident)
            dve.tensor_copy(FARB[:, :], CST[:, C_FAR:C_FAR + P])
            dve.tensor_scalar(NSK[:, :], VEC[:, V_SINK:V_SINK + H + 1], -1.0, None, ALU.mult).then_inc(sem("row_ev"), 1)
            dve.wait_ge(sem("row_ev"), 1)
            for i in range(NADA0 // 4):
                dve.wait_ge(sem("ada_group"), i + 1)
                dve.tensor_copy(RA[:, i * 512:(i + 1) * 512], PS[0:NTOK1, i, :]).then_inc(sem("ada_rows"), 1)
            dve.wait_ge(sem("ada_turned"), 1)
            dve.tensor_tensor(ADA[:, 0:NADA0, :], PS[:, 4, 0:NADA0 * NTOK1].rearrange("p (a n) -> p a n", a=NADA0),
                              VEC[:, V_BIAS:V_BIAS + NADA0].unsqueeze(2).to_broadcast([P, NADA0, NTOK1]), ALU.add)\
               .then_inc(sem("ada_ev"), 1)
            dve.wait_ge(sem("ada_ev"), 1)

            def gains(name, part, g0):
                a0 = ADA0[name]
                dve.scalar_tensor_tensor(AG[:, part, :, :], ADA[:, a0 + NC:a0 + 2 * NC, :], 1.0,
                                         VEC[:, g0:g0 + NC].unsqueeze(2).to_broadcast([P, NC, NTOK1]), ALU.add, ALU.mult)\
                   .then_inc(sem(name + "_ag"), 1)
                dve.wait_ge(sem(name + "_ag"), 1)

            gains("a", 0, V_GA)

            def norm(name):
                dve.wait_ge(sem("rstd"), NRM[name] + 1)
                if name == "f":
                    for c in range(NC):
                        dve.scalar_tensor_tensor(XT[:, c, :], HT[:, c, :], VEC[:, V_GF + c:V_GF + c + 1], PB[:, 2, :],
                                                 ALU.mult, ALU.mult).then_inc(sem("y_out"), 1)

            def low(part, c):
                dve.wait_ge(sem("mod_hi"), part * NC + c + 1)
                dve.tensor_tensor(XTR[:, c, 0:SEQ], XT[:, c, 0:SEQ], HTR[:, c, 0:SEQ], ALU.subtract).then_inc(sem("mod_lo"), 1)

            def modulate(name, part, x=None):
                a0 = ADA0[name]
                dec = (slice(None), slice(None), slice(SEQ, TOK))
                if x is not None:
                    step(dve.tensor_tensor(MT[dec], x[dec], PB[:, 2, SEQ:TOK].unsqueeze(1).to_broadcast([P, NC, DEC]), ALU.mult))
                step(dve.tensor_tensor(XT[dec], MT[dec], AG[:, part, :, 1:NTOK1], ALU.mult))
                step(dve.tensor_tensor(XT[dec], XT[dec], ADA[:, a0:a0 + NC, 1:NTOK1], ALU.add))
                if name == "kv":
                    dve.wait_ge(sem("x_spilled"), 16 * NC)
                step(dve.tensor_copy(HTR[dec], XT[dec]))
                dve.tensor_tensor(XTR[dec], XT[dec], HTR[dec], ALU.subtract).then_inc(sem("mod_dec"), 1)
                for c in range(NC + 2):
                    if x is not None and c < NC:
                        dve.tensor_tensor(MT[:, c, 0:SEQ], x[:, c, 0:SEQ], PB[:, 2, 0:SEQ], ALU.mult)\
                           .then_inc(sem(name.replace("kv", "b") + "_y"), 1)
                    if c >= 2:
                        low(part, c - 2)

            def split_decode_output():
                dec = (slice(None), slice(None), slice(SEQ, TOK))
                step(dve.tensor_copy(XTR[dec], MT[dec]))
                dve.tensor_tensor(MTR[dec], MT[dec], XTR[dec], ALU.subtract).then_inc(sem("mt_dec"), 1)

            norm("a")
            modulate("a", 0, XT)
            dve.wait_ge(sem("scratch"), 16 * COPIES // DEC)
            for k, dst in enumerate((KD[:, 0, 0, :], KD[:, 0, 1, :], PB[:, 0, :])):
                dve.wait_ge(sem("lin_mm"), L_A0 + k + 1)
                dve.tensor_copy(third(dst), lin_set(k)).then_inc(sem("lin_ev"), 1)
            dve.wait_ge(sem("lin_ev"), L_A)

            def new_keys(j, kd):
                for g in range(KVH):
                    rows = slice(g * HDIM, (g + 1) * HDIM)
                    dve.tensor_copy(KN[rows, j, :], KD[rows, kd, g, SEQ:TOK]).then_inc(sem("new_keys"), 1)

            new_keys(0, 0)
            dve.wait_ge(sem("a_vt"), 1)
            dve.tensor_copy(VN[:, 0, :], PS[0:DEC, 6, 0:P]).then_inc(sem("a_vt_ev"), 1)
            dve.wait_ge(sem("a_v_stored"), 16)
            dve.wait_ge(sem("qs_zero"), 1)

            def pairs(ph):
                pl, C = plans[ph], CHUNKS[ph]
                units, jobs = pl["units"], pl["jobs"]
                RC = sum(1 if b == "a" else 3 if b == "cmp" else 2 for b, _ in jobs)
                CC = 4 * sum(1 for un in units if un["b"] == "cmp")
                first = pl["first"]

                def third_out(fl, bank, i):
                    cols = slice(fl["third"] * THIRD, (fl["third"] + 1) * THIRD)
                    tile = SZ[fl["b"]]
                    dve.scalar_tensor_tensor(tile[:, cols], tile[:, cols], 1.0, PS[:, bank, 0:THIRD], ALU.add, ALU.mult)\
                       .then_inc(sem("fill_ev"), 1)

                def decode_gate(b, i):
                    dve.tensor_copy(SZS[:, BR[b], bass.ds(i, 1), :].rearrange("p o n -> p (o n)"), SZ[b][:, SEQ:TOK])\
                       .then_inc(sem("szs_set"), 1)

                dve.memset(NM[:, 0, 1:2], 0.0).then_inc(sem(ph + "_mix"), 1)
                for fl in first:
                    if fl["kind"] == "gate":
                        dve.wait_ge(sem("fill_tanh"), FT0[ph] + fl["tanh"] + 1)
                        third_out(fl, first_bank(ph, fl["f"]), 0)
                        if fl["third"] == 2:
                            dve.wait_ge(sem("fill_ev"), FV0[ph] + fl["ev"] + 1)
                            decode_gate(fl["b"], 0)

                def pair(g, it, last_):
                        dve.wait_ge(sem("q_ready"), it + (PAIRS if ph == "b" else 0) + 1)
                        for s in range(2):
                            dve.tensor_copy(QS[g * HDIM:(g + 1) * HDIM, :].rearrange("p (n x) -> p n x", x=144)
                                            [:, :, bass.ds(it * 2 + s, 1)].rearrange("p n o -> p (n o)"),
                                            QT[s * HDIM:(s + 1) * HDIM, SEQ:TOK]).then_inc(sem("qs_set"), 1)
                        if ph == "a":
                            for s in range(3):
                                dve.tensor_copy(PB[:, s, 0:1], NSK[:, bass.ds(it * 2, 1)]).then_inc(sem("sink_set"), 1)
                        for what, x in pl["last_plan" if last_ else "plan"]:
                            if what == "fe" and x["kind"] == "ada":
                                dve.wait_ge(sem("ada_mm"), it * 2 + x["third"] + 1)
                                dve.tensor_copy(RP[x["third"]], PS[0:NTOK1, 7, 0:3 * P]).then_inc(sem("fill_ev"), 1)
                            elif what == "fe" and x["kind"] == "turn":
                                dve.wait_ge(sem("ada_turned"), it * 2 + x["third"] + 2)
                                c0 = it * NPA + NADA0 + 3 * x["third"]
                                dve.tensor_tensor(ADA[:, bass.ds(c0, 3), :], PS[:, 7, 0:3 * NTOK1].rearrange("p (a n) -> p a n", a=3),
                                                  VEC[:, bass.ds(c0 + V_BIAS, 3)].unsqueeze(2).to_broadcast([P, 3, NTOK1]), ALU.add)\
                                   .then_inc(sem("fill_ev"), 1)
                            elif what == "fe" and x["kind"] == "gate":
                                dve.wait_ge(sem("fill_tanh"), it * pl["FT"] + FT0[ph] + sum(1 for fl in first if fl["kind"] == "gate") + x["tanh"] + 1)
                                third_out(x, 7, it)
                                if x["third"] == 2:
                                    dve.wait_ge(sem("fill_ev"), it * pl["FV"] + FV1[ph] + x["ev"] + 1)
                                    decode_gate(x["b"], it + x["after"])
                            elif what == "sm":
                                un = units[x]
                                L = un["keys"]
                                if un["b"] in ("a", "sel") and un["qb"] == 0:
                                    dve.wait_ge(sem(f"strip{un['s']}"), it * 64 + (64 * PAIRS if ph == "b" else 0) + 64)
                                if ph == "a" and x < 3:
                                    dve.wait_ge(sem("sink_set"), it * 6 + 3)
                                if x >= 3:
                                    dve.wait_ge(sem(ph + "_tr"), it * pl["N"] + units[x - 3]["trs"])
                                if ph == "a" and QB <= x < QB + 3:
                                    dve.tensor_scalar(PB[:, x % 3, 0:1], NSK[:, bass.ds(it * 2 + 1, 1)], 1.0, None, ALU.mult).then_inc(sem("sink_set"), 1)
                                    dve.wait_ge(sem("sink_set"), it * 6 + 3 + x - QB + 1)
                                if un["b"] == "cmp":
                                    cc = 3 * x
                                    dve.wait_ge(sem(ph + "_qk"), it * pl["U"] + x + 1)
                                    xx = PB[:, x % 3, 0:L]
                                    x3 = xx.rearrange("p (q c) -> p q c", q=QB)
                                    dve.scalar_tensor_tensor(xx, PS[:, 2 * (x % 2), 0:L], -SCALE, CST[:, C_CM:C_CM + L],
                                                             ALU.mult, ALU.add).then_inc(sem("cmp_step"), 1)
                                    dve.wait_ge(sem("cmp_step"), it * CC + cc + 1)
                                    dve.tensor_reduce(NM[:, x % 3, :], x3, AX, ALU.min).then_inc(sem("cmp_step"), 1)
                                    dve.wait_ge(sem("cmp_step"), it * CC + cc + 2)
                                    dve.tensor_scalar(NM[:, x % 3, :], NM[:, x % 3, :], BIG / 10, None, ALU.min).then_inc(sem("cmp_step"), 1)
                                    dve.wait_ge(sem("cmp_step"), it * CC + cc + 3)
                                    dve.scalar_tensor_tensor(x3, x3, -1.0, NM[:, x % 3, :].unsqueeze(2).to_broadcast([P, QB, NCB]),
                                                             ALU.mult, ALU.add).then_inc(sem(ph + "_sm"), 1)
                                else:
                                    at = 1 if ph == "a" else 0
                                    dve.wait_ge(sem(ph + "_qk"), it * pl["U"] + x + 1)
                                    dve.memset(NM[:, x % 3, 1:2], 0.0)
                                    dve.tensor_tensor_reduce(PB[:, x % 3, at:at + L], PSf[:, 1024 * (x % 2):1024 * (x % 2) + L],
                                                             STR[:, un["s"], SEQ - L:SEQ], -SCALE,
                                                             (PB[:, x % 3, 0:1] if ph == "a" else 3 * BIG), ALU.add, ALU.min,
                                                             NM[:, x % 3, 0:1]).then_inc(sem(ph + "_sm"), 1)
                            elif what == "ev" and x["c"] % 2:
                                c, un = x["c"], units[x["unit"]]
                                if un["b"] == "cmp" and x["part"] == 1:
                                    dve.wait_ge(sem(ph + "_ex"), it * pl["U"] + x["unit"] + 1)
                                    dve.tensor_reduce(DEN[:, un["job"], :], PB[:, x["unit"] % 3, 0:un["keys"]]
                                                      .rearrange("p (q c) -> p q c", q=QB), AX, ALU.add).then_inc(sem("cmp_step"), 1)
                                dve.wait_ge(sem(ph + "_tr"), it * pl["N"] + x["n"] + 1)
                                if c > 1:
                                    dve.wait_ge(sem(ph + "_pv"), it * pl["C"] + c - 1)
                                m = NCB if un["b"] == "cmp" else P
                                n = 512 if un["b"] == "cmp" else min(512, un["keys"] - 512 * x["part"])
                                dve.tensor_copy(PT[0:m, c % 2, 0:n], PS[0:m, 4 + x["n"] % 2, 0:n]).then_inc(sem(ph + "_evd"), 1)
                            elif what == "oe":
                                b, s = jobs[x]
                                rc0 = sum(1 if jobs[i][0] == "a" else 3 if jobs[i][0] == "cmp" else 2 for i in range(x))
                                lastg = [g_ for un in units if un["job"] == x for g_ in un["groups"]][-1]
                                if b == "cmp":
                                    dve.wait_ge(sem("cmp_step"), it * CC + 6 + x + 1)
                                    dve.tensor_scalar(DEN[:, x, :], DEN[:, x, :], 1.0 / BIG, None, ALU.max).then_inc(sem(ph + "_rc"), 1)
                                    rc0 += 1
                                    dve.wait_ge(sem(ph + "_rc"), it * RC + rc0)
                                if x:
                                    dve.wait_ge(sem(ph + "_oe"), it * pl["J"] + x)
                                dve.reciprocal(RG[:, :], DEN[:, x, :]).then_inc(sem(ph + "_rc"), 1)
                                rc0 += 1
                                dve.wait_ge(sem(ph + "_rc"), it * RC + rc0)
                                if ph == "b":
                                    dve.tensor_tensor(RG[:, :], RG[:, :],
                                                      SG[:, :, bass.ds(it * 2 + BR[b] * H + s, 1)].rearrange("p q o -> p (q o)"),
                                                      ALU.mult).then_inc(sem(ph + "_rc"), 1)
                                    rc0 += 1
                                    dve.wait_ge(sem(ph + "_rc"), it * RC + rc0)
                                dve.wait_ge(sem(ph + "_pv"), it * pl["C"] + lastg["c"] + 1)
                                if x >= 2 and s == 0:
                                    og = [o for o in pl["order"] if o["kind"] == "o" and o["b"] == jobs[x - 1][0]][-1]
                                    dve.wait_ge(sem(ph + "_tr"), it * pl["N"] + og["n"] + 1)
                                dve.tensor_tensor(OS[:, :, s * HDIM:(s + 1) * HDIM],
                                                  PS[:, 6, :].rearrange("p (q d) -> p q d", q=QB),
                                                  RG[:, :].unsqueeze(2).to_broadcast([P, QB, HDIM]), ALU.mult).then_inc(sem(ph + "_oe"), 1)
                            elif what == "mix":
                                half = slice(512 * x["part"], 512 * x["part"] + 512)
                                dve.wait_ge(sem(ph + "_tr"), it * pl["N"] + x["n"] + 1)
                                out = MT[:, bass.ds(it, 1), half].rearrange("p o n -> p (o n)")
                                if x["b"] == pl["branches"][0]:
                                    dve.scalar_tensor_tensor(out, PS[:, 4 + x["n"] % 2, :], 0.5, SZ[x["b"]][:, half],
                                                             ALU.mult, ALU.mult).then_inc(sem(ph + "_mix"), 1)
                                else:
                                    ms = x["m"] - 1
                                    dve.scalar_tensor_tensor(SS[:, :], PS[:, 4 + x["n"] % 2, :], 0.5, SZ[x["b"]][:, half],
                                                             ALU.mult, ALU.mult).then_inc(sem("mix_step"), 1)
                                    dve.wait_ge(sem("mix_step"), it * (pl["M"] - 2) + ms)
                                    dve.wait_ge(sem(ph + "_mix"), it * pl["M"] + x["m"])
                                    dve.tensor_tensor(out, out, SS[:, :], ALU.add).then_inc(sem(ph + "_mix"), 1)
                                    dve.wait_ge(sem(ph + "_mix"), it * pl["M"] + x["m"] + 2)
                        dve.wait_ge(sem(ph + "_oe"), it * pl["J"] + pl["J"])
                        dve.wait_ge(sem(ph + "_tr"), it * pl["N"] + pl["N"])

                for g, i0, i1 in ((0, 0, PAIRS // 2), (1, PAIRS // 2, PAIRS - 1)):
                    with dve.Fori(i0, i1) as it:
                        pair(g, it, False)
                pair(1, PAIRS - 1, True)

            pairs("a")
            dve.wait_ge(sem("szs_set"), 8)
            dve.wait_ge(sem("sink_set"), 48)

            def decode(b, keys, extra, new):
                dve.wait_ge(sem("d_qk"), DN[b])
                nm, den, r = SS[:, 200:201], SS[:, 201:202], SS[:, 202:203]
                if b == "cmp":
                    step(dve.tensor_scalar(PB[:, 0, 0:keys], PSf[:, 0:keys], -SCALE, None, ALU.mult))
                    dve.tensor_reduce(nm, PB[:, 0, 0:keys], AX, ALU.min).then_inc(sem("d_sm"), 1)
                else:
                    if b == "a":
                        dve.tensor_copy(PB[:, 0, keys + 1:keys + 2], NSK[:, H:H + 1])
                    dve.tensor_tensor_reduce(PB[:, 0, 0:keys + 1], PSf[:, 0:keys + 1],
                                             STR[:, :, :].rearrange("p a n -> p (a n)")[:, PAST - keys:PAST + 1], -SCALE,
                                             (NSK[:, H:H + 1] if b == "a" else 3 * BIG), ALU.add, ALU.min, nm)\
                       .then_inc(sem("d_sm"), 1)
                dve.wait_ge(sem("d_ex"), DN[b])
                step(dve.reciprocal(r, den))
                if b == "cmp":
                    step(dve.tensor_scalar(PB[:, 1, 0:keys], PB[:, 1, 0:keys], r, None, ALU.mult))
                    dve.scalar_tensor_tensor(PB[:, 2, 0:P].rearrange("p (r c) -> p r c", r=4),
                                             PB[:, 1, 0:keys].unsqueeze(1).to_broadcast([P, 4, keys]), SGS[:, 0:1],
                                             CST[:, C_M4:C_M4 + 4].unsqueeze(2).to_broadcast([P, 4, keys]), ALU.mult, ALU.mult)\
                       .then_inc(sem("d_p"), 1)
                    return
                gate = ONE[:, 0:1] if b == "a" else SGS[:, BR[b]:BR[b] + 1]
                step(dve.tensor_scalar(PB[:, 2, 0:keys + 1], PB[:, 1, 0:keys + 1], r, gate, ALU.mult, ALU.mult))
                dve.tensor_scalar(SS[:, 0:DEC], CST[:, C_DN:C_DN + DEC], PB[:, 2, keys:keys + 1], None, ALU.mult)\
                   .then_inc(sem("d_p"), 1)
                dve.wait_ge(sem("d_tr"), DN[b])
                dve.tensor_copy(SS[0:DEC, 16:16 + P], PS[0:DEC, 6, 0:P]).then_inc(sem("d_pt"), 1)

            def decode_out(b, first_):
                dve.wait_ge(sem("d_pv"), DN[b])
                os_ = SS[:, 256:320].rearrange("p (c n) -> p c n", c=NC)
                for g in range(KVH):
                    for s in range(2):
                        src = PS[g * HDIM:(g + 1) * HDIM, 7, 0:P].rearrange("p (n g c s) -> p g s c n", n=DEC, g=2, s=2)[:, g, s]
                        ins = dve.tensor_copy(os_[s * HDIM:(s + 1) * HDIM, 4 * g:4 * g + 4, :], src)
                step(ins)
                out = MT[:, :, SEQ:TOK]
                if first_:
                    dve.scalar_tensor_tensor(out, os_, 0.5, SZS[:, BR[b], :, :], ALU.mult, ALU.mult).then_inc(sem("d_out"), 1)
                else:
                    o2 = SS[:, 320:384].rearrange("p (c n) -> p c n", c=NC)
                    step(dve.scalar_tensor_tensor(o2, os_, 0.5, SZS[:, BR[b], :, :], ALU.mult, ALU.mult))
                    dve.tensor_tensor(out, out, o2, ALU.add).then_inc(sem("d_out"), 1)
                dve.wait_ge(sem("d_out"), DN[b])

            dve.wait_ge(sem("a_rows_in"), 16)
            dve.wait_ge(sem("new_keys"), 2)
            decode("a", WIN_A, 2, 0)
            decode_out("a", True)
            split_decode_output()

            def residual(n0, a0):
                for c in range(NC):
                    gate, x = ADA[:, a0 + c, :], HT[:, c, :]
                    dve.wait_ge(sem(f"x_in{c % 2}"), {0: 64, NC: 128}[n0] + 16 * (c // 2 + 1))
                    for a in range(3):
                        dve.wait_ge(sem("op_mm"), 3 * (n0 + c) + a + 1)
                        n = THIRD if a < 2 else THIRD - DEC
                        b = EARLY[a] if n0 == NC and c == 0 else a
                        if a == 2:
                            dve.tensor_tensor(SS[:, 384:392], PS[:, b, n:THIRD], gate[:, 1:NTOK1], ALU.mult).then_inc(sem("res_step"), 1)
                        ins = dve.scalar_tensor_tensor(x[:, a * THIRD:a * THIRD + n], PS[:, b, 0:n], gate[:, 0:1],
                                                       x[:, a * THIRD:a * THIRD + n], ALU.mult, ALU.add)
                        if a < 2:
                            ins.then_inc(sem("op_ev"), 1)
                    dve.wait_ge(sem("res_step"), n0 + c + 1)
                    dve.tensor_tensor(x[:, SEQ:TOK], x[:, SEQ:TOK], SS[:, 384:392], ALU.add).then_inc(sem("op_ev"), 1)
                    dve.wait_ge(sem("op_ev"), 3 * (n0 + c) + 3)

            residual(0, 16)
            gains("kv", 1, V_GKV)
            gains("b", 2, V_GB)
            norm("b")
            modulate("kv", 1, HT)
            kv_dst = (PB[:, 0, :], PB[:, 1, :], KD[:, 0, 0, :], KD[:, 0, 1, :], PB[:, 2, :], KD[:, 1, 0, :], KD[:, 1, 1, :], QT[:, :])
            for k, dst in enumerate(kv_dst):
                dve.wait_ge(sem("lin_mm"), L_KV + k + 1)
                dve.tensor_copy(third(dst), lin_set(k)).then_inc(sem("lin_ev"), 1)
            dve.wait_ge(sem("lin_ev"), L_KV + 8)
            new_keys(1, 0)
            new_keys(2, 1)
            for j, tag in ((1, "sel_vt"), (2, "win_vt")):
                dve.wait_ge(sem(tag), 1)
                dve.tensor_copy(VN[:, j, :], PS[0:DEC, 6, 0:P]).then_inc(sem(tag + "_ev"), 1)
            modulate("b", 2)
            dve.wait_ge(sem("gl_tanh"), 1)
            dve.tensor_scalar(GL[0:3 * H, :], GL[0:3 * H, :], 1.0, 0.5, ALU.add, ALU.mult).then_inc(sem("lin_ev"), 1)
            dve.wait_ge(sem("gl_tr"), 1)
            dve.tensor_copy(SG[:, :, :].rearrange("p q c -> p (q c)"), PS[:, 6, 0:QB * 3 * H]).then_inc(sem("gl_ev"), 1)
            dve.tensor_copy(SS[0:DEC, 0:3 * H], PS[0:DEC, 7, 0:3 * H]).then_inc(sem("gl_ev"), 1)
            dve.wait_ge(sem("gs_mm"), 1)
            own = SS[:, 64:112].rearrange("p (b h) -> p b h", b=3)
            step(dve.tensor_tensor(own, PS[:, 6, 0:3 * H].rearrange("p (b h) -> p b h", b=3),
                                   CST[:, C_DH:C_DH + H].unsqueeze(1).to_broadcast([P, 3, H]), ALU.mult))
            dve.tensor_reduce(SGS[:, :], own, AX, ALU.add).then_inc(sem("gs_ev"), 1)
            dve.wait_ge(sem("gs_ev"), 1)
            dve.wait_ge(sem("pc_mm"), 1)
            dve.tensor_copy(PC[:, :], PS[:, 3, 0:2]).then_inc(sem("pc_ev"), 1)
            dve.tensor_scalar(PCH[:, :], PS[:, 3, 0:2], 0.5, None, ALU.mult).then_inc(sem("pc_ev"), 1)
            dve.wait_ge(sem("pc_ev"), 2)
            for st in range(6):
                k, third_ = divmod(st, 3)
                if third_ == 2:
                    if st >= 2:
                        dve.wait_ge(sem("cm_mm"), st - 1)
                    pages = CM[st % 2][:, 16 * P:24 * P].rearrange("p (j g x) -> p j g x", j=8, g=2)
                    for g in range(KVH):
                        for par in range(2):
                            src = PB[g * HDIM:(g + 1) * HDIM, k, 0:SEQ].rearrange("p (j x r) -> p r j x", j=8, r=2)[:, par]
                            ins = dve.tensor_copy(pages[par * HDIM:(par + 1) * HDIM, :, g, :], src)
                    ins.then_inc(sem("cm_own"), 1)
                dve.wait_ge(sem("hid_tanh"), st + 1)
                if st:
                    dve.wait_ge(sem("ckv_mm"), st)
                n = CM_PAGES * 8
                step(dve.tensor_scalar(HS[:, :], PS[:, st % 2, 0:n], PC[:, k:k + 1], None, ALU.add))
                last = dve.scalar_tensor_tensor(HS[:, :], HX[:, :], 1.0, HS[:, :], ALU.add, ALU.mult)
                if k == 1:
                    step(last)
                    for n_ in range(3):
                        last = dve.tensor_copy(HX.rearrange("p (n g j b) -> p n g j b", n=3, g=2, j=8)[:, n_],
                                               HS.rearrange("p (n j g b) -> p n g j b", n=3, j=8, g=2)[:, n_])
                last.then_inc(sem("hid"), 1)
                dve.wait_ge(sem("ckv_mm"), st + 1)
                if k == 0:
                    dve.tensor_scalar(CK[:, third_ * n:(third_ + 1) * n], PS[:, 2, 0:n], 0.5, None, ALU.mult).then_inc(sem("ckv_ev"), 1)
                elif third_ == 2:
                    dve.tensor_scalar(CV[:, 0:2, :].rearrange("p n c -> p (n c)"), PS[:, 2, 0:2 * P], 0.5, None, ALU.mult)\
                       .then_inc(sem("ckv_ev"), 1)
                    dve.tensor_scalar(CV[0:NCB, 2, :], PS[0:NCB, 2, 2 * P:3 * P], 0.5, None, ALU.mult).then_inc(sem("ckv_ev"), 1)
            dve.wait_ge(sem("ckv_ev"), 5)
            dve.tensor_copy(CKP[:, :], CK[:, 512:576]).then_inc(sem("cks"), 1)
            for g in range(KVH):
                rows = slice(g * HDIM, (g + 1) * HDIM)
                dve.tensor_copy(CKS[rows, :, :].rearrange("p n (j b) -> p (n j) b", b=4),
                                CK[rows, 0:512].rearrange("p (m g b) -> p m g b", g=2, b=4)[:, :, g, :]).then_inc(sem("cks"), 1)
            dve.wait_ge(sem("kv_stored"), 64)
            pairs("b")
            dve.wait_ge(sem("szs_set"), 32)
            dve.wait_ge(sem("qs_set"), 32)
            decode("cmp", NCB, 0, None)
            dve.wait_ge(sem("imp_mm"), 1)
            imp, eq, mn, dr = SS[:, 400:416], SS[:, 416:430], SS[:, 206:207], SS[:, 207:208]
            pen = SS[:, 432:448]
            step(dve.tensor_reduce(imp, PS[:, 1, 0:NCB].rearrange("p (j c) -> p j c", c=2), AX, ALU.add))
            step(dve.tensor_reduce(mn, imp[:, 1:15], AX, ALU.min))
            step(dve.scalar_tensor_tensor(eq, imp[:, 1:15], mn, CST[:, C_JW + 1:C_JW + 15], ALU.is_equal, ALU.mult))
            step(dve.tensor_reduce(dr, eq, AX, ALU.max))
            step(dve.tensor_scalar(pen, CST[:, C_JW:C_JW + 16], dr, -BIG / SCALE, ALU.is_equal, ALU.mult))
            dve.wait_ge(sem("b_rows_in"), 16)
            rowf = STR[:, :, :].rearrange("p a n -> p (a n)")
            row2 = QT
            dve.tensor_tensor(row2[:, 0:PAST].rearrange("p (j x) -> p j x", j=16), rowf[:, 0:PAST].rearrange("p (j x) -> p j x", j=16),
                              pen.unsqueeze(2).to_broadcast([P, 16, SB]), ALU.add)
            dve.tensor_copy(row2[:, PAST:PAST + 1], rowf[:, PAST:PAST + 1]).then_inc(sem("imp_done"), 1)
            dve.wait_ge(sem("imp_done"), 1)
            decode_out("cmp", True)
            dve.wait_ge(sem("d_qk"), DN["sel"])
            dve.wait_ge(sem("new_keys"), 6)
            nm, den, r = SS[:, 200:201], SS[:, 201:202], SS[:, 202:203]
            dve.tensor_tensor_reduce(PB[:, 0, 0:PAST + 1], PSf[:, 0:PAST + 1], row2[:, 0:PAST + 1], -SCALE, 3 * BIG,
                                     ALU.add, ALU.min, nm).then_inc(sem("d_sm"), 1)
            dve.wait_ge(sem("d_ex"), DN["sel"])
            step(dve.reciprocal(r, den))
            step(dve.tensor_scalar(PB[:, 2, 0:PAST + 1], PB[:, 1, 0:PAST + 1], r, SGS[:, 1:2], ALU.mult, ALU.mult))
            dve.tensor_scalar(SS[:, 0:DEC], CST[:, C_DN:C_DN + DEC], PB[:, 2, PAST:PAST + 1], None, ALU.mult).then_inc(sem("d_p"), 1)
            dve.wait_ge(sem("d_tr"), DN["sel"])
            dve.tensor_copy(SS[0:DEC, 16:16 + P], PS[0:DEC, 6, 0:P]).then_inc(sem("d_pt"), 1)
            decode_out("sel", False)
            decode("win", WIN_B, 1, 2)
            decode_out("win", False)
            split_decode_output()
            residual(NC, 56)
            norm("f")


def kernel(**inputs):
    import concourse.bacc as _bacc
    from concourse.bass_utils import run_bass_kernel_spmd as _run

    f = {k: np.asarray(v) for k, v in inputs.items()}
    chunked = lambda a: np.ascontiguousarray(a.reshape(NC, P, -1).transpose(1, 0, 2))

    def tiles(w):
        return np.ascontiguousarray(w.reshape(NC, P, -1, P).transpose(2, 1, 0, 3))

    def vec(a):
        return a.reshape(-1, P).T

    x = np.concatenate([f["x_prompt"][0], f["x_sample"][:, 0]], 0).T
    c = np.concatenate([f["c_prompt"], f["c_sample"]], 0).T
    wa, wkv, wb = f["a_w_in"][0], f["kv_w_in"], f["b_w_in"][0]
    hd, kvd = H * HDIM, KVH * HDIM

    def both(w):
        return np.concatenate([w, w], 1)

    def kv_cols(w, at):
        return [both(w[:, at:at + HDIM]), both(w[:, at + HDIM:at + 2 * HDIM]), w[:, at + kvd:at + 2 * kvd]]

    w_a0 = np.concatenate(kv_cols(wa, hd), 1)
    pair = lambda w, at, i: w[:, at + i * P:at + (i + 1) * P]
    w_a = np.concatenate([pair(wa, at, i) for i in range(PAIRS) for at in (0, hd + 2 * kvd)], 1)
    w_kv = np.concatenate([wkv[:, 0:2 * kvd]] + kv_cols(wkv, 2 * kvd) + kv_cols(wkv, 4 * kvd), 1)
    w_b = np.concatenate([pair(wb, at, i) for i in range(PAIRS) for at in (0, hd, 2 * hd, 3 * hd)], 1)
    w_gl = np.concatenate([wb[:, 4 * hd:], np.zeros((DM, P - 3 * H), wb.dtype)], 1)
    w_ada = np.concatenate([tiles(f["a_w_ada"][0]), tiles(f["kv_w_ada"]), tiles(f["b_w_ada"][0])], 0)
    sink = f["a_sinks"][0]
    pos = f["cmp_pos"].reshape(16, 2, 2, HDIM).transpose(1, 3, 2, 0).reshape(P, 32)
    vecs = np.concatenate([vec(f["a_norm_g"][0]), vec(f["kv_norm_g"]), vec(f["b_norm_g"][0]), vec(f["final_norm_g"]),
                           vec(f["a_b_ada"][0]), vec(f["kv_b_ada"]), vec(f["b_b_ada"][0]),
                           np.tile(sink, (P, 1)), np.tile(sink, DEC)[:, None], pos], 1)
    w1 = f["cmp_w1"].reshape(2, 16, P, P).transpose(2, 0, 1, 3).reshape(P, 4096)
    w2 = f["cmp_w2"].transpose(1, 0, 2)
    pool = f["cache_cmp_kv"].reshape(-1, 4, 16, 2, 2, KVH, HDIM).transpose(0, 4, 3, 6, 5, 1, 2).reshape(-1, 2, P, P)
    sel, sa, sw = f["cache_sel_kv"], f["state_a_kv"][0], f["state_win_kv"]
    rows = lambda a, k: a[:, :, k].reshape(a.shape[0], a.shape[1], P)

    const = np.zeros((P, C_END), np.float32)
    const[:, C_ID:C_ID + P] = np.eye(P)
    q = np.arange(P)
    ends = np.arange(NCB) * CB + CB - 1
    for qb in range(QB):
        const[:, C_CM + qb * NCB:C_CM + (qb + 1) * NCB] = np.where(ends[None] <= qb * P + q[:, None], 0.0, BIG)
    const[q, C_DN + q // H] = 1.0
    const[q, C_DH + q % H] = 1.0
    const[:, C_GS:C_GS + P] = (q[:, None] // 8 == q[None] // 8)
    const[:, C_FAR:C_FAR + P] = np.where(q[:, None] <= q[None], 0.0, -BIG / SCALE)
    for n in range(DEC):
        const[n, C_EN + n * H:C_EN + (n + 1) * H] = 1.0
    const[:, C_JW:C_JW + 16] = np.arange(1, 17)
    const[q, C_M4 + q // H % 4] = 1.0
    dist = PAST - np.arange(NBIAS)
    n_ = np.maximum(dist, 0)
    large = 16 + (np.log(np.maximum(n_, 16).astype(np.float32) / np.float32(16)) / np.float32(np.log(8.0)) * np.float32(16)).astype(np.int32)
    bucket = np.where(n_ < 16, n_, np.minimum(large, 31))
    onehot = (np.arange(32)[:, None] == bucket[None]).astype(np.float32)
    causal = np.tile(np.where(dist < 0, -BIG / SCALE, 0.0).astype(np.float32), (P, 1))

    ins = dict(
        c=chunked(c), const=const, vec=vecs, w_ada=w_ada, table=np.tile(f["rel_bias_table"], (1, DEC)), onehot=onehot, causal=causal,
        pages=f["page_table"].reshape(1, -1).astype(np.int32), w2=w2, x=chunked(x),
        sa_kT=rows(sa, 0).transpose(0, 2, 1), sa_v=rows(sa, 1), sw_kT=rows(sw, 0).transpose(0, 2, 1), sw_v=rows(sw, 1),
        w_a0=tiles(w_a0), w_a=tiles(w_a), w_ao=tiles(f["a_w_out"][0]), w_kv=tiles(w_kv), w1=w1, w_gl=tiles(w_gl)[0],
        cmp_pool=pool, w_b=tiles(w_b), sel_kT=rows(sel, 0).transpose(0, 2, 1), sel_v=rows(sel, 1), w_bo=tiles(f["b_w_out"][0]),
    )
    outs = dict(o_sa_k=(DEC, P, WIN_A - 1), o_sa_v=(DEC, WIN_A - 1, P), o_sw_k=(DEC, P, WIN_B - 1), o_sw_v=(DEC, WIN_B - 1, P),
                o_kv_a=(2, P, WIN_A + DEC), o_kv=(6, P, TOK), o_y=(P, NC, TOK))
    nc = _bacc.Bacc("TRN2", target_bir_lowering=False, num_devices=1)
    t, arrays = {}, {}
    for name, a in ins.items():
        a = np.ascontiguousarray(a)
        arrays[name] = a
        t[name] = nc.dram_tensor(name, a.shape, mybir.dt.from_np(a.dtype), kind="ExternalInput").ap()
    for name, shape in outs.items():
        t[name] = nc.dram_tensor(name, shape, F32, kind="ExternalOutput").ap()
    t["x_mid"] = nc.dram_tensor("x_mid", (P, NC, TOK), F32, kind="Internal").ap()
    t["scratch"] = nc.dram_tensor("scratch", (COPIES * H, NBIAS), F32, kind="Internal").ap()
    build(nc, t)
    r = _run(nc, [arrays], core_ids=[0]).results[0]
    o = {name: np.asarray(r[name]) for name in outs}

    kvr = lambda k, v: np.stack([k, v], 0).reshape(2, KVH, HDIM, -1).transpose(3, 0, 1, 2)
    y = o["o_y"].transpose(1, 0, 2).reshape(DM, TOK).T
    a_new = kvr(o["o_kv_a"][0], o["o_kv_a"][1])
    cmp_r, sel_r, win_r = (kvr(o["o_kv"][2 * i], o["o_kv"][2 * i + 1]) for i in range(3))

    def shifted(k, v, new):
        old = np.stack([k.transpose(0, 2, 1), v], 2).reshape(DEC, -1, 2, KVH, HDIM)
        return np.concatenate([old, new[:, None]], 1)

    return (y[None, :SEQ], y[SEQ:, None],
            a_new[None, None, :WIN_A], shifted(o["o_sa_k"], o["o_sa_v"], a_new[WIN_A:])[None],
            cmp_r[None, :SEQ], cmp_r[SEQ:, None], sel_r[None, :SEQ], sel_r[SEQ:, None],
            win_r[None, SEQ - WIN_B:SEQ], shifted(o["o_sw_k"], o["o_sw_v"], win_r[SEQ:]))
```
